# Optimizing a Trainium2 kernel written in Bass

```python
import jax, jax.numpy as jnp
from jax import lax
import numpy as np

D_MODEL = 1024
BATCH = 1
SEQ = 256
DEPTH = 2
DEC_BATCH = 1
DEC_SEQ = 32
PAST_LEN = 512

CHUNK = 64
N_MIXERS = 2
N_A_LAYERS = (DEPTH + 1) // 2
N_B_LAYERS = DEPTH // 2
M_HEADS = 4
M_DK = D_MODEL // 8
M_DV = D_MODEL // M_HEADS
M_PROJ = 2 * M_HEADS * M_DK + 2 * M_HEADS * M_DV + 2 * M_HEADS
A_HEADS = 16
A_KV_HEADS = 4
A_HD = D_MODEL // A_HEADS
A_GROUP = A_HEADS // A_KV_HEADS
WINDOW = 128
WINDOW_CHUNKS = WINDOW // CHUNK
SWA_ROWS = min(WINDOW, PAST_LEN)
ROPE_THETA = 10000.0
D_FF = 11 * D_MODEL // 4
FFN_RES = 0.5
EPS = 1e-6

kernel_name = "hybrid_mlstm_swa_streaming_step"

def rms_norm(x, g):
    xf = x.astype(jnp.float32)
    y = xf * lax.rsqrt(jnp.mean(xf * xf, axis=-1, keepdims=True) + EPS)
    return (y * g.astype(jnp.float32)).astype(x.dtype)

def swiglu(x, w_in, w_out):
    gate, up = jnp.split(x @ w_in, 2, axis=-1)
    return (jax.nn.silu(gate) * up) @ w_out

def half_ffn(x, g, w_in, w_out):
    return x + FFN_RES * swiglu(rms_norm(x, g), w_in, w_out)

def rope(x, pos):
    inv = ROPE_THETA ** (-jnp.arange(0, A_HD, 2, dtype=jnp.float32) / A_HD)
    ang = pos.astype(jnp.float32)[:, None] * inv[None, :]
    cos = jnp.cos(ang)[None, :, None, :]
    sin = jnp.sin(ang)[None, :, None, :]
    xf = x.astype(jnp.float32)
    x1, x2 = xf[..., : A_HD // 2], xf[..., A_HD // 2:]
    return jnp.concatenate([x1 * cos - x2 * sin, x2 * cos + x1 * sin], axis=-1).astype(x.dtype)

def mlstm_chunk_step(carry, inp):
    C, n, m = carry
    q, k, v, ig, lf = inp
    L = q.shape[2]
    b = jnp.cumsum(lf, axis=-1)
    causal = jnp.tril(jnp.ones((L, L), dtype=bool))
    d = jnp.where(causal, b[..., :, None] - b[..., None, :] + ig[..., None, :], -jnp.inf)
    g = b + m[..., None]
    m_t = jnp.maximum(g, jnp.max(d, axis=-1))
    w = jnp.exp(d - m_t[..., None]) * jnp.einsum('bhtd,bhsd->bhts', q, k)
    inter = jnp.exp(g - m_t)
    num = inter[..., None] * jnp.einsum('bhtd,bhde->bhte', q, C) + jnp.einsum('bhts,bhse->bhte', w, v)
    den = inter * jnp.einsum('bhtd,bhd->bht', q, n) + jnp.sum(w, axis=-1)
    h = num / jnp.maximum(jnp.abs(den), jnp.exp(-m_t))[..., None]
    b_last = b[..., -1]
    a = b_last[..., None] - b + ig
    m_new = jnp.maximum(m + b_last, jnp.max(a, axis=-1))
    decay = jnp.exp(m + b_last - m_new)
    wk = jnp.exp(a - m_new[..., None])[..., None] * k
    C_new = decay[..., None, None] * C + jnp.einsum('bhsd,bhse->bhde', wk, v)
    n_new = decay[..., None] * n + jnp.sum(wk, axis=2)
    return (C_new, n_new, m_new), h

def mlstm_scan(q, k, v, ig, lf, C0, n0, m0):
    B, T = q.shape[0], q.shape[1]
    L = min(CHUNK, T)
    nc = T // L
    blk = lambda a: a.reshape((B, nc, L) + a.shape[2:]).transpose((1, 0, 3, 2) + tuple(range(4, a.ndim + 1)))
    (C, n, m), h = lax.scan(mlstm_chunk_step, (C0, n0, m0),
                            (blk(q), blk(k), blk(v), blk(ig), blk(lf)))
    h = h.transpose(1, 0, 3, 2, 4).reshape(B, T, M_HEADS, M_DV)
    return h, C, n, m

def mlstm_mixer(x, w_in, b_gates, head_norm, w_out, C0, n0, m0):
    B, T, _ = x.shape
    f32 = jnp.float32
    hk, hv = M_HEADS * M_DK, M_HEADS * M_DV
    q, k, v, o, gates = jnp.split(x @ w_in, [hk, 2 * hk, 2 * hk + hv, 2 * hk + 2 * hv], axis=-1)
    q = q.reshape(B, T, M_HEADS, M_DK).astype(f32)
    k = k.reshape(B, T, M_HEADS, M_DK).astype(f32) * (M_DK ** -0.5)
    v = v.reshape(B, T, M_HEADS, M_DV).astype(f32)
    gates = gates.astype(f32) + b_gates.astype(f32)
    ig, fg = gates[..., :M_HEADS], gates[..., M_HEADS:]
    lf = jax.nn.log_sigmoid(fg)
    h, C, n, m = mlstm_scan(q, k, v, ig, lf, C0.astype(f32), n0.astype(f32), m0.astype(f32))
    h = h * lax.rsqrt(jnp.mean(h * h, axis=-1, keepdims=True) + EPS)
    h = h.reshape(B, T, hv) * head_norm.astype(f32)
    out = (jax.nn.sigmoid(o.astype(f32)) * h).astype(x.dtype) @ w_out
    return out, C, n, m

def swa_project(x, w_qkv, pos):
    B, T, _ = x.shape
    q, k, v = jnp.split(x @ w_qkv, [A_HEADS * A_HD, (A_HEADS + A_KV_HEADS) * A_HD], axis=-1)
    q = rope(q.reshape(B, T, A_HEADS, A_HD), pos)
    k = rope(k.reshape(B, T, A_KV_HEADS, A_HD), pos)
    v = v.reshape(B, T, A_KV_HEADS, A_HD)
    return q, k, v

def sink_softmax(s, sinks):
    sk = sinks[:, :, None, None]
    m = jnp.maximum(jnp.max(s, axis=-1, keepdims=True), sk)
    p = jnp.exp(s - m)
    return p / (jnp.sum(p, axis=-1, keepdims=True) + jnp.exp(sk - m))

def swa_prompt(x, w_qkv, sinks, w_out):
    B, T, _ = x.shape
    nc = T // CHUNK
    q, k, v = swa_project(x, w_qkv, jnp.arange(T))
    qc = q.reshape(B, nc, CHUNK, A_KV_HEADS, A_GROUP, A_HD)
    pad = ((0, 0), (WINDOW_CHUNKS, 0), (0, 0), (0, 0), (0, 0))
    kp = jnp.pad(k.reshape(B, nc, CHUNK, A_KV_HEADS, A_HD), pad)
    vp = jnp.pad(v.reshape(B, nc, CHUNK, A_KV_HEADS, A_HD), pad)
    kb = jnp.concatenate([kp[:, j:j + nc] for j in range(WINDOW_CHUNKS + 1)], axis=2)
    vb = jnp.concatenate([vp[:, j:j + nc] for j in range(WINDOW_CHUNKS + 1)], axis=2)
    chunk_idx = jnp.arange(nc)[:, None] - WINDOW_CHUNKS + jnp.arange(WINDOW_CHUNKS + 1)[None, :]
    valid = jnp.repeat(chunk_idx >= 0, CHUNK, axis=1)
    s = jnp.einsum('bnqkgd,bnskd->bnkgqs', qc, kb).astype(jnp.float32) * (A_HD ** -0.5)
    s = jnp.where(valid[None, :, None, None, None, :], s, -jnp.inf)
    p = sink_softmax(s, sinks.reshape(A_KV_HEADS, A_GROUP).astype(jnp.float32))
    o = jnp.einsum('bnkgqs,bnskd->bnqkgd', p.astype(vb.dtype), vb).reshape(B, T, A_HEADS * A_HD)
    keep = min(WINDOW, T)
    return o @ w_out, k[:, T - keep:], v[:, T - keep:]

def swa_sample(x, cache_k, cache_v, w_qkv, sinks, w_out):
    B, T, _ = x.shape
    q, k, v = swa_project(x, w_qkv, PAST_LEN + jnp.arange(T))
    ka = jnp.concatenate([cache_k.astype(k.dtype), k], axis=1)
    va = jnp.concatenate([cache_v.astype(v.dtype), v], axis=1)
    qg = q.reshape(B, T, A_KV_HEADS, A_GROUP, A_HD)
    s = jnp.einsum('bqkgd,bskd->bkgqs', qg, ka).astype(jnp.float32) * (A_HD ** -0.5)
    p = sink_softmax(s, sinks.reshape(A_KV_HEADS, A_GROUP).astype(jnp.float32))
    o = jnp.einsum('bkgqs,bskd->bqkgd', p.astype(va.dtype), va).reshape(B, T, A_HEADS * A_HD)
    return o @ w_out, k, v

def setup_inputs(seed: int = 0) -> dict:
    key = jax.random.key(seed)
    ks = jax.random.split(key, 24)
    nrm = lambda k, shape, scale: scale * jax.random.normal(k, shape, jnp.float32)
    gb = jnp.concatenate([nrm(ks[9], (N_A_LAYERS, M_HEADS), 0.1),
                          3.0 + nrm(ks[10], (N_A_LAYERS, M_HEADS), 0.5)], axis=-1)
    return {
        "x_prompt": nrm(ks[0], (BATCH, SEQ, D_MODEL), 1.0),
        "x_sample": nrm(ks[1], (DEC_BATCH, DEC_SEQ, D_MODEL), 1.0),
        "state_mlstm_C": nrm(ks[2], (N_A_LAYERS, DEC_BATCH, M_HEADS, M_DK, M_DV), 0.1),
        "state_mlstm_n": nrm(ks[3], (N_A_LAYERS, DEC_BATCH, M_HEADS, M_DK), 0.1),
        "state_mlstm_m": nrm(ks[4], (N_A_LAYERS, DEC_BATCH, M_HEADS), 1.0),
        "cache_swa_k": nrm(ks[5], (N_B_LAYERS, DEC_BATCH, SWA_ROWS, A_KV_HEADS, A_HD), 1.0),
        "cache_swa_v": nrm(ks[6], (N_B_LAYERS, DEC_BATCH, SWA_ROWS, A_KV_HEADS, A_HD), 1.0),
        "ffn_norm1": 1.0 + nrm(ks[7], (DEPTH, D_MODEL), 0.05),
        "ffn_w_in1": nrm(ks[8], (DEPTH, D_MODEL, 2 * D_FF), D_MODEL ** -0.5),
        "ffn_w_out1": nrm(ks[11], (DEPTH, D_FF, D_MODEL), D_FF ** -0.5),
        "mix_norm": 1.0 + nrm(ks[12], (DEPTH, D_MODEL), 0.05),
        "mlstm_w_in": nrm(ks[13], (N_A_LAYERS, D_MODEL, M_PROJ), D_MODEL ** -0.5),
        "mlstm_b_gates": gb,
        "mlstm_head_norm": 1.0 + nrm(ks[14], (N_A_LAYERS, M_HEADS * M_DV), 0.05),
        "mlstm_w_out": nrm(ks[15], (N_A_LAYERS, M_HEADS * M_DV, D_MODEL), (M_HEADS * M_DV) ** -0.5),
        "swa_w_qkv": nrm(ks[16], (N_B_LAYERS, D_MODEL, (A_HEADS + 2 * A_KV_HEADS) * A_HD), D_MODEL ** -0.5),
        "swa_sinks": nrm(ks[17], (N_B_LAYERS, A_HEADS), 0.5),
        "swa_w_out": nrm(ks[18], (N_B_LAYERS, A_HEADS * A_HD, D_MODEL), (A_HEADS * A_HD) ** -0.5),
        "ffn_norm2": 1.0 + nrm(ks[19], (DEPTH, D_MODEL), 0.05),
        "ffn_w_in2": nrm(ks[20], (DEPTH, D_MODEL, 2 * D_FF), D_MODEL ** -0.5),
        "ffn_w_out2": nrm(ks[21], (DEPTH, D_FF, D_MODEL), D_FF ** -0.5),
        "final_norm": 1.0 + nrm(ks[22], (D_MODEL,), 0.05),
    }

def reference(x_prompt, x_sample, state_mlstm_C, state_mlstm_n, state_mlstm_m, cache_swa_k, cache_swa_v,
              ffn_norm1, ffn_w_in1, ffn_w_out1, mix_norm, mlstm_w_in, mlstm_b_gates, mlstm_head_norm,
              mlstm_w_out, swa_w_qkv, swa_sinks, swa_w_out, ffn_norm2, ffn_w_in2, ffn_w_out2, final_norm):
    yp, ys = x_prompt, x_sample
    Bp = x_prompt.shape[0]
    pC, pn, pm, pk, pv = [], [], [], [], []
    sC, sn, sm, sk, sv = [], [], [], [], []
    for i in range(DEPTH):
        yp = half_ffn(yp, ffn_norm1[i], ffn_w_in1[i], ffn_w_out1[i])
        ys = half_ffn(ys, ffn_norm1[i], ffn_w_in1[i], ffn_w_out1[i])
        hp = rms_norm(yp, mix_norm[i])
        hs = rms_norm(ys, mix_norm[i])
        j = i // N_MIXERS
        if i % N_MIXERS == 0:
            C0 = jnp.zeros((Bp, M_HEADS, M_DK, M_DV), jnp.float32)
            n0 = jnp.zeros((Bp, M_HEADS, M_DK), jnp.float32)
            m0 = jnp.zeros((Bp, M_HEADS), jnp.float32)
            op, C, n, m = mlstm_mixer(hp, mlstm_w_in[j], mlstm_b_gates[j], mlstm_head_norm[j],
                                      mlstm_w_out[j], C0, n0, m0)
            os_, C2, n2, m2 = mlstm_mixer(hs, mlstm_w_in[j], mlstm_b_gates[j], mlstm_head_norm[j],
                                          mlstm_w_out[j], state_mlstm_C[j], state_mlstm_n[j], state_mlstm_m[j])
            pC.append(C); pn.append(n); pm.append(m)
            sC.append(C2); sn.append(n2); sm.append(m2)
        else:
            op, kk, vv = swa_prompt(hp, swa_w_qkv[j], swa_sinks[j], swa_w_out[j])
            os_, kn, vn = swa_sample(hs, cache_swa_k[j], cache_swa_v[j], swa_w_qkv[j], swa_sinks[j], swa_w_out[j])
            pk.append(kk); pv.append(vv)
            sk.append(kn); sv.append(vn)
        yp = yp + op
        ys = ys + os_
        yp = half_ffn(yp, ffn_norm2[i], ffn_w_in2[i], ffn_w_out2[i])
        ys = half_ffn(ys, ffn_norm2[i], ffn_w_in2[i], ffn_w_out2[i])
    y_prompt = rms_norm(yp, final_norm)
    y_sample = rms_norm(ys, final_norm)
    return (y_prompt, y_sample,
            jnp.stack(pC), jnp.stack(pn), jnp.stack(pm), jnp.stack(pk), jnp.stack(pv),
            jnp.stack(sC), jnp.stack(sn), jnp.stack(sm), jnp.stack(sk), jnp.stack(sv))


_drawn_inputs = setup_inputs


def setup_inputs(seed=0):
    import zlib

    import numpy as np

    out = dict(_drawn_inputs(seed))
    spreads = {}
    factors = {'state_mlstm_n': 4.293, 'swa_sinks': 8.0}
    for name, (base, spread) in spreads.items():
        noise = np.random.default_rng([zlib.crc32(name.encode()), seed]).standard_normal(out[name].shape)
        drawn = base * np.exp(spread * noise) if base else spread * noise
        out[name] = __import__('jax').numpy.asarray(drawn.astype(out[name].dtype))
    for name, factor in factors.items():
        out[name] = (out[name] * factor).astype(out[name].dtype)
    return out
```

```python
from contextlib import ExitStack

import numpy as np

import concourse.bass as bass
from concourse import mybir

F32 = mybir.dt.float32
F32R = mybir.dt.float32r
ALU = mybir.AluOpType
ACT = mybir.ActivationFunctionType

P = 128
D = 1024
KD = D // P
TP, TS = 256, 32
T = TP + TS
FF = 11 * D // 4
KF = FF // P
NH, DK, DV = 4, 128, 256
AH, KV, HD = 16, 4, 64
CACHE = 128
PAST = 512
CHUNK, WIN = 64, 2
EPS = 1e-6
BIG = 1e30
RAW = 2 * (KF // 2)
TOK = [(0, 128), (128, 128), (256, 32)]

STAGES = [("ffn_in", 22, 44, 8), ("ffn_out", 8, 8, 11), ("mlstm_in", 12, 24, 8), ("mix_out", 4, 8, 8),
          ("ffn_in", 22, 44, 8), ("ffn_out", 8, 8, 11), ("ffn_in", 22, 44, 8), ("ffn_out", 8, 8, 11),
          ("swa_in", 6, 22, 8), ("mix_out", 4, 8, 8), ("ffn_in", 22, 44, 8), ("ffn_out", 8, 8, 11)]
FIRST_UNIT = [sum(s[1] for s in STAGES[:i]) for i in range(len(STAGES) + 1)]
FIRST_GROUP = [sum(s[2] for s in STAGES[:i]) for i in range(len(STAGES) + 1)]
UNITS = FIRST_UNIT[-1]
TILES = [s[3] for s in STAGES for _ in range(s[1])]
N_F1, N_MIX, N_F2, N_FINAL, N_HEAD = 0, 1, 2, 6, 7

C_ID, C_ONE, C_PERM, C_TRI, C_SEL = 0, 128, 256, 384, 640
C_COS = C_SEL + NH * P
C_SIN = C_COS + T
C_MASK = C_SIN + T
N_MASK = 3 * P + CACHE + TS
N_CONST = C_MASK + N_MASK


def constants():
    c = np.zeros((P, N_CONST), np.float32)
    p = np.arange(P)
    c[:, C_ID:C_ID + P] = np.eye(P)
    c[:, C_ONE:C_ONE + P] = 1.0
    c[p, C_PERM + (p ^ 32)] = 1.0
    c[:, C_TRI:C_TRI + P] = np.where(p[:, None] > p[None, :], BIG, 0.0)
    for h in range(NH):
        c[h, C_SEL + h * P:C_SEL + (h + 1) * P] = 1.0
    pos = np.concatenate([np.arange(TP), PAST + np.arange(TS)]).astype(np.float32)
    inv = (np.float32(10000.0) ** (-np.arange(0, HD, 2, dtype=np.float32) / np.float32(HD))).astype(np.float32)
    ang = inv[p % 32][:, None] * pos[None, :]
    c[:, C_COS:C_COS + T] = np.cos(ang)
    c[:, C_SIN:C_SIN + T] = np.sin(ang) * np.where(p % HD < 32, -1.0, 1.0)[:, None]
    for tile in range(2):
        q = (tile * P + p) // CHUNK
        k = np.arange((tile + 1) * P) // CHUNK
        ok = (k[None, :] <= q[:, None]) & (k[None, :] >= q[:, None] - WIN)
        at = C_MASK + tile * P
        c[:, at:at + (tile + 1) * P] = np.where(ok, 0.0, -BIG)
    return c


def program(nc, a):
    ctx = ExitStack()
    with ctx:
        def sb(name, shape, dt=F32):
            return ctx.enter_context(nc.sbuf_tensor(name, shape, dt))

        def sem(name):
            return ctx.enter_context(nc.semaphore(name))

        raw = sb("raw", [P, 2, RAW * P])
        whi = sb("whi", [P, 4, KF // 2, P], F32R)
        wlo = sb("wlo", [P, 4, KF // 2, P], F32R)
        x = sb("x", [P, KD, T])
        xhi = sb("xhi", [P, KD, T], F32R)
        xlo = sb("xlo", [P, KD, T], F32R)
        ahi = sb("ahi", [P, KF, T], F32R)
        alo = sb("alo", [P, KF, T], F32R)
        rstd = sb("rstd", [P, T])
        std = sb("std", [P, T])
        ssq = sb("ssq", [P, T])
        sqr = sb("sqr", [P, 2, T])
        norms = sb("norms", [P, 8, KD])
        epst = sb("epst", [P, 1])
        cst = sb("cst", [P, 3 * P])
        ghi = sb("ghi", [P, KD, P], F32R)
        glo = sb("glo", [P, KD, P], F32R)
        graw = sb("graw", [P, KD, 2 * NH])
        bg = sb("bg", [NH, 2])
        m0 = sb("m0", [NH, 1])
        mout = sb("mout", [NH, 2])
        acol = sb("acol", [P, 3 * NH])
        one_row = cst[0:NH, P:P + 1].to_broadcast([NH, TP])
        work = sb("work", [P, 12496])
        ident, ones, perm = cst[:, 0:P], cst[:, P:2 * P], cst[:, 2 * P:3 * P]

        def w(at, *shape):
            n = int(np.prod(shape))
            v = work[:, at:at + n]
            if len(shape) == 2:
                v = v.rearrange("p (a b) -> p a b", a=shape[0])
            if len(shape) == 3:
                v = v.rearrange("p (a b c) -> p a b c", a=shape[0], b=shape[1])
            return v

        f_gate, f_up, f_silu, f_prod = (w(i * 2 * T, 2, T) for i in range(4))
        kT, qT, vT, oT = w(0, 2, T), w(576, 2, T), w(1152, 2, 2, T), w(2304, 2, 2, T)
        ktok, vtok = w(3456, 3, P), w(3840, 3, DV + 1)
        dec = w(4612, NH, 416)
        emb, intb = w(6276, NH, T), w(7428, NH, TS)
        wts, qi, n0rep = w(7556, 416), w(7972, TS), w(8004, P)
        sqn, den, rinv, hn, den2 = w(8132, 2, T), w(8708, T), w(8996, T), w(9284, 2, T), w(9860, T)
        row = [work[0:NH, 8132 + i * T:8132 + (i + 1) * T] for i in range(7)]
        r_em = work[0:NH, 8132 + 6 * T:8132 + 7 * T + TS]
        outp, outs, c0 = w(10180, DV + 1), w(10438, DV + 1), w(10696, NH, DV + 1)
        tri, sel = w(11724, 2 * P), w(11980, NH, P)
        s_raw, s_t1, s_t2, s_vT = w(0, 2, T), w(576, 2, T), w(1152, 2, T), w(1728, 2, T)
        s_q, s_k, s_v = w(2304, KD, T), w(4608, 2, T), w(5184, 3, 2 * P)
        rc, rs = w(5952, T), w(6240, T)
        prob, probT = w(6528, 2, 3 * P), w(7296, 2, 3 * P)
        s_mx, s_neg, s_sum, s_sk, s_den, s_inv = (w(8064 + 4 * i, 2, 2) for i in range(6))
        vc, ks = w(8192, 2 * P), w(8448, 2, CACHE + TS)
        cos, sin = w(8768, T), w(9056, T)
        mask = w(9344, N_MASK)
        snk, snks = w(9888, AH), w(9904, KV)
        s_qs = w(9920, 2, 4 * TS)

        acc = [ctx.enter_context(nc.psum_tensor(f"acc{i}", [P, 512], F32)) for i in range(4)]
        num = ctx.enter_context(nc.psum_tensor("num", [P, 2, 512], F32))
        mb = [num[:, 0, :], num[:, 1, :],
              ctx.enter_context(nc.psum_tensor("mb2", [P, 512], F32))[:, :],
              ctx.enter_context(nc.psum_tensor("mb3", [P, 512], F32))[:, :]]

        landed = [sem("landed0"), sem("landed1")]
        hi_done, lo_done = sem("hi_done"), sem("lo_done")
        piece_done = sem("piece_done")
        evac = sem("evac")
        x_in, par_in, mix_in = sem("x_in"), sem("par_in"), sem("mix_in")
        silu_done, prod_done, ahi_done, alo_done = sem("silu_done"), sem("prod_done"), sem("ahi_done"), sem("alo_done")
        xhi_done, xlo_done = sem("xhi_done"), sem("xlo_done")
        pool_sq, ss_done, ss_mm, std_done, r_done = (sem(n) for n in ("pool_sq", "ss_done", "ss_mm", "std_done", "r_done"))
        const_done = sem("const_done")
        g_zero, g_hi, g_done = sem("g_zero"), sem("g_hi"), sem("g_done")
        out_dma, st_dma = sem("out_dma"), sem("st_dma")
        chain_d, chain_a = sem("vector_chain"), sem("scalar_chain")
        g_mm, fg_ready, l_ready, rows_ready, em_ready = (sem(n) for n in ("g_mm", "fg_ready", "l_ready", "rows_ready", "em_ready"))
        at_mm, acol_ready, mb_mm, dm_ready, d_ready, ei_mm, ei_ready = (
            sem(n) for n in ("at_mm", "acol_ready", "mb_mm", "dm_ready", "d_ready", "ei_mm", "ei_ready"))
        tok_mm, tok_ready, qk_mm, wts_ready, num_mm, den_mm, den_used = (
            sem(n) for n in ("tok_mm", "tok_ready", "qk_mm", "wts_ready", "num_mm", "den_mm", "den_used"))
        sqn_ready, stp_mm, outp_ready, sts_mm, outs_ready, ssq_mm = (
            sem(n) for n in ("sqn_ready", "stp_mm", "outp_ready", "sts_mm", "outs_ready", "ssq_mm"))
        y_ready, sd_ready, th_ready, hn_used, m_ready, mhi_ready, mlo_ready = (
            sem(n) for n in ("y_ready", "sd_ready", "th_ready", "hn_used", "m_ready", "mhi_ready", "mlo_ready"))
        rcs_ready, t1_ready, rope_done, ks_ready, vt_mm, vt_ready = (
            sem(n) for n in ("rcs_ready", "t1_ready", "rope_done", "ks_ready", "vt_mm", "vt_ready"))
        s_mm, neg_ready, exp_ready, p_ready, pt_mm, pt_ready, pv_mm, ohi_ready, olo_ready = (
            sem(n) for n in ("s_mm", "neg_ready", "exp_ready", "p_ready", "pt_mm", "pt_ready", "pv_mm", "ohi_ready", "olo_ready"))
        sw_mm, y_out = sem("sw_mm"), sem("y_out")
        y_dma = sem("y_dma")

        block = ctx.enter_context(nc.Block())

        ITEMS = [("p", c, half) for c in range(KD) for half in range(2)] + [("s", kv // 2, kv % 2) for kv in range(KV)]

        TAIL_TICKS = range(12, len(ITEMS) + 2)

        @block.sync
        def _(sp):
            def load(src, L, it, u):
                dst = raw[:, u % 2, 0:2 * L * P]
                sp.dma_start(dst, src).then_inc(landed[u % 2], 16)

            for h in range(2):
                sp.dma_start(x[:, 4 * h:4 * h + 4, :], a["xT"][:, 4 * h:4 * h + 4, :]).then_inc(x_in, 16)
            for i, (kind, units, _, L) in enumerate(STAGES):
                src = a[f"w{i}"]
                u0 = FIRST_UNIT[i]
                first = 2 if i == 0 else 0
                for u in range(first):
                    load(src[u], L, 0, u)
                with sp.Fori(0, (units - first) // 2) as it:
                    for u in range(2):
                        sp.wait_ge(lo_done, 4 * it + 2 * (u0 + first + u - 2) + 2)
                        load(src[bass.ds(2 * it + (first + u), 1)].rearrange("a p n -> p (a n)"), L, it, u0 + first + u)

        def split_hi(act, it, c, L):
            act.wait_ge(landed[(c // 2) % 2], 16 * it + 16 * (c // 4 + 1))
            if c >= 4:
                act.wait_ge(piece_done, 4 * it + c - 3)
            src = raw[:, (c // 2) % 2, (c % 2) * L * P:(c % 2 + 1) * L * P]
            dst = whi[:, c % 4, 0:L, :].rearrange("p a b -> p (a b)")
            act.activation(dst, src, ACT.Copy).then_inc(hi_done, 1)

        def split_lo(dve, it, c, L):
            dve.wait_ge(hi_done, 4 * it + c + 1)
            src = raw[:, (c // 2) % 2, (c % 2) * L * P:(c % 2 + 1) * L * P]
            hi = whi[:, c % 4, 0:L, :].rearrange("p a b -> p (a b)").bitcast(F32)
            dst = wlo[:, c % 4, 0:L, :].rearrange("p a b -> p (a b)")
            dve.tensor_tensor(dst, src, hi, ALU.subtract).then_inc(lo_done, 1)

        def ahead(c):
            n = c // 2 + 2
            return TILES[n] if n < UNITS else None

        def products(pe, out, slot, tiles, hi, lo, first, last, before=None):
            for n, (t, k) in enumerate(tiles):
                if before:
                    before(k)
                wh, wl = whi[:, slot, t, :], wlo[:, slot, t, :]
                pe.matmul(out, wh, hi[:, k, :], start=(first and n == 0), stop=False)
                pe.matmul(out, wh, lo[:, k, :], start=False, stop=False)
                mm = pe.matmul(out, wl, hi[:, k, :], start=False, stop=(last and n == len(tiles) - 1))
            return mm

        def in_bank(g):
            return acc[(g + 2) % 4][:, 0:T]

        @block.tensor
        def _(pe):
            norm_no = [0]

            def x_ready(k):
                pe.wait_ge(xlo_done, KD * norm_no[0] + k + 1)

            def ss_sum():
                pe.wait_ge(ss_done, norm_no[0] + 1)
                pe.matmul(mb[3][:, 0:T], ones, ssq[:, :], start=True, stop=True).then_inc(ss_mm, 1)

            def in_piece(it, c, g, G, first_unit=False):
                pe.wait_ge(lo_done, 4 * it + c + 1)
                pe.wait_ge(evac, 4 * it + G - 3) if not (isinstance(it, int) and 4 * it + G < 4) else None
                products(pe, in_bank(g), c % 4, [(k, k) for k in range(KD)], xhi, xlo, True, True).then_inc(piece_done, 1)

            def first_two(c, G):
                for q in range(2):
                    pe.wait_ge(lo_done, c + q + 1)
                    if G + q >= 4:
                        pe.wait_ge(evac, G + q - 3)
                    products(pe, in_bank(q), (c + q) % 4, [(k, k) for k in range(KD - 1)], xhi, xlo, True, False,
                             before=x_ready if q == 0 else None)
                    if q == 0:
                        ss_sum()
                x_ready(KD - 1)
                for q in range(2):
                    products(pe, in_bank(q), (c + q) % 4, [(KD - 1, KD - 1)], xhi, xlo, False, True).then_inc(piece_done, 1)
                norm_no[0] += 1

            def ffn_in(i):
                c0_, G0 = 2 * FIRST_UNIT[i], FIRST_GROUP[i]
                first_two(c0_, G0)
                for q in range(2, 4):
                    in_piece(0, c0_ + q, q, G0 + q)
                with pe.Fori(1, KF // 2) as it:
                    for q in range(4):
                        in_piece(it, c0_ + q, q, G0 + q)

            n_alo = [0]

            def ffn_out(i):
                c0_, G0 = 2 * FIRST_UNIT[i], FIRST_GROUP[i]

                def unit(it, u, before=None):
                    pe.wait_ge(evac, 2 * it + G0 + u - 1)
                    for q in range(2):
                        c = c0_ + 2 * u + q
                        pe.wait_ge(lo_done, 4 * it + c + 1)
                        products(pe, acc[u][:, 0:T], c % 4, [(t, t + 11 * q) for t in range(11)], ahi, alo,
                                 q == 0, q == 1, before).then_inc(piece_done, 1)

                unit(0, 0, before=lambda k: pe.wait_ge(alo_done, n_alo[0] + k + 1))
                n_alo[0] += KF
                unit(0, 1)
                with pe.Fori(1, 4) as it:
                    for u in range(2):
                        unit(it, u)

            def mix_out(i, ready):
                c0_, G0 = 2 * FIRST_UNIT[i], FIRST_GROUP[i]
                for m in range(KD):
                    pe.wait_ge(evac, G0 if m == 0 else G0 + m - 1)
                    pe.wait_ge(lo_done, c0_ + m + 1)
                    products(pe, acc[m % 2][:, 0:T], (c0_ + m) % 4, [(k, k) for k in range(KD)], ahi, alo, True, True,
                             ready if m == 0 else None).then_inc(piece_done, 1)

            def gates():
                pe.wait_ge(g_done, 2)
                for k in range(KD):
                    for n, (wt, xt) in enumerate(((ghi, xhi), (ghi, xlo), (glo, xhi))):
                        mm = pe.matmul(mb[0][:, 0:T], wt[:, k, :], xt[:, k, :], start=(k == 0 and n == 0),
                                       stop=(k == KD - 1 and n == 2))
                mm.then_inc(g_mm, 1)

            def row_spread(part):
                if part == 0:
                    pe.wait_ge(rows_ready, 1)
                    for t, (s, n) in enumerate(TOK):
                        mm = pe.transpose(mb[1][0:n, NH * t:NH * t + NH], row[0][:, s:s + n], ident[0:NH, 0:NH])
                    mm.then_inc(at_mm, 1)
                    for h in range(NH):
                        if h >= 2:
                            pe.wait_ge(dm_ready, 3 * (h - 1))
                        pe.matmul(mb[2 + h % 2][:, 0:T], sel[0:NH, h, :], row[5], start=True, stop=True).then_inc(mb_mm, 1)
                else:
                    pe.wait_ge(em_ready, 2)
                    for h in range(NH):
                        if h < 2:
                            pe.wait_ge(dm_ready, 3 * (h + 3))
                        else:
                            pe.wait_ge(ei_ready, 2 * (h - 1))
                        pe.matmul(mb[2 + h % 2][:, 0:T + TS], sel[0:NH, h, :], r_em, start=True, stop=True).then_inc(ei_mm, 1)

            def head_work(h, hook, G0):
                b = h % 2
                if hook == 0:
                    pe.wait_ge(evac, G0 + 6 * h + 4)
                    if h >= 1:
                        pe.wait_ge(hn_used, 2 * h)
                    else:
                        pe.wait_ge(ei_ready, 2 * NH)
                    for t, (s, n) in enumerate(TOK):
                        for j, src in enumerate((kT[:, b], vT[:, b, 0], vT[:, b, 1])):
                            mm = pe.transpose(mb[t][0:n, j * P:(j + 1) * P], src[:, s:s + n], ident)
                        mm.then_inc(tok_mm, 1)
                    if h >= 1:
                        pe.wait_ge(outs_ready, h)
                    pe.matmul(mb[3][:, 0:256], kT[:, b, 0:128], qT[:, b, 0:256], start=True, stop=True)
                    pe.matmul(mb[3][:, 256:384], kT[:, b, 128:256], qT[:, b, 128:256], start=True, stop=True)
                    pe.matmul(mb[3][0:TS, 384:416], kT[:, b, 256:288], qT[:, b, 256:288], start=True, stop=True).then_inc(qk_mm, 1)
                if hook == 1:
                    pe.wait_ge(tok_ready, 6 * (h + 1))
                    pe.wait_ge(wts_ready, 4 * (h + 1))
                    for e in range(3):
                        if e < 2:
                            src = [vtok[0:n, t, e * P:(e + 1) * P] for t, (_, n) in enumerate(TOK)]
                            st = c0[:, h, e * P:(e + 1) * P]
                        else:
                            src, st = [ones[0:n, :] for _, n in TOK], n0rep
                        kw = dict(skip_group_check=True)
                        pe.matmul(mb[e][:, 0:256], src[0], wts[:, 0:256], start=True, stop=False, **kw)
                        pe.matmul(mb[e][:, 128:256], src[1], wts[:, 256:384], start=False, stop=False, **kw)
                        pe.matmul(mb[e][:, 256:288], src[2], wts[0:TS, 384:416], start=False, stop=False, **kw)
                        mm = pe.matmul(mb[e][:, 256:288], st, qi, start=False, stop=True, **kw)
                        if e == 1:
                            mm.then_inc(num_mm, 1)
                    mm.then_inc(den_mm, 1)
                if hook == 2:
                    for t in range(2):
                        mm = pe.matmul(mb[3][:, 0:DV + 1], ktok[:, t, :], vtok[:, t, :], start=(t == 0), stop=(t == 1))
                    mm.then_inc(stp_mm, 1)
                if hook == 3:
                    pe.wait_ge(den_used, h + 1)
                    pe.wait_ge(sqn_ready, h + 1)
                    pe.matmul(mb[2][:, 0:T], ones, sqn[:, 0, :], start=True, stop=False)
                    pe.matmul(mb[2][:, 0:T], ones, sqn[:, 1, :], start=False, stop=True).then_inc(ssq_mm, 1)
                if hook == 4:
                    pe.wait_ge(outp_ready, h + 1)
                    pe.matmul(mb[3][:, 0:DV + 1], ktok[0:TS, 2, :], vtok[0:TS, 2, :], start=True, stop=True).then_inc(sts_mm, 1)

            def mlstm_in(i):
                c0_, G0 = 2 * FIRST_UNIT[i], FIRST_GROUP[i]
                for h in range(NH + 1):
                    for q in range(6):
                        n = 6 * h + q
                        if n == 0:
                            first_two(c0_, G0)
                        elif n > 1 and h < NH:
                            in_piece(0, c0_ + n, n, G0 + n)
                        if h == 0 and q == 1:
                            gates()
                        if h == 0 and q == 3:
                            row_spread(0)
                        if h == 0 and q == 4:
                            row_spread(1)
                        if h >= 1:
                            head_work(h - 1, q, G0)

            def v_tokens():
                for t, (s, n) in enumerate(TOK):
                    if t == 2:
                        pe.wait_ge(vt_ready, 1)
                    for c in range(2):
                        mm = pe.transpose(mb[2 + t % 2][0:n, c * P:(c + 1) * P], s_vT[:, c, s:s + n], ident)
                    mm.then_inc(vt_mm, 1)

            def tick(t):
                if t < len(ITEMS):
                    kind, c, half = ITEMS[t]
                    lo_, hi_ = half * HD, half * HD + HD
                    if t >= 2:
                        pe.wait_ge(neg_ready, t - 1)
                    bank = mb[t % 2]
                    if kind == "p":
                        pe.wait_ge(rope_done, 2 + c + 1)
                        kk = s_k[lo_:hi_, c // 4, :]
                        pe.matmul(bank[:, 0:128], s_q[lo_:hi_, c, 0:128], kk[:, 0:128], start=True, stop=True)
                        mm = pe.matmul(bank[:, 128:384], s_q[lo_:hi_, c, 128:256], kk[:, 0:256], start=True, stop=True)
                    else:
                        pe.wait_ge(rope_done, 2 + KD)
                        pe.wait_ge(ks_ready, 2 + KD)
                        mm = pe.matmul(bank[:, 0:CACHE + TS], s_qs[lo_:hi_, c, :], ks[lo_:hi_, c, :],
                                       start=True, stop=True)
                    mm.then_inc(s_mm, 1)
                if 1 <= t <= len(ITEMS):
                    kind = ITEMS[t - 1][0]
                    pe.wait_ge(p_ready, t)
                    if t == 1:
                        pe.wait_ge(vt_ready, 3)
                    if t >= 2:
                        pe.wait_ge(pt_ready, t - 1)
                    pr = prob[:, (t - 1) % 2, :]
                    if kind == "p":
                        for j in range(3):
                            mm = pe.transpose(mb[2][:, j * P:(j + 1) * P], pr[:, j * P:(j + 1) * P], ident)
                    else:
                        pe.transpose(mb[2][:, 0:P], pr[:, 0:P], ident)
                        mm = pe.transpose(mb[2][0:TS, P:2 * P], pr[:, P:P + TS], ident)
                    mm.then_inc(pt_mm, 1)
                if t >= 2:
                    n = t - 2
                    kind, c, half = ITEMS[n]
                    if n % 2 == 0 and n >= 2:
                        pe.wait_ge(olo_ready, n // 2)
                    pe.wait_ge(pt_ready, n + 1)
                    lo_, hi_ = half * HD, half * HD + HD
                    pt = probT[:, n % 2, :]
                    kw = dict(skip_group_check=True)
                    if kind == "p":
                        kv = 2 * (c // 4) + half
                        v0, v1 = (s_v[:, j, kv * HD:(kv + 1) * HD] for j in range(2))
                        pe.matmul(mb[3][lo_:hi_, 0:128], v0, pt[:, 0:128], start=True, stop=False, **kw)
                        pe.matmul(mb[3][lo_:hi_, 128:256], v0, pt[:, 128:256], start=False, stop=False, **kw)
                        mm = pe.matmul(mb[3][lo_:hi_, 128:256], v1, pt[:, 256:384], start=False, stop=True, **kw)
                    else:
                        kv = 2 * c + half
                        pe.matmul(mb[3][lo_:hi_, 0:128], vc[:, kv * HD:(kv + 1) * HD], pt[:, 0:128], start=True, stop=False, **kw)
                        mm = pe.matmul(mb[3][lo_:hi_, 0:128], s_v[0:TS, 2, kv * HD:(kv + 1) * HD], pt[0:TS, 128:256],
                                       start=False, stop=True, **kw)
                    mm.then_inc(pv_mm, 1)

            def swa(i):
                c0_, G0 = 2 * FIRST_UNIT[i], FIRST_GROUP[i]
                pe.wait_ge(mix_in, MIX_SWA)
                for g, (what, n) in enumerate(SWA_GROUPS):
                    if what == "piece":
                        if n == 0:
                            first_two(c0_, G0)
                        if n > 1:
                            in_piece(0, c0_ + n, g, G0 + g)
                    else:
                        pe.wait_ge(evac, max(G0 + SWA_GROUPS.index(("piece", rope_piece(n))) + 1, G0 + g - 3))
                        pe.matmul(in_bank(g), perm, s_raw[:, n % 2, :], start=True, stop=True).then_inc(sw_mm, 1)
                    if (what, n) == ("piece", 4):
                        pe.wait_ge(evac, G0 + SWA_GROUPS.index(("piece", 3)) + 1)
                        v_tokens()
                    for t in SWA_TICKS.get((what, n), ()):
                        tick(t)
                for t in TAIL_TICKS:
                    tick(t)

            pe.wait_ge(par_in, PAR_IN)
            ffn_in(0)
            ffn_out(1)
            mlstm_in(2)
            mix_out(3, lambda k: pe.wait_ge(mlo_ready, k // 2 + 1))
            ffn_in(4)
            ffn_out(5)
            ffn_in(6)
            ffn_out(7)
            swa(8)
            mix_out(9, lambda k: pe.wait_ge(olo_ready, 10) if k == 0 else None)
            ffn_in(10)
            ffn_out(11)
            ss_sum()

        @block.scalar
        def _(act):
            n_s = [0]

            def hi_of_x(m, norm):
                act.activation(xhi[:, m, :], x[:, m, :], ACT.Copy, scale=norms[:, norm, m:m + 1]).then_inc(xhi_done, 1)

            def rms(done):
                act.wait_ge(ss_mm, done)
                act.activation(std[:, :], mb[3][:, 0:T], ACT.Sqrt, bias=epst[:, :], scale=1.0 / D).then_inc(std_done, 1)

            def hi_ahead(it, c):
                L = ahead(c)
                if L:
                    split_hi(act, it, c + 4, L)

            def ffn_in(i, norm):
                c0_, G0 = 2 * FIRST_UNIT[i], FIRST_GROUP[i]
                f0 = KF * FFN_NO[i]
                rms(norm + 1)

                def unit(it, u, look):
                    c, G = c0_ + 2 * u, G0 + 2 * u
                    if look:
                        split_hi(act, it, c + 4, look)
                    act.wait_ge(evac, 4 * it + G + 1)
                    act.activation(f_silu[:, u % 2, :], f_gate[:, u % 2, :], ACT.Silu).then_inc(silu_done, 1)
                    if look:
                        split_hi(act, it, c + 5, look)
                    act.wait_ge(prod_done, 2 * it + f0 + u + 1)
                    act.activation(ahi[:, bass.ds(2 * it + u, 1), :], f_prod[:, u % 2:u % 2 + 1, :], ACT.Copy)\
                        .then_inc(ahi_done, 1)

                unit(0, 0, 8)
                unit(0, 1, 8)
                with act.Fori(1, KF // 2 - 1) as it:
                    unit(it, 0, 8)
                    unit(it, 1, 8)
                for u in range(2):
                    unit(KF // 2 - 1, u, 11)

            def ffn_out(i, norm):
                c0_, G0 = 2 * FIRST_UNIT[i], FIRST_GROUP[i]

                def unit(it, u, look):
                    c = c0_ + 2 * u
                    if look:
                        split_hi(act, it, c + 4, look)
                    act.wait_ge(evac, 2 * it + G0 + u + 1)
                    if norm < N_FINAL:
                        act.activation(xhi[:, bass.ds(2 * it + u, 1), :], x[:, bass.ds(2 * it + u, 1), :], ACT.Copy,
                                       scale=norms[:, norm, bass.ds(2 * it + u, 1)]).then_inc(xhi_done, 1)
                    if look:
                        split_hi(act, it, c + 5, look)

                with act.Fori(0, 3) as it:
                    for u in range(2):
                        unit(it, u, 11)
                for u in range(2):
                    unit(3, u, ahead(c0_ + 12 + 2 * u))

            def mix_out(i, norm):
                c0_, G0 = 2 * FIRST_UNIT[i], FIRST_GROUP[i]
                for m in range(KD):
                    hi_ahead(0, c0_ + m)
                    act.wait_ge(evac, G0 + m + 1)
                    hi_of_x(m, norm)

            def gate_logs():
                act.wait_ge(fg_ready, 1)
                n = n_s[0]
                act.activation(row[2], row[1], ACT.Abs).then_inc(chain_a, 1)
                act.wait_ge(chain_a, n + 1)
                act.activation(row[2], row[2], ACT.Exp, scale=-1.0).then_inc(chain_a, 1)
                act.wait_ge(chain_a, n + 2)
                act.activation(row[2], row[2], ACT.Ln, bias=cst[0:NH, P:P + 1]).then_inc(l_ready, 1)
                n_s[0] += 2

            def gate_exps():
                act.wait_ge(rows_ready, 1)
                act.activation(r_em[:, 0:T], row[1], ACT.Exp, scale=-2.0).then_inc(em_ready, 1)
                act.activation(r_em[:, T:T + TS], row[5][:, TP:T], ACT.Exp, scale=-1.0, bias=m0[:, :]).then_inc(em_ready, 1)

            def decays():
                for h in range(NH):
                    act.wait_ge(dm_ready, 3 * h + 3)
                    for t, (lo_, hi_, n) in enumerate(((0, 256, P), (256, 384, P), (384, 416, TS))):
                        v = dec[0:n, h, lo_:hi_]
                        act.activation(v, v, ACT.Exp, scale=-1.0, bias=acol[0:n, NH * t + h:NH * t + h + 1]).then_inc(d_ready, 1)

            def head_work(h, hook, G0):
                b = h % 2
                if hook == 0:
                    act.wait_ge(d_ready, 3 * h + 3)
                    for t, (_, n) in enumerate(TOK):
                        act.wait_ge(tok_mm, 3 * h + t + 1)
                        act.activation(vtok[0:n, t, 0:DV], mb[t][0:n, P:3 * P], ACT.Copy).then_inc(tok_ready, 1)
                        col = (255, 383, 415)[t]
                        act.activation(ktok[0:n, t, :], mb[t][0:n, 0:P], ACT.Copy,
                                       scale=dec[0:n, h, col:col + 1]).then_inc(tok_ready, 1)
                    act.wait_ge(evac, G0 + 6 * h + 6)
                    act.activation(oT[:, b, :, :], oT[:, b, :, :], ACT.Tanh, scale=0.5).then_inc(th_ready, 1)
                if hook == 1:
                    act.wait_ge(num_mm, h + 1)
                    act.activation(sqn[:, :, :], num[:, :, 0:T], ACT.Square).then_inc(sqn_ready, 1)
                    act.wait_ge(den_mm, h + 1)
                    act.activation(den[:, :], mb[2][:, 0:T], ACT.Square).then_inc(den_used, 1)
                if hook == 2:
                    act.wait_ge(stp_mm, h + 1)
                    if h >= 1:
                        act.wait_ge(st_dma, 32 * h)
                    act.activation(outp[:, :], mb[3][:, 0:DV + 1], ACT.Copy).then_inc(outp_ready, 1)
                if hook == 3:
                    act.wait_ge(y_ready, h + 1)
                    act.activation(rinv[:, :], den2[:, :], ACT.Sqrt, scale=1.0 / DV).then_inc(sd_ready, 1)
                if hook == 5:
                    act.wait_ge(m_ready, h + 1)
                    act.activation(ahi[:, 2 * h:2 * h + 2, :], hn[:, :, :], ACT.Copy).then_inc(mhi_ready, 1)

            def mlstm_in(i, norm):
                c0_, G0 = 2 * FIRST_UNIT[i], FIRST_GROUP[i]
                rms(norm + 1)
                for h in range(NH + 1):
                    for q in range(6):
                        if h < NH:
                            hi_ahead(0, c0_ + 6 * h + q)
                        if h == 0 and q == 1:
                            gate_logs()
                        if h == 0 and q == 2:
                            gate_exps()
                        if h == 0 and q == 3:
                            decays()
                        if h >= 1:
                            head_work(h - 1, q, G0)

            def tick(t):
                if t < len(ITEMS):
                    kind, c, half = ITEMS[t]
                    b = t % 2
                    act.wait_ge(neg_ready, t + 1)
                    if kind == "p":
                        head = (2 * (c // 4) + half) * 4 + c % 4
                        parts, sink = ((0, P), (P, 3 * P)), snk[:, head:head + 1]
                    else:
                        parts, sink = ((0, CACHE + TS),), snks[:, 2 * c + half:2 * c + half + 1]
                    for j, (lo_, hi_) in enumerate(parts):
                        v = prob[:, b, lo_:hi_]
                        act.activation(v, v, ACT.Exp, bias=s_neg[:, b, j:j + 1], accum_out=s_sum[:, b, j:j + 1])
                    act.activation(s_sk[:, b, 0:len(parts)], s_neg[:, b, 0:len(parts)], ACT.Exp, bias=sink).then_inc(exp_ready, 1)
                if 1 <= t <= len(ITEMS):
                    n = t - 1
                    act.wait_ge(pt_mm, n + 1)
                    if n >= 2:
                        act.wait_ge(pv_mm, n - 1)
                    if ITEMS[n][0] == "p":
                        act.activation(probT[:, n % 2, :], mb[2][:, 0:3 * P], ACT.Copy).then_inc(pt_ready, 1)
                    else:
                        act.activation(probT[:, n % 2, 0:P], mb[2][:, 0:P], ACT.Copy)
                        act.activation(probT[0:TS, n % 2, P:2 * P], mb[2][0:TS, P:2 * P], ACT.Copy).then_inc(pt_ready, 1)
                if t >= 3 and t % 2 == 1:
                    kind, c, _ = ITEMS[t - 2]
                    act.wait_ge(pv_mm, t - 1)
                    if kind == "p":
                        act.activation(ahi[:, c, 0:TP], mb[3][:, 0:TP], ACT.Copy).then_inc(ohi_ready, 1)
                    else:
                        act.activation(ahi[:, 4 * c:4 * c + 4, TP:T], mb[3][:, 0:P].rearrange("p (g t) -> p g t", g=4),
                                       ACT.Copy).then_inc(ohi_ready, 1)

            def swa(i, norm):
                c0_, G0 = 2 * FIRST_UNIT[i], FIRST_GROUP[i]
                act.wait_ge(mix_in, MIX_SWA)
                rms(norm + 1)
                for what, n in SWA_GROUPS:
                    if what == "piece":
                        hi_ahead(0, c0_ + n)
                    if (what, n) == ("piece", 4):
                        for t, (_, m) in enumerate(TOK):
                            act.wait_ge(vt_mm, t + 1)
                            act.activation(s_v[0:m, t, :], mb[2 + t % 2][0:m, 0:2 * P], ACT.Copy).then_inc(vt_ready, 1)
                    for t in SWA_TICKS.get((what, n), ()):
                        tick(t)
                for t in TAIL_TICKS:
                    tick(t)

            act.dma_start(norms[:, :, :], a["norms"]).then_inc(par_in, 16)
            act.dma_start(cst[:, :], a["cst"][:, 0:3 * P]).then_inc(par_in, 16)
            act.dma_start(graw[:, :, :], a["w_gates"]).then_inc(par_in, 16)
            act.dma_start(bg[:, :], a["b_gates"]).then_inc(par_in, 16)
            act.dma_start(m0[:, :], a["m0"]).then_inc(par_in, 16)
            act.dma_start(c0[:, :, :], a["c0"]).then_inc(par_in, 16)
            act.dma_start(tri[:, :], a["cst"][:, C_TRI:C_TRI + 2 * P]).then_inc(par_in, 16)
            act.dma_start(sel[:, :, :], a["cst"][:, C_SEL:C_SEL + NH * P]).then_inc(par_in, 16)
            act.wait_ge(par_in, PAR_IN)
            act.wait_ge(x_in, 32)
            split_hi(act, 0, 0, 8)
            for m in range(KD):
                hi_of_x(m, N_F1)
                if m < 3:
                    split_hi(act, 0, m + 1, 8)
            act.wait_ge(const_done, 1)
            ffn_in(0, 0)
            act.wait_ge(g_zero, 2)
            for j in range(2):
                act.activation(ghi[:, :, 32 * j:32 * j + NH], graw[:, :, NH * j:NH * j + NH], ACT.Copy).then_inc(g_hi, 1)
            ffn_out(1, 1)
            mlstm_in(2, 1)
            mix_out(3, 2)
            ffn_in(4, 2)
            ffn_out(5, 3)
            ffn_in(6, 3)
            ffn_out(7, 4)
            swa(8, 4)
            mix_out(9, 5)
            ffn_in(10, 5)
            ffn_out(11, 6)
            rms(7)
            act.wait_ge(y_out, KD // 2)
            act.dma_start(a["yT"][:, 0:KD // 2, :], x[:, 0:KD // 2, :]).then_inc(y_dma, 16)
            act.wait_ge(y_out, KD)
            act.dma_start(a["yT"][:, KD // 2:KD, :], x[:, KD // 2:KD, :]).then_inc(y_dma, 16)
            act.wait_ge(y_dma, 32)

        @block.vector
        def _(dve):
            n_d = [0]

            def own(ins):
                n_d[0] += 1
                ins.then_inc(chain_d, 1)
                dve.wait_ge(chain_d, n_d[0])

            def lo_of_x(m, norm, n):
                dve.wait_ge(xhi_done, n)
                dve.scalar_tensor_tensor(xlo[:, m, :], x[:, m, :], norms[:, norm, m:m + 1], xhi[:, m, :].bitcast(F32),
                                         ALU.mult, ALU.subtract).then_inc(xlo_done, 1)

            def rms(done):
                dve.wait_ge(std_done, done)
                dve.reciprocal(rstd[:, :], std[:, :]).then_inc(r_done, 1)
                dve.wait_ge(r_done, done)

            def lo_ahead(it, c):
                L = ahead(c)
                if L:
                    split_lo(dve, it, c + 4, L)

            def ffn_in(i, norm):
                c0_, G0 = 2 * FIRST_UNIT[i], FIRST_GROUP[i]
                f0 = KF * FFN_NO[i]
                rms(norm + 1)

                def unit(it, u, look):
                    c, G = c0_ + 2 * u, G0 + 2 * u
                    b = u % 2
                    dve.wait_ge(piece_done, 4 * it + c + 1)
                    dve.tensor_tensor(f_gate[:, b, :], in_bank(2 * u), rstd[:, :], ALU.mult).then_inc(evac, 1)
                    if look:
                        split_lo(dve, it, c + 4, look)
                    dve.wait_ge(piece_done, 4 * it + c + 2)
                    dve.tensor_tensor(f_up[:, b, :], in_bank(2 * u + 1), rstd[:, :], ALU.mult).then_inc(evac, 1)
                    dve.wait_ge(silu_done, 2 * it + f0 + u + 1)
                    dve.wait_ge(evac, 4 * it + G + 2)
                    dve.tensor_tensor(f_prod[:, b, :], f_silu[:, b, :], f_up[:, b, :], ALU.mult).then_inc(prod_done, 1)
                    if look:
                        split_lo(dve, it, c + 5, look)
                    dve.wait_ge(ahi_done, 2 * it + f0 + u + 1)
                    dve.tensor_tensor(alo[:, bass.ds(2 * it + u, 1), :], f_prod[:, b:b + 1, :],
                                      ahi[:, bass.ds(2 * it + u, 1), :].bitcast(F32), ALU.subtract).then_inc(alo_done, 1)

                unit(0, 0, 8)
                unit(0, 1, 8)
                with dve.Fori(1, KF // 2 - 1) as it:
                    unit(it, 0, 8)
                    unit(it, 1, 8)
                for u in range(2):
                    unit(KF // 2 - 1, u, 11)

            def ffn_out(i, norm):
                c0_, G0 = 2 * FIRST_UNIT[i], FIRST_GROUP[i]

                def unit(it, u, look):
                    c = c0_ + 2 * u
                    m = bass.ds(2 * it + u, 1)
                    if look:
                        split_lo(dve, it, c + 4, look)
                    dve.wait_ge(piece_done, 4 * it + c + 2)
                    dve.scalar_tensor_tensor(x[:, m, :], acc[u][:, 0:T].rearrange("p (a t) -> p a t", a=1), 0.5, x[:, m, :],
                                             ALU.mult, ALU.add).then_inc(evac, 1)
                    if norm < N_FINAL:
                        dve.wait_ge(xhi_done, 2 * it + KD * norm + u + 1)
                        dve.scalar_tensor_tensor(xlo[:, m, :], x[:, m, :], norms[:, norm, m], xhi[:, m, :].bitcast(F32),
                                                 ALU.mult, ALU.subtract).then_inc(xlo_done, 1)
                    if look:
                        split_lo(dve, it, c + 5, look)

                with dve.Fori(0, 3) as it:
                    for u in range(2):
                        unit(it, u, 11)
                for u in range(2):
                    unit(3, u, ahead(c0_ + 12 + 2 * u))

            def mix_out(i, norm):
                c0_, G0 = 2 * FIRST_UNIT[i], FIRST_GROUP[i]
                for m in range(KD):
                    dve.wait_ge(piece_done, c0_ + m + 1)
                    dve.tensor_tensor(x[:, m, :], acc[m % 2][:, 0:T], x[:, m, :], ALU.add).then_inc(evac, 1)
                    lo_of_x(m, norm, KD * norm + m + 1)
                    lo_ahead(0, c0_ + m)

            def gate_rows(part):
                if part == 0:
                    dve.wait_ge(g_mm, 1)
                    dve.tensor_tensor(row[0], mb[0][0:NH, 0:T], rstd[0:NH, :], ALU.mult)
                    own(dve.tensor_tensor(row[1], mb[0][32:32 + NH, 0:T], rstd[32:32 + NH, :], ALU.mult))
                    dve.tensor_scalar(row[1], row[1], bg[:, 1:2], None, ALU.add).then_inc(fg_ready, 1)
                    own(dve.tensor_scalar(row[0], row[0], bg[:, 0:1], None, ALU.add))
                    return
                dve.wait_ge(l_ready, 1)
                dve.wait_ge(fg_ready, 1)
                own(dve.scalar_tensor_tensor(row[3], row[1], 0.0, row[2], ALU.min, ALU.subtract))
                dve.tensor_tensor_scan(row[4][:, 0:TP], one_row, row[3][:, 0:TP], 0.0, ALU.mult, ALU.add)
                own(dve.tensor_tensor_scan(row[4][:, TP:T], one_row[:, 0:TS], row[3][:, TP:T], 0.0, ALU.mult, ALU.add))
                own(dve.tensor_tensor(row[0], row[0], row[4], ALU.subtract))
                dve.tensor_tensor_scan(row[5][:, 0:TP], one_row, row[0][:, 0:TP], 0.0, ALU.mult, ALU.max)
                own(dve.tensor_tensor_scan(row[5][:, TP:T], one_row[:, 0:TS], row[0][:, TP:T], m0[:, 0:1], ALU.mult, ALU.max))
                own(dve.tensor_tensor(row[1], row[4], row[5], ALU.add))
                dve.tensor_copy(mout[:, 0:1], row[1][:, TP - 1:TP])
                dve.tensor_copy(mout[:, 1:2], row[1][:, T - 1:T]).then_inc(rows_ready, 1)

            def decay_rows():
                dve.wait_ge(at_mm, 1)
                dve.tensor_copy(acol[:, 0:2 * NH], mb[1][:, 0:2 * NH])
                dve.tensor_copy(acol[0:TS, 2 * NH:3 * NH], mb[1][0:TS, 2 * NH:3 * NH])
                for h in range(NH):
                    dve.wait_ge(mb_mm, h + 1)
                    bank = mb[2 + h % 2]
                    dve.tensor_tensor(dec[:, h, 0:256], bank[:, 0:256], tri, ALU.add).then_inc(dm_ready, 1)
                    dve.tensor_tensor(dec[:, h, 256:384], bank[:, 128:256], tri[:, 0:P], ALU.add).then_inc(dm_ready, 1)
                    dve.tensor_tensor(dec[0:TS, h, 384:416], bank[0:TS, TP:T], tri[0:TS, 0:TS], ALU.add).then_inc(dm_ready, 1)

            def em_rows():
                for h in range(NH):
                    dve.wait_ge(ei_mm, h + 1)
                    bank = mb[2 + h % 2]
                    dve.tensor_copy(emb[:, h, :], bank[:, 0:T]).then_inc(ei_ready, 1)
                    dve.tensor_copy(intb[:, h, :], bank[:, T:T + TS]).then_inc(ei_ready, 1)

            def head_work(h, hook, G0):
                b = h % 2
                if hook == 0:
                    dve.wait_ge(qk_mm, h + 1)
                    dve.wait_ge(d_ready, 3 * h + 3)
                    dve.wait_ge(ei_ready, 2 * NH)
                    dve.tensor_tensor(wts[:, 0:384], mb[3][:, 0:384], dec[:, h, 0:384], ALU.mult).then_inc(wts_ready, 1)
                    dve.tensor_tensor(wts[0:TS, 384:416], mb[3][0:TS, 384:416], dec[0:TS, h, 384:416], ALU.mult).then_inc(wts_ready, 1)
                    dve.tensor_tensor(qi, qT[:, b, TP:T], intb[:, h, :], ALU.mult).then_inc(wts_ready, 1)
                    dve.tensor_scalar(n0rep, ones, c0[:, h, DV:DV + 1], None, ALU.mult).then_inc(wts_ready, 1)
                if hook == 1:
                    dve.wait_ge(den_used, h + 1)
                    own(dve.tensor_tensor(den[:, :], den[:, :], emb[:, h, :], ALU.max))
                if hook == 3:
                    dve.wait_ge(ssq_mm, h + 1)
                    dve.scalar_tensor_tensor(den2[:, :], den[:, :], DV * EPS, mb[2][:, 0:T], ALU.mult, ALU.add).then_inc(y_ready, 1)
                if hook == 4:
                    dve.wait_ge(sts_mm, h + 1)
                    if h >= 1:
                        dve.wait_ge(st_dma, 32 * h)
                    dve.scalar_tensor_tensor(outs[:, :], c0[:, h, :], intb[:, h, TS - 1:TS], mb[3][:, 0:DV + 1],
                                             ALU.mult, ALU.add).then_inc(outs_ready, 1)
                    dve.wait_ge(sd_ready, h + 1)
                    own(dve.reciprocal(rinv[:, :], rinv[:, :]))
                    for e in range(2):
                        c = 2 * h + e
                        dve.scalar_tensor_tensor(hn[:, e, :], num[:, e, 0:T], norms[:, N_HEAD, c:c + 1], rinv[:, :],
                                                 ALU.mult, ALU.mult).then_inc(hn_used, 1)
                    dve.wait_ge(th_ready, h + 1)
                    dve.wait_ge(hn_used, 2 * h + 2)
                    dve.scalar_tensor_tensor(hn[:, :, :], oT[:, b, :, :], 1.0, hn[:, :, :], ALU.add, ALU.mult).then_inc(m_ready, 1)
                if hook == 5:
                    dve.wait_ge(mhi_ready, h + 1)
                    dve.tensor_tensor(alo[:, 2 * h:2 * h + 2, :], hn[:, :, :], ahi[:, 2 * h:2 * h + 2, :].bitcast(F32),
                                      ALU.subtract).then_inc(mlo_ready, 1)

            def mlstm_in(i, norm):
                c0_, G0 = 2 * FIRST_UNIT[i], FIRST_GROUP[i]
                rms(norm + 1)
                own(dve.tensor_scalar(norms[:, N_HEAD, :], norms[:, N_HEAD, :], 0.5, None, ALU.mult))
                dve.memset(vtok[:, :, DV:DV + 1], 1.0)
                for h in range(NH + 1):
                    b = h % 2
                    for q in range(6):
                        if h < NH:
                            n = 6 * h + q
                            dve.wait_ge(piece_done, c0_ + n + 1)
                            ps = in_bank(n)
                            if q == 0:
                                dve.scalar_tensor_tensor(kT[:, b, :], ps, float(DK) ** -0.5, rstd[:, :], ALU.mult, ALU.mult)\
                                    .then_inc(evac, 1)
                            else:
                                dst = (None, qT[:, b, :], vT[:, b, 0, :], vT[:, b, 1, :], oT[:, b, 0, :], oT[:, b, 1, :])[q]
                                dve.tensor_tensor(dst, ps, rstd[:, :], ALU.mult).then_inc(evac, 1)
                            lo_ahead(0, c0_ + n)
                        if h == 0 and q == 1:
                            gate_rows(0)
                        if h == 0 and q == 2:
                            gate_rows(1)
                        if h == 0 and q == 3:
                            decay_rows()
                        if h == 0 and q == 4:
                            em_rows()
                        if h >= 1:
                            head_work(h - 1, q, G0)

            def tick(t):
                if t < len(ITEMS):
                    kind, c, half = ITEMS[t]
                    b = t % 2
                    dve.wait_ge(s_mm, t + 1)
                    if t >= 2:
                        dve.wait_ge(pt_mm, t - 1)
                    if kind == "p":
                        head = (2 * (c // 4) + half) * 4 + c % 4
                        parts, sink = ((0, P), (P, 3 * P)), snk[:, head:head + 1]
                        offs = (0, P)
                    else:
                        parts, sink = ((0, CACHE + TS),), snks[:, 2 * c + half:2 * c + half + 1]
                        offs = (3 * P,)
                    for j, ((lo_, hi_), o) in enumerate(zip(parts, offs)):
                        ins = dve.tensor_tensor_reduce(prob[:, b, lo_:hi_], mb[b][:, lo_:hi_], mask[:, o:o + hi_ - lo_],
                                                       float(HD) ** -0.5, -3e38, ALU.add, ALU.max, s_mx[:, b, j:j + 1])
                    own(ins)
                    dve.tensor_scalar(s_neg[:, b, 0:len(parts)], s_mx[:, b, 0:len(parts)], sink, -1.0, ALU.max, ALU.mult)\
                        .then_inc(neg_ready, 1)
                if 1 <= t <= len(ITEMS):
                    n = t - 1
                    b = n % 2
                    parts = ((0, P), (P, 3 * P)) if ITEMS[n][0] == "p" else ((0, CACHE + TS),)
                    dve.wait_ge(exp_ready, n + 1)
                    J = len(parts)
                    own(dve.tensor_tensor(s_den[:, b, 0:J], s_sum[:, b, 0:J], s_sk[:, b, 0:J], ALU.add))
                    own(dve.reciprocal(s_inv[:, b, 0:J], s_den[:, b, 0:J]))
                    for j, (lo_, hi_) in enumerate(parts):
                        v = prob[:, b, lo_:hi_]
                        ins = dve.tensor_scalar(v, v, s_inv[:, b, j:j + 1], None, ALU.mult)
                    ins.then_inc(p_ready, 1)
                if t >= 3 and t % 2 == 1:
                    kind, c, _ = ITEMS[t - 2]
                    dve.wait_ge(ohi_ready, (t - 1) // 2)
                    if kind == "p":
                        dve.tensor_tensor(alo[:, c, 0:TP], mb[3][:, 0:TP], ahi[:, c, 0:TP].bitcast(F32), ALU.subtract)\
                            .then_inc(olo_ready, 1)
                    else:
                        dve.tensor_tensor(alo[:, 4 * c:4 * c + 4, TP:T], mb[3][:, 0:P].rearrange("p (g t) -> p g t", g=4),
                                          ahi[:, 4 * c:4 * c + 4, TP:T].bitcast(F32), ALU.subtract).then_inc(olo_ready, 1)

            def swa(i, norm):
                c0_, G0 = 2 * FIRST_UNIT[i], FIRST_GROUP[i]
                rms(norm + 1)
                dve.wait_ge(mix_in, MIX_SWA)
                dve.tensor_tensor(rc, cos, rstd[:, :], ALU.mult).then_inc(rcs_ready, 1)
                own(dve.tensor_tensor(rs, sin, rstd[:, :], ALU.mult))
                for g, (what, n) in enumerate(SWA_GROUPS):
                    if what == "piece":
                        dve.wait_ge(piece_done, c0_ + n + 1)
                        if n in (2, 3):
                            dve.tensor_tensor(s_vT[:, n - 2, :], in_bank(g), rstd[:, :], ALU.mult).then_inc(evac, 1)
                        else:
                            xi = n if n < 2 else n - 2
                            if xi >= 2:
                                dve.wait_ge(t1_ready, xi - 1)
                            dve.tensor_copy(s_raw[:, xi % 2, :], in_bank(g)).then_inc(evac, 1)
                        lo_ahead(0, c0_ + n)
                    else:
                        dve.wait_ge(sw_mm, n + 1)
                        if n >= 2:
                            dve.wait_ge(rope_done, n - 1)
                        dve.tensor_tensor(s_t2[:, n % 2, :], in_bank(g), rs, ALU.mult).then_inc(evac, 1)
                    for t in SWA_TICKS.get((what, n), ()):
                        tick(t)
                for t in TAIL_TICKS:
                    tick(t)

            dve.memset(epst[:, :], EPS).then_inc(const_done, 1)
            dve.memset(ghi[:, :, :].bitcast(F32), 0.0).then_inc(g_zero, 1)
            dve.memset(glo[:, :, :].bitcast(F32), 0.0).then_inc(g_zero, 1)
            dve.wait_ge(par_in, PAR_IN)
            split_lo(dve, 0, 0, 8)
            for m in range(KD):
                lo_of_x(m, N_F1, m + 1)
                if m < 3:
                    split_lo(dve, 0, m + 1, 8)
            ffn_in(0, 0)
            for j in range(2):
                dve.wait_ge(g_hi, j + 1)
                dve.tensor_tensor(glo[:, :, 32 * j:32 * j + NH], graw[:, :, NH * j:NH * j + NH],
                                  ghi[:, :, 32 * j:32 * j + NH].bitcast(F32), ALU.subtract).then_inc(g_done, 1)
            ffn_out(1, 1)
            mlstm_in(2, 1)
            mix_out(3, 2)
            ffn_in(4, 2)
            ffn_out(5, 3)
            ffn_in(6, 3)
            ffn_out(7, 4)
            swa(8, 4)
            mix_out(9, 5)
            ffn_in(10, 5)
            ffn_out(11, 6)
            rms(7)
            for m in range(KD):
                dve.scalar_tensor_tensor(x[:, m, :], x[:, m, :], norms[:, N_FINAL, m:m + 1], rstd[:, :], ALU.mult, ALU.mult)\
                    .then_inc(y_out, 1)

        @block.gpsimd
        def _(pool):
            n_p = [0]

            def squares(norm, done, first=None):
                for m in range(KD):
                    done(m)
                    if m == 0:
                        if norm:
                            pool.wait_ge(ss_mm, norm)
                        pool.tensor_tensor(ssq[:, :], x[:, 0, :], x[:, 0, :], ALU.mult).then_inc(pool_sq, 1)
                        n_p[0] += 1
                        continue
                    pool.tensor_tensor(sqr[:, m % 2, :], x[:, m, :], x[:, m, :], ALU.mult).then_inc(pool_sq, 1)
                    n_p[0] += 1
                    pool.wait_ge(pool_sq, n_p[0])
                    add = pool.tensor_tensor(ssq[:, :], ssq[:, :], sqr[:, m % 2, :], ALU.add)
                    if m == KD - 1:
                        add.then_inc(ss_done, 1)
                    else:
                        add.then_inc(pool_sq, 1)
                        n_p[0] += 1

            def after(i):
                return lambda m: pool.wait_ge(evac, FIRST_GROUP[i] + m + 1)

            pool.wait_ge(x_in, 32)
            squares(0, lambda m: None)
            squares(1, after(1))
            for h in range(NH):
                pool.wait_ge(outp_ready, h + 1)
                pool.dma_start(a["cp"][:, h, :], outp[:, :]).then_inc(st_dma, 16)
                pool.wait_ge(outs_ready, h + 1)
                pool.dma_start(a["cs"][:, h, :], outs[:, :]).then_inc(st_dma, 16)
            pool.dma_start(a["mo"], mout[:, :]).then_inc(out_dma, 16)
            squares(2, after(3))
            pool.wait_ge(mlo_ready, NH)
            pool.wait_ge(ss_done, 3)
            pool.dma_start(vc[:, :], a["cache_v"]).then_inc(mix_in, 16)
            pool.dma_start(ks[:, :, 0:CACHE], a["cache_kT"]).then_inc(mix_in, 16)
            pool.dma_start(work[:, 8768:8768 + 2 * T + N_MASK], a["cst"][:, C_COS:N_CONST]).then_inc(mix_in, 16)
            pool.dma_start(snk[:, :], a["sinks"].to_broadcast([P, AH])).then_inc(mix_in, 16)
            for g in range(4):
                pool.dma_start(snks[TS * g:TS * g + TS, :], a["sinks_g"][g:g + 1, :].to_broadcast([TS, KV])).then_inc(mix_in, 16)
            squares(3, after(5))
            squares(4, after(7))
            G0 = FIRST_GROUP[8]
            pool.wait_ge(rcs_ready, 1)
            pool.wait_ge(mix_in, MIX_SWA)
            for xi in range(2 + KD):
                b = xi % 2
                pool.wait_ge(evac, G0 + SWA_GROUPS.index(("piece", rope_piece(xi))) + 1)
                pool.tensor_tensor(s_t1[:, b, :], s_raw[:, b, :], rc, ALU.mult).then_inc(t1_ready, 1)
                pool.wait_ge(evac, G0 + SWA_GROUPS.index(("swap", xi)) + 1)
                pool.wait_ge(t1_ready, xi + 1)
                dst = s_k[:, xi, :] if xi < 2 else s_q[:, xi - 2, :]
                pool.tensor_tensor(dst, s_t1[:, b, :], s_t2[:, b, :], ALU.add).then_inc(rope_done, 1)
                pool.wait_ge(rope_done, xi + 1)
                c = xi - 2
                again = ks[:, xi, CACHE:CACHE + TS] if xi < 2 else s_qs[:, c // 4, TS * (c % 4):TS * (c % 4) + TS]
                pool.tensor_copy(again, dst[:, TP:T]).then_inc(ks_ready, 1)
            pool.dma_start(a["kT_out"], s_k[:, :, TP - P:T]).then_inc(out_dma, 16)
            pool.wait_ge(vt_ready, 3)
            pool.dma_start(a["v_out"][0:P, :], s_v[:, 1, :]).then_inc(out_dma, 16)
            pool.dma_start(a["v_out"][P:P + TS, :], s_v[0:TS, 2, :]).then_inc(out_dma, 16)
            squares(5, after(9))
            squares(6, after(11))
            pool.wait_ge(st_dma, 32 * NH)
            pool.wait_ge(out_dma, 16 * OUT_DMAS)


def prod(v):
    return int(np.prod(v))


FFN_NO = {0: 0, 4: 1, 6: 2, 10: 3}
PAR_IN = 16 * 8
MIX_SWA = 16 * 8
OUT_DMAS = 4


def rope_piece(xi):
    return xi if xi < 2 else xi + 2


SWA_GROUPS = [("piece", 0), ("piece", 1), ("piece", 2), ("swap", 0), ("piece", 3), ("swap", 1), ("piece", 4)]
for _n in range(5, 12):
    SWA_GROUPS += [("piece", _n), ("swap", _n - 3)]
SWA_GROUPS += [("swap", 9)]
SWA_TICKS = {("swap", c + 3): (2 * c, 2 * c + 1) for c in range(6)}
assert len(SWA_GROUPS) == 22


def layouts(v):
    f = np.ascontiguousarray

    def pieces(wt, per):
        k, n = wt.shape[0] // P, wt.shape[1] // P
        return f(wt.reshape(k, P, n // per, per, P).transpose(2, 1, 3, 0, 4)).reshape(n // per, P, per * k * P)

    def chunks(g):
        return g.reshape(KD, P).T

    def ffn_in(wt):
        gate, up = wt[:, :FF].reshape(D, KF, 1, P), wt[:, FF:].reshape(D, KF, 1, P)
        return pieces(np.concatenate([gate, up], axis=2).reshape(D, 2 * FF), 2)

    a = {}
    x = np.concatenate([v["x_prompt"][0], v["x_sample"][0]])
    a["xT"] = f(x.T.reshape(KD, P, T).transpose(1, 0, 2))
    ffn = [(v[f"ffn_w_in{n}"][i], v[f"ffn_w_out{n}"][i]) for i in range(2) for n in (1, 2)]
    for i, (w_in, w_out) in zip((0, 4, 6, 10), ffn):
        a[f"w{i}"], a[f"w{i + 1}"] = ffn_in(w_in), pieces(w_out, 1)
    m = v["mlstm_w_in"][0]
    hk, hv = NH * DK, NH * DV
    part = [m[:, hk:2 * hk].reshape(D, NH, DK), m[:, 0:hk].reshape(D, NH, DK),
            m[:, 2 * hk:2 * hk + hv].reshape(D, NH, DV), m[:, 2 * hk + hv:2 * hk + 2 * hv].reshape(D, NH, DV)]
    a["w2"] = pieces(np.concatenate(part, axis=2).reshape(D, -1), 2)
    a["w_gates"] = f(m[:, 2 * hk + 2 * hv:].reshape(KD, P, 2 * NH).transpose(1, 0, 2))
    a["w3"] = pieces(v["mlstm_w_out"][0], 2)
    q = v["swa_w_qkv"][0]
    def pairs(t, axis):
        s = t.shape
        t = t.reshape(*s[:axis], 2, 2, 4, HD, *s[axis + 1:])
        return np.swapaxes(t, axis + 1, axis + 2).reshape(s)
    a["w8"] = pieces(np.concatenate([q[:, AH * HD:], pairs(q[:, :AH * HD], 1)], axis=1), 2)
    a["w9"] = pieces(pairs(v["swa_w_out"][0], 0), 2)
    rows = []
    for i in range(2):
        rows += [v["ffn_norm1"][i], v["mix_norm"][i], v["ffn_norm2"][i]]
    rows += [v["final_norm"], v["mlstm_head_norm"][0]]
    a["norms"] = f(np.stack([chunks(r) for r in rows], axis=1))
    a["b_gates"] = f(v["mlstm_b_gates"][0].reshape(2, NH).T)
    a["m0"] = f(v["state_mlstm_m"][0, 0].reshape(NH, 1))
    c = np.concatenate([v["state_mlstm_C"][0, 0], v["state_mlstm_n"][0, 0][:, :, None]], axis=2)
    a["c0"] = f(c.transpose(1, 0, 2))
    a["cache_kT"] = f(v["cache_swa_k"][0, 0].reshape(CACHE, 2, 2 * HD).transpose(2, 1, 0))
    a["cache_v"] = f(v["cache_swa_v"][0, 0].reshape(CACHE, KV * HD))
    a["sinks"] = f(v["swa_sinks"])
    a["sinks_g"] = f(v["swa_sinks"].reshape(KV, 4).T)
    a["cst"] = constants()
    return a


OUTS = {"yT": (P, KD, T), "cp": (P, NH, DV + 1), "cs": (P, NH, DV + 1), "mo": (NH, 2),
        "kT_out": (P, 2, P + TS), "v_out": (P + TS, KV * HD)}


def kernel(**inputs):
    import concourse.bacc as bacc
    from concourse.bass_utils import run_bass_kernel_spmd

    nc = bacc.Bacc("TRN2", target_bir_lowering=False, num_devices=1)
    arrays = layouts({k: np.asarray(t) for k, t in inputs.items()})
    aps = {k: nc.dram_tensor(f"in_{k}", t.shape, F32, kind="ExternalInput").ap() for k, t in arrays.items()}
    aps.update({k: nc.dram_tensor(f"out_{k}", s, F32, kind="ExternalOutput").ap() for k, s in OUTS.items()})
    program(nc, aps)
    r = run_bass_kernel_spmd(nc, [{f"in_{k}": t for k, t in arrays.items()}], core_ids=[0]).results[0]
    o = {k: np.asarray(r[f"out_{k}"]) for k in OUTS}
    y = o["yT"].transpose(1, 0, 2).reshape(D, T).T
    kT = o["kT_out"].transpose(2, 1, 0).reshape(P + TS, KV, HD)
    v = o["v_out"].reshape(P + TS, KV, HD)
    c = {g: o[g].transpose(1, 0, 2) for g in ("cp", "cs")}
    f = np.ascontiguousarray
    return (f(y[None, :TP]), f(y[None, TP:]),
            f(c["cp"][None, None, :, :, :DV]), f(c["cp"][None, None, :, :, DV]), f(o["mo"][:, 0][None, None]),
            f(kT[None, None, :P]), f(v[None, None, :P]),
            f(c["cs"][None, None, :, :, :DV]), f(c["cs"][None, None, :, :, DV]), f(o["mo"][:, 1][None, None]),
            f(kT[None, None, P:]), f(v[None, None, P:]))
```

```python
from contextlib import ExitStack

import numpy as np

import concourse.bass as bass
from concourse import mybir

F32 = mybir.dt.float32
F32R = mybir.dt.float32r
ALU = mybir.AluOpType
ACT = mybir.ActivationFunctionType

P = 128
D = 1024
KD = D // P
TP, TS = 256, 32
T = TP + TS
FF = 11 * D // 4
KF = FF // P
NH, DK, DV = 4, 128, 256
AH, KV, HD = 16, 4, 64
CACHE = 128
PAST = 512
CHUNK, WIN = 64, 2
EPS = 1e-6
BIG = 1e30
Y_POOL = 5
WARM_UP = 16
RAW = 2 * (KF // 2)
TOK = [(0, 128), (128, 128), (256, 32)]

STAGES = [("ffn_in", 22, 44, 8), ("ffn_out", 8, 8, 11), ("mlstm_in", 12, 24, 8), ("mix_out", 4, 8, 8),
          ("ffn_in", 22, 44, 8), ("ffn_out", 8, 8, 11), ("ffn_in", 22, 44, 8), ("ffn_out", 8, 8, 11),
          ("swa_in", 6, 24, 8), ("mix_out", 4, 8, 8), ("ffn_in", 22, 44, 8), ("ffn_out", 8, 8, 11)]
FIRST_UNIT = [sum(s[1] for s in STAGES[:i]) for i in range(len(STAGES) + 1)]
FIRST_GROUP = [sum(s[2] for s in STAGES[:i]) for i in range(len(STAGES) + 1)]
UNITS = FIRST_UNIT[-1]
TILES = [s[3] for s in STAGES for _ in range(s[1])]
BANK = 2

SWA_PIECES = ["k0", "v0", "q0", "q1", "q2", "q3", "k1", "v1", "q4", "q5", "q6", "q7"]
ROPE = [p for p in SWA_PIECES if p[0] != "v"]
SWA_GROUPS = []
for _n, _p in enumerate(SWA_PIECES + [None]):
    SWA_GROUPS += [("piece", _p)] * (_p is not None)
    if _n:
        SWA_GROUPS.append(("turn" if SWA_PIECES[_n - 1][0] == "v" else "swap", SWA_PIECES[_n - 1]))
ITEMS = [it for i in range(2) for it in
         [("p", c, half) for c in range(4 * i, 4 * i + 4) for half in range(2)] + [("s", i, half) for half in range(2)]]
SWA_TICKS = {}
for _c, _n in ((0, 4), (1, 5), (2, 6), (3, 7), (4, 8), (5, 10), (6, 11)):
    SWA_TICKS[SWA_GROUPS[2 * _n - 1]] = 2 * _c
    SWA_TICKS[SWA_GROUPS[2 * _n]] = 2 * _c + 1
TAIL_TICKS = range(14, len(ITEMS) + 4)
HEAD_START = (7, 12, 17, 22)
HEAD_STEPS = {p + s: (h, s) for h, p in enumerate(HEAD_START) for s in range(5)}


def group_of(what, piece):
    return SWA_GROUPS.index((what, piece))


N_F1, N_MIX, N_F2, N_FINAL, N_HEAD = 0, 1, 2, 6, 7

C_ID, C_ONE, C_PERM, C_TRI, C_SEL = 0, 128, 256, 384, 640
C_COS = C_SEL + NH * P
C_SIN = C_COS + T
C_MASK = C_SIN + T
N_MASK = 3 * P + CACHE + TS
N_CONST = C_MASK + N_MASK


def constants():
    c = np.zeros((P, N_CONST), np.float32)
    p = np.arange(P)
    c[:, C_ID:C_ID + P] = np.eye(P)
    c[:, C_ONE:C_ONE + P] = 1.0
    c[p, C_PERM + (p ^ 32)] = 1.0
    c[:, C_TRI:C_TRI + P] = np.where(p[:, None] > p[None, :], BIG, 0.0)
    for h in range(NH):
        c[h, C_SEL + h * P:C_SEL + (h + 1) * P] = 1.0
    pos = np.concatenate([np.arange(TP), PAST + np.arange(TS)]).astype(np.float32)
    inv = (np.float32(10000.0) ** (-np.arange(0, HD, 2, dtype=np.float32) / np.float32(HD))).astype(np.float32)
    ang = inv[p % 32][:, None] * pos[None, :]
    c[:, C_COS:C_COS + T] = np.cos(ang)
    c[:, C_SIN:C_SIN + T] = np.sin(ang) * np.where(p % HD < 32, -1.0, 1.0)[:, None]
    for tile in range(2):
        q = (tile * P + p) // CHUNK
        k = np.arange((tile + 1) * P) // CHUNK
        ok = (k[None, :] <= q[:, None]) & (k[None, :] >= q[:, None] - WIN)
        at = C_MASK + tile * P
        c[:, at:at + (tile + 1) * P] = np.where(ok, 0.0, -BIG)
    return c


def program(nc, a):
    ctx = ExitStack()
    with ctx:
        def sb(name, shape, dt=F32):
            return ctx.enter_context(nc.sbuf_tensor(name, shape, dt))

        def sem(name):
            return ctx.enter_context(nc.semaphore(name))

        raw = sb("raw", [P, 2, RAW * P])
        whi = sb("whi", [P, 4, KF // 2, P], F32R)
        wlo = sb("wlo", [P, 4, KF // 2, P], F32R)
        x = sb("x", [P, KD, T])
        xhi = sb("xhi", [P, KD, T], F32R)
        xlo = sb("xlo", [P, KD, T], F32R)
        ahi = sb("ahi", [P, KF, T], F32R)
        alo = sb("alo", [P, KF, T], F32R)
        rstd = sb("rstd", [P, T])
        std = sb("std", [P, T])
        ssq = sb("ssq", [P, T])
        sqr = sb("sqr", [P, 2, T])
        norms = sb("norms", [P, 8, KD])
        epst, warm = sb("epst", [P, 1]), sb("warm", [P, 1])
        cst = sb("cst", [P, 3 * P])
        ghi = sb("ghi", [P, KD, P], F32R)
        glo = sb("glo", [P, KD, P], F32R)
        graw = sb("graw", [P, KD, 2 * NH])
        bg = sb("bg", [NH, 2])
        m0 = sb("m0", [NH, 1])
        mout = sb("mout", [NH, 2])
        acol = sb("acol", [P, 3 * NH])
        one_row = cst[0:NH, P:P + 1].to_broadcast([NH, TP])
        work = sb("work", [P, 12496])
        ident, ones, perm = cst[:, 0:P], cst[:, P:2 * P], cst[:, 2 * P:3 * P]

        def w(at, *shape):
            n = int(np.prod(shape))
            v = work[:, at:at + n]
            if len(shape) == 2:
                v = v.rearrange("p (a b) -> p a b", a=shape[0])
            if len(shape) == 3:
                v = v.rearrange("p (a b c) -> p a b c", a=shape[0], b=shape[1])
            return v

        x_squares = w(0, KD // 2, T)
        f_gate, f_up, f_silu, f_prod = (w(i * 2 * T, 2, T) for i in range(4))
        xg = w(4 * 2 * T, KD, T)
        kT, qT, vT, oT = w(0, 2, T), w(576, 2, T), w(1152, 2, 2, T), w(2304, 2, 2, T)
        ktok, vtok = w(3456, 3, P), w(3840, 3, DV + 1)
        dec = w(4612, NH, 416)
        emb, intb = w(6276, NH, T), w(7428, NH, TS)
        wts, qi, n0rep = w(7556, 416), w(7972, TS), w(8004, P)
        sqn, den, rinv, hn, den2 = w(8132, 2, T), w(8708, T), w(8996, T), w(9284, 2, T), w(9860, T)
        row = [work[0:NH, 8132 + i * T:8132 + (i + 1) * T] for i in range(7)]
        r_em = work[0:NH, 8132 + 6 * T:8132 + 7 * T + TS]
        outp, outs, c0 = w(10180, DV + 1), w(10438, DV + 1), w(10696, NH, DV + 1)
        tri, sel = w(11724, 2 * P), w(11980, NH, P)
        s_raw, s_t1, s_t2, s_vT = w(0, 2, T), w(576, 2, T), w(1152, 2, T), w(1728, T)
        s_q, s_k, s_v = w(2304, KD, T), w(4608, 2, T), w(5184, 3, 2 * P)
        rc, rs = w(5952, T), w(6240, T)
        prob, probT = w(6528, 4, 3 * P), w(10176, 4, 3 * P)
        s_mx, s_neg, s_sum, s_sk, s_den, s_inv = (w(8064 + 4 * i, 2, 2) for i in range(6))
        vc, ks = w(8192, 2 * P), w(8448, 2, CACHE + TS)
        cos, sin = w(8768, T), w(9056, T)
        mask = w(9344, N_MASK)
        snk, snks = w(9888, AH), w(9904, KV)
        s_qs = w(9920, 2, 4 * TS)

        acc = [ctx.enter_context(nc.psum_tensor(f"acc{i}", [P, 512], F32)) for i in range(4)]
        num = ctx.enter_context(nc.psum_tensor("num", [P, 2, 512], F32))
        mb = [num[:, 0, :], num[:, 1, :],
              ctx.enter_context(nc.psum_tensor("mb2", [P, 512], F32))[:, :],
              ctx.enter_context(nc.psum_tensor("mb3", [P, 512], F32))[:, :]]

        landed = [sem("landed0"), sem("landed1")]
        hi_done, lo_done = sem("hi_done"), sem("lo_done")
        piece_done = sem("piece_done")
        evac = sem("evac")
        first_in = sem("first_in")
        x_in = [sem(f"x_in{i}") for i in range(KD // 2)]
        norms_in, cst_in, par_in, mix_in = sem("norms_in"), sem("cst_in"), sem("par_in"), sem("mix_in")
        x_sq = sem("x_sq")
        silu_done, prod_done, ahi_done, alo_done = sem("silu_done"), sem("prod_done"), sem("ahi_done"), sem("alo_done")
        xhi_done, xlo_done = sem("xhi_done"), sem("xlo_done")
        pool_sq, ss_done, ss_mm, std_done, r_done = (sem(n) for n in ("pool_sq", "ss_done", "ss_mm", "std_done", "r_done"))
        const_done = sem("const_done")
        g_zero, g_hi, g_done = sem("g_zero"), sem("g_hi"), sem("g_done")
        out_dma, st_dma = sem("out_dma"), sem("st_dma")
        chain_d, chain_a = sem("vector_chain"), sem("scalar_chain")
        g_mm, fg_ready, l_ready, rows_ready, em_ready = (sem(n) for n in ("g_mm", "fg_ready", "l_ready", "rows_ready", "em_ready"))
        at_mm, acol_ready, mb_mm, dm_ready, d_ready, ei_mm, ei_ready = (
            sem(n) for n in ("at_mm", "acol_ready", "mb_mm", "dm_ready", "d_ready", "ei_mm", "ei_ready"))
        tok_mm, tok_ready, qk_mm, wts_ready, num_mm, den_mm, den_used = (
            sem(n) for n in ("tok_mm", "tok_ready", "qk_mm", "wts_ready", "num_mm", "den_mm", "den_used"))
        sqn_ready, stp_mm, outp_ready, sts_mm, outs_ready, ssq_mm = (
            sem(n) for n in ("sqn_ready", "stp_mm", "outp_ready", "sts_mm", "outs_ready", "ssq_mm"))
        y_ready, sd_ready, th_ready, hn_used, m_ready, mhi_ready, mlo_ready = (
            sem(n) for n in ("y_ready", "sd_ready", "th_ready", "hn_used", "m_ready", "mhi_ready", "mlo_ready"))
        rcs_ready, t1_ready, rope_done, ks_ready = (sem(n) for n in ("rcs_ready", "t1_ready", "rope_done", "ks_ready"))
        s_mm, neg_ready, exp_ready, p_ready, pt_mm, pt_ready, pv_mm, ohi_ready, olo_ready = (
            sem(n) for n in ("s_mm", "neg_ready", "exp_ready", "p_ready", "pt_mm", "pt_ready", "pv_mm", "ohi_ready", "olo_ready"))
        turn_mm, y_out, y_out_pool = sem("turn_mm"), sem("y_out"), sem("y_out_pool")
        y_dma = sem("y_dma")

        block = ctx.enter_context(nc.Block())

        @block.sync
        def _(sp):
            def load(src, L, it, u):
                dst = raw[:, u % 2, 0:2 * L * P]
                sp.dma_start(dst, src).then_inc(landed[u % 2], 16)

            half = TILES[0] * P
            for n in range(KD // 2):
                if n == 0:
                    sp.dma_start(raw[:, 0, 0:half], a["w0"][0][:, 0:half]).then_inc(first_in, 16)
                if n == 2:
                    sp.dma_start(raw[:, 0, half:2 * half], a["w0"][0][:, half:2 * half]).then_inc(landed[0], 16)
                sp.dma_start(x[:, 2 * n:2 * n + 2, :], a["xT"][:, 2 * n:2 * n + 2, :]).then_inc(x_in[n], 16)
            for i, (kind, units, _, L) in enumerate(STAGES):
                src = a[f"w{i}"]
                u0 = FIRST_UNIT[i]
                first = 2 if i == 0 else 0
                if i == 0:
                    load(src[1], L, 0, 1)
                with sp.Fori(0, (units - first) // 2) as it:
                    for u in range(2):
                        sp.wait_ge(lo_done, 4 * it + 2 * (u0 + first + u - 2) + 2)
                        load(src[bass.ds(2 * it + (first + u), 1)].rearrange("a p n -> p (a n)"), L, it, u0 + first + u)

        def split_hi(act, it, c, L):
            if c == 0 and isinstance(it, int):
                act.wait_ge(first_in, 16)
            else:
                act.wait_ge(landed[(c // 2) % 2], 16 * it + 16 * (c // 4 + 1))
            if c >= 4:
                act.wait_ge(piece_done, 4 * it + c - 3)
            src = raw[:, (c // 2) % 2, (c % 2) * L * P:(c % 2 + 1) * L * P]
            dst = whi[:, c % 4, 0:L, :].rearrange("p a b -> p (a b)")
            act.activation(dst, src, ACT.Copy).then_inc(hi_done, 1)

        def split_lo(dve, it, c, L):
            dve.wait_ge(hi_done, 4 * it + c + 1)
            src = raw[:, (c // 2) % 2, (c % 2) * L * P:(c % 2 + 1) * L * P]
            hi = whi[:, c % 4, 0:L, :].rearrange("p a b -> p (a b)").bitcast(F32)
            dst = wlo[:, c % 4, 0:L, :].rearrange("p a b -> p (a b)")
            dve.tensor_tensor(dst, src, hi, ALU.subtract).then_inc(lo_done, 1)

        def ahead(c):
            n = c // 2 + 2
            return TILES[n] if n < UNITS else None

        def products(pe, out, slot, tiles, hi, lo, first, last, before=None):
            for n, (t, k) in enumerate(tiles):
                if before:
                    before(k)
                wh, wl = whi[:, slot, t, :], wlo[:, slot, t, :]
                pe.matmul(out, wh, hi[:, k, :], start=(first and n == 0), stop=False)
                pe.matmul(out, wh, lo[:, k, :], start=False, stop=False)
                mm = pe.matmul(out, wl, hi[:, k, :], start=False, stop=(last and n == len(tiles) - 1))
            return mm

        def group_bank(g):
            return acc[(g + BANK) % 4][:, 0:T]

        def spread_bank(h):
            return mb[(h + 2) % 4]

        @block.tensor
        def _(pe):
            norm_no = [0]

            def x_ready(k):
                pe.wait_ge(xlo_done, KD * norm_no[0] + k + 1)

            def ss_sum():
                if norm_no[0] == 0:
                    pe.wait_ge(cst_in, 16)
                pe.wait_ge(ss_done, norm_no[0] + 1)
                pe.matmul(mb[3][:, 0:T], ones, ssq[:, :], start=True, stop=True).then_inc(ss_mm, 1)

            def in_piece(i, it, c, g, G):
                pe.wait_ge(lo_done, 4 * it + c + 1)
                pe.wait_ge(evac, 4 * it + G - 3) if not (isinstance(it, int) and 4 * it + G < 4) else None
                products(pe, group_bank(g), c % 4, [(k, k) for k in range(KD)], xhi, xlo, True, True).then_inc(piece_done, 1)

            def first_two(i, c, G):
                for ks in (range(0, 4), range(4, KD - 1), range(KD - 1, KD)):
                    for q in range(2):
                        if ks[0] == 0:
                            pe.wait_ge(lo_done, c + q + 1)
                            if G + q >= 4:
                                pe.wait_ge(evac, G + q - 3)
                        mm = products(pe, group_bank(q), (c + q) % 4, [(k, k) for k in ks], xhi, xlo,
                                      ks[0] == 0, ks[-1] == KD - 1, before=x_ready if q == 0 else None)
                        if ks[-1] == KD - 1:
                            mm.then_inc(piece_done, 1)
                ss_sum()
                norm_no[0] += 1

            def ffn_in(i):
                c0_, G0 = 2 * FIRST_UNIT[i], FIRST_GROUP[i]
                first_two(i, c0_, G0)
                for q in range(2, 4):
                    in_piece(i, 0, c0_ + q, q, G0 + q)
                with pe.Fori(1, KF // 2) as it:
                    for q in range(4):
                        in_piece(i, it, c0_ + q, q, G0 + q)

            n_alo = [0]

            def ffn_out(i):
                c0_, G0 = 2 * FIRST_UNIT[i], FIRST_GROUP[i]

                def unit(it, u, before=None):
                    pe.wait_ge(evac, 2 * it + G0 + u - 1)
                    for q in range(2):
                        c = c0_ + 2 * u + q
                        pe.wait_ge(lo_done, 4 * it + c + 1)
                        products(pe, acc[u][:, 0:T], c % 4, [(t, t + 11 * q) for t in range(11)], ahi, alo,
                                 q == 0, q == 1, before).then_inc(piece_done, 1)

                unit(0, 0, before=lambda k: pe.wait_ge(alo_done, n_alo[0] + k + 1))
                n_alo[0] += KF
                unit(0, 1)
                with pe.Fori(1, 4) as it:
                    for u in range(2):
                        unit(it, u)

            def mix_partial(i, m, chunks):
                c = 2 * FIRST_UNIT[i] + m
                if chunks[0] == 0:
                    pe.wait_ge(evac, FIRST_GROUP[i] - 3 + m)
                    pe.wait_ge(lo_done, c + 1)
                mm = products(pe, group_bank(m), c % 4, [(k, k) for k in chunks], ahi, alo,
                              chunks[0] == 0, chunks[-1] == KD - 1)
                if chunks[-1] == KD - 1:
                    mm.then_inc(piece_done, 1)

            def mix_rest(i):
                c0_, G0 = 2 * FIRST_UNIT[i], FIRST_GROUP[i]
                for m in range(4, KD):
                    pe.wait_ge(evac, G0 + m - 3)
                    pe.wait_ge(lo_done, c0_ + m + 1)
                    products(pe, group_bank(m), (c0_ + m) % 4, [(k, k) for k in range(KD)], ahi, alo, True, True)\
                        .then_inc(piece_done, 1)

            def gates():
                pe.wait_ge(g_done, 2)
                for k in range(KD):
                    for n, (wt, xt) in enumerate(((ghi, xhi), (ghi, xlo), (glo, xhi))):
                        mm = pe.matmul(mb[0][:, 0:T], wt[:, k, :], xt[:, k, :], start=(k == 0 and n == 0),
                                       stop=(k == KD - 1 and n == 2))
                mm.then_inc(g_mm, 1)

            def row_spread(part):
                if part == 0:
                    pe.wait_ge(rows_ready, 1)
                    for t, (s, n) in enumerate(TOK):
                        mm = pe.transpose(mb[1][0:n, NH * t:NH * t + NH], row[0][:, s:s + n], ident[0:NH, 0:NH])
                    mm.then_inc(at_mm, 1)
                    for h in range(NH):
                        if h == 3:
                            pe.wait_ge(acol_ready, 1)
                        pe.matmul(spread_bank(h)[:, 0:T], sel[0:NH, h, :], row[5], start=True, stop=True).then_inc(mb_mm, 1)
                else:
                    pe.wait_ge(em_ready, 2)
                    for h in range(NH):
                        pe.wait_ge(dm_ready, 3 * (h + 1))
                        pe.matmul(spread_bank(h)[:, 0:T + TS], sel[0:NH, h, :], r_em, start=True, stop=True).then_inc(ei_mm, 1)

            def head_work(h, step, G0):
                b = h % 2
                if step == 0:
                    pe.wait_ge(evac, G0 + 6 * h + 4)
                    if h >= 1:
                        pe.wait_ge(hn_used, 2 * h)
                    else:
                        pe.wait_ge(ei_ready, 2 * NH)
                    for t, (s, n) in enumerate(TOK):
                        for j, src in enumerate((kT[:, b], vT[:, b, 0], vT[:, b, 1])):
                            mm = pe.transpose(mb[t][0:n, j * P:(j + 1) * P], src[:, s:s + n], ident)
                        mm.then_inc(tok_mm, 1)
                    if h >= 1:
                        pe.wait_ge(outs_ready, h)
                    pe.matmul(mb[3][:, 0:256], kT[:, b, 0:128], qT[:, b, 0:256], start=True, stop=True)
                    pe.matmul(mb[3][:, 256:384], kT[:, b, 128:256], qT[:, b, 128:256], start=True, stop=True)
                    pe.matmul(mb[3][0:TS, 384:416], kT[:, b, 256:288], qT[:, b, 256:288], start=True, stop=True).then_inc(qk_mm, 1)
                if step == 1:
                    pe.wait_ge(tok_ready, 6 * (h + 1))
                    pe.wait_ge(wts_ready, 4 * (h + 1))
                    for e in range(3):
                        if e < 2:
                            src = [vtok[0:n, t, e * P:(e + 1) * P] for t, (_, n) in enumerate(TOK)]
                            st = c0[:, h, e * P:(e + 1) * P]
                        else:
                            src, st = [ones[0:n, :] for _, n in TOK], n0rep
                        kw = dict(skip_group_check=True)
                        pe.matmul(mb[e][:, 0:256], src[0], wts[:, 0:256], start=True, stop=False, **kw)
                        pe.matmul(mb[e][:, 128:256], src[1], wts[:, 256:384], start=False, stop=False, **kw)
                        pe.matmul(mb[e][:, 256:288], src[2], wts[0:TS, 384:416], start=False, stop=False, **kw)
                        mm = pe.matmul(mb[e][:, 256:288], st, qi, start=False, stop=True, **kw)
                        if e == 1:
                            mm.then_inc(num_mm, 1)
                    mm.then_inc(den_mm, 1)
                    for t in range(2):
                        mm = pe.matmul(mb[3][:, 0:DV + 1], ktok[:, t, :], vtok[:, t, :], start=(t == 0), stop=(t == 1))
                    mm.then_inc(stp_mm, 1)
                if step == 2:
                    pe.wait_ge(den_used, h + 1)
                    pe.wait_ge(sqn_ready, h + 1)
                    pe.matmul(mb[2][:, 0:T], ones, sqn[:, 0, :], start=True, stop=False)
                    pe.matmul(mb[2][:, 0:T], ones, sqn[:, 1, :], start=False, stop=True).then_inc(ssq_mm, 1)
                    pe.wait_ge(outp_ready, h + 1)
                    pe.matmul(mb[3][:, 0:DV + 1], ktok[0:TS, 2, :], vtok[0:TS, 2, :], start=True, stop=True).then_inc(sts_mm, 1)

            def mlstm_in(i):
                c0_, G0 = 2 * FIRST_UNIT[i], FIRST_GROUP[i]
                for n in range(HEAD_START[-1] + 5):
                    if n == 0:
                        first_two(i, c0_, G0)
                    elif 1 < n < 6 * NH:
                        in_piece(i, 0, c0_ + n, n, G0 + n)
                    if n == 1:
                        gates()
                    if n == 5:
                        row_spread(0)
                    if n == 6:
                        row_spread(1)
                    if n in HEAD_STEPS:
                        head_work(*HEAD_STEPS[n], G0)

            def mlstm_out(i):
                for m in range(4):
                    for h in range(NH - 1):
                        if m == 0:
                            pe.wait_ge(mlo_ready, h + 1)
                        mix_partial(i, m, [2 * h, 2 * h + 1])
                pe.wait_ge(mlo_ready, NH)
                for m in range(4):
                    mix_partial(i, m, [KD - 2, KD - 1])
                mix_rest(i)

            def tick(t, G0):
                if t < len(ITEMS):
                    kind, c, half = ITEMS[t]
                    lo_, hi_ = half * HD, half * HD + HD
                    if t >= 2:
                        pe.wait_ge(neg_ready, t - 1)
                    bank = mb[t % 2]
                    if kind == "p":
                        pe.wait_ge(rope_done, ROPE.index(f"q{c}") + 1)
                        kk = s_k[lo_:hi_, c // 4, :]
                        pe.matmul(bank[:, 0:128], s_q[lo_:hi_, c, 0:128], kk[:, 0:128], start=True, stop=True)
                        mm = pe.matmul(bank[:, 128:384], s_q[lo_:hi_, c, 128:256], kk[:, 0:256], start=True, stop=True)
                    else:
                        pe.wait_ge(ks_ready, ROPE.index(f"q{4 * c + 3}") + 1)
                        mm = pe.matmul(bank[:, 0:CACHE + TS], s_qs[lo_:hi_, c, :], ks[lo_:hi_, c, :],
                                       start=True, stop=True)
                    mm.then_inc(s_mm, 1)
                if 2 <= t < len(ITEMS) + 2:
                    n = t - 2
                    pe.wait_ge(p_ready, n + 1)
                    if n >= 1:
                        pe.wait_ge(pt_ready, n)
                    pr = prob[:, n % 4, :]
                    if ITEMS[n][0] == "p":
                        for j in range(3):
                            mm = pe.transpose(mb[2][:, j * P:(j + 1) * P], pr[:, j * P:(j + 1) * P], ident)
                    else:
                        pe.transpose(mb[2][:, 0:P], pr[:, 0:P], ident)
                        mm = pe.transpose(mb[2][0:TS, P:2 * P], pr[:, P:P + TS], ident)
                    mm.then_inc(pt_mm, 1)
                if t >= 4 and t % 2 == 0:
                    for n in (t - 4, t - 3):
                        kind, c, half = ITEMS[n]
                        pe.wait_ge(pt_ready, n + 1)
                        if n % 2 == 0:
                            pe.wait_ge(evac, G0 + group_of("turn", f"v{c // 4 if kind == 'p' else c}") + 1)
                            if n >= 2:
                                pe.wait_ge(olo_ready, n // 2)
                        lo_, hi_ = half * HD, half * HD + HD
                        pt = probT[:, n % 4, :]
                        kw = dict(skip_group_check=True)
                        if kind == "p":
                            kv = 2 * (c // 4) + half
                            v0, v1 = (s_v[:, j, kv * HD:(kv + 1) * HD] for j in range(2))
                            pe.matmul(mb[3][lo_:hi_, 0:128], v0, pt[:, 0:128], start=True, stop=False, **kw)
                            pe.matmul(mb[3][lo_:hi_, 128:256], v0, pt[:, 128:256], start=False, stop=False, **kw)
                            mm = pe.matmul(mb[3][lo_:hi_, 128:256], v1, pt[:, 256:384], start=False, stop=True, **kw)
                        else:
                            kv = 2 * c + half
                            pe.matmul(mb[3][lo_:hi_, 0:128], vc[:, kv * HD:(kv + 1) * HD], pt[:, 0:128], start=True, stop=False, **kw)
                            mm = pe.matmul(mb[3][lo_:hi_, 0:128], s_v[0:TS, 2, kv * HD:(kv + 1) * HD], pt[0:TS, 128:256],
                                           start=False, stop=True, **kw)
                        mm.then_inc(pv_mm, 1)

            def swa_in(i):
                c0_, G0 = 2 * FIRST_UNIT[i], FIRST_GROUP[i]
                pe.wait_ge(mix_in, MIX_SWA)
                for g, (what, p) in enumerate(SWA_GROUPS):
                    n = SWA_PIECES.index(p)
                    bank = group_bank(g)
                    if what == "piece":
                        if n == 0:
                            first_two(i, c0_, G0)
                        if n > 1:
                            in_piece(i, 0, c0_ + n, g, G0 + g)
                    elif what == "swap":
                        pe.wait_ge(evac, max(G0 + group_of("piece", p) + 1, G0 + g - 3))
                        pe.matmul(bank, perm, s_raw[:, ROPE.index(p) % 2, :], start=True, stop=True).then_inc(turn_mm, 1)
                    else:
                        pe.wait_ge(evac, max(G0 + group_of("piece", p) + 1, G0 + g - 3))
                        for t, (at, m) in enumerate(TOK):
                            mm = pe.transpose(acc[(g + BANK) % 4][0:m, t * P:(t + 1) * P], s_vT[:, at:at + m], ident)
                        mm.then_inc(turn_mm, 1)
                    if (what, p) in SWA_TICKS:
                        tick(SWA_TICKS[what, p], G0)

            def swa_out(i):
                G0 = FIRST_GROUP[i - 1]
                for n, t in enumerate(TAIL_TICKS):
                    tick(t, G0)
                    if 1 <= n <= 8:
                        pe.wait_ge(olo_ready, 5)
                        mix_partial(i, (n - 1) // 2, [0, 1] if n % 2 else [2, 3])
                pe.wait_ge(olo_ready, len(ITEMS) // 2)
                for m in range(4):
                    mix_partial(i, m, [4, 5, 6, 7])
                mix_rest(i)

            pe.wait_ge(g_zero, 1)
            for _ in range(WARM_UP):
                pe.matmul(group_bank(0), ghi[:, 0, :], ghi[:, 0:3, 0:T // 3], start=True, stop=True)
            ffn_in(0)
            ffn_out(1)
            pe.wait_ge(par_in, PAR_IN)
            mlstm_in(2)
            mlstm_out(3)
            ffn_in(4)
            ffn_out(5)
            ffn_in(6)
            ffn_out(7)
            swa_in(8)
            swa_out(9)
            ffn_in(10)
            ffn_out(11)
            ss_sum()

        @block.scalar
        def _(act):
            n_s = [0]

            def hi_of_x(m, norm):
                act.activation(xhi[:, m, :], x[:, m, :], ACT.Copy, scale=norms[:, norm, m:m + 1]).then_inc(xhi_done, 1)

            def rms(done):
                act.activation(warm[:, :], epst[:, :], ACT.Sqrt)
                act.wait_ge(ss_mm, done)
                act.activation(std[:, :], mb[3][:, 0:T], ACT.Sqrt, bias=epst[:, :], scale=1.0 / D).then_inc(std_done, 1)

            def hi_ahead(it, c):
                L = ahead(c)
                if L:
                    split_hi(act, it, c + 4, L)

            def ffn_in(i, norm):
                c0_, G0 = 2 * FIRST_UNIT[i], FIRST_GROUP[i]
                f0 = KF * FFN_NO[i]
                split_hi(act, 0, c0_ + 4, 8)
                rms(norm + 1)

                def unit(it, u, look, begun=False):
                    c, G = c0_ + 2 * u, G0 + 2 * u
                    if look and not begun:
                        split_hi(act, it, c + 4, look)
                    act.wait_ge(evac, 4 * it + G + 1)
                    act.activation(f_silu[:, u % 2, :], f_gate[:, u % 2, :], ACT.Silu).then_inc(silu_done, 1)
                    if look:
                        split_hi(act, it, c + 5, look)
                    act.wait_ge(prod_done, 2 * it + f0 + u + 1)
                    act.activation(ahi[:, bass.ds(2 * it + u, 1), :], f_prod[:, u % 2:u % 2 + 1, :], ACT.Copy)\
                        .then_inc(ahi_done, 1)

                unit(0, 0, 8, begun=True)
                unit(0, 1, 8)
                with act.Fori(1, KF // 2 - 1) as it:
                    unit(it, 0, 8)
                    unit(it, 1, 8)
                for u in range(2):
                    unit(KF // 2 - 1, u, 11)

            def ffn_out(i, norm):
                c0_, G0 = 2 * FIRST_UNIT[i], FIRST_GROUP[i]

                def unit(it, u, look):
                    c = c0_ + 2 * u
                    if look:
                        split_hi(act, it, c + 4, look)
                    act.wait_ge(evac, 2 * it + G0 + u + 1)
                    m = bass.ds(2 * it + u, 1)
                    act.activation(xhi[:, m, :] if norm < N_FINAL else xg[:, m, :], x[:, m, :], ACT.Copy,
                                   scale=norms[:, norm, m]).then_inc(xhi_done, 1)
                    if look:
                        split_hi(act, it, c + 5, look)

                with act.Fori(0, 3) as it:
                    for u in range(2):
                        unit(it, u, 11)
                for u in range(2):
                    unit(3, u, ahead(c0_ + 12 + 2 * u))

            def mix_out(i, norm):
                c0_, G0 = 2 * FIRST_UNIT[i], FIRST_GROUP[i]
                for m in range(KD):
                    hi_ahead(0, c0_ + m)
                    act.wait_ge(evac, G0 + m + 1)
                    hi_of_x(m, norm)

            def gate_logs():
                act.wait_ge(fg_ready, 1)
                n = n_s[0]
                act.activation(row[2], row[1], ACT.Abs).then_inc(chain_a, 1)
                act.wait_ge(chain_a, n + 1)
                act.activation(row[2], row[2], ACT.Exp, scale=-1.0).then_inc(chain_a, 1)
                act.wait_ge(chain_a, n + 2)
                act.activation(row[2], row[2], ACT.Ln, bias=cst[0:NH, P:P + 1]).then_inc(l_ready, 1)
                n_s[0] += 2

            def gate_exps():
                act.wait_ge(rows_ready, 1)
                act.activation(r_em[:, 0:T], row[1], ACT.Exp, scale=-2.0).then_inc(em_ready, 1)
                act.activation(r_em[:, T:T + TS], row[5][:, TP:T], ACT.Exp, scale=-1.0, bias=m0[:, :]).then_inc(em_ready, 1)

            def decays():
                for h in range(NH):
                    act.wait_ge(dm_ready, 3 * h + 3)
                    for t, (lo_, hi_, n) in enumerate(((0, 256, P), (256, 384, P), (384, 416, TS))):
                        v = dec[0:n, h, lo_:hi_]
                        act.activation(v, v, ACT.Exp, scale=-1.0, bias=acol[0:n, NH * t + h:NH * t + h + 1]).then_inc(d_ready, 1)

            def head_work(h, step, G0):
                b = h % 2
                if step == 0:
                    act.wait_ge(d_ready, 3 * h + 3)
                    for t, (_, n) in enumerate(TOK):
                        act.wait_ge(tok_mm, 3 * h + t + 1)
                        act.activation(vtok[0:n, t, 0:DV], mb[t][0:n, P:3 * P], ACT.Copy).then_inc(tok_ready, 1)
                        col = (255, 383, 415)[t]
                        act.activation(ktok[0:n, t, :], mb[t][0:n, 0:P], ACT.Copy,
                                       scale=dec[0:n, h, col:col + 1]).then_inc(tok_ready, 1)
                if step == 1:
                    act.wait_ge(num_mm, h + 1)
                    act.activation(sqn[:, :, :], num[:, :, 0:T], ACT.Square).then_inc(sqn_ready, 1)
                    act.wait_ge(den_mm, h + 1)
                    act.activation(den[:, :], mb[2][:, 0:T], ACT.Square).then_inc(den_used, 1)
                    act.wait_ge(stp_mm, h + 1)
                    if h >= 1:
                        act.wait_ge(st_dma, 32 * h)
                    act.activation(outp[:, :], mb[3][:, 0:DV + 1], ACT.Copy).then_inc(outp_ready, 1)
                if step == 2:
                    act.wait_ge(evac, G0 + 6 * h + 6)
                    act.activation(oT[:, b, :, :], oT[:, b, :, :], ACT.Tanh, scale=0.5).then_inc(th_ready, 1)
                    act.wait_ge(y_ready, h + 1)
                    act.activation(rinv[:, :], den2[:, :], ACT.Sqrt, scale=1.0 / DV).then_inc(sd_ready, 1)
                if step == 4:
                    act.wait_ge(m_ready, h + 1)
                    act.activation(ahi[:, 2 * h:2 * h + 2, :], hn[:, :, :], ACT.Copy).then_inc(mhi_ready, 1)

            def mlstm_in(i, norm):
                c0_, G0 = 2 * FIRST_UNIT[i], FIRST_GROUP[i]
                rms(norm + 1)
                for n in range(HEAD_START[-1] + 5):
                    if n < 6 * NH:
                        hi_ahead(0, c0_ + n)
                    if n == 1:
                        gate_logs()
                    if n == 3:
                        gate_exps()
                    if n == 5:
                        decays()
                    if n in HEAD_STEPS:
                        head_work(*HEAD_STEPS[n], G0)

            def tick(t):
                if t >= 5 and t % 2 == 1:
                    kind, c, _ = ITEMS[t - 5]
                    act.wait_ge(pv_mm, t - 3)
                    if kind == "p":
                        act.activation(ahi[:, c, 0:TP], mb[3][:, 0:TP], ACT.Copy).then_inc(ohi_ready, 1)
                    else:
                        act.activation(ahi[:, 4 * c:4 * c + 4, TP:T], mb[3][:, 0:P].rearrange("p (g t) -> p g t", g=4),
                                       ACT.Copy).then_inc(ohi_ready, 1)
                if 2 <= t < len(ITEMS) + 2:
                    n = t - 2
                    act.wait_ge(pt_mm, n + 1)
                    if n >= 4:
                        act.wait_ge(pv_mm, n - 3)
                    if ITEMS[n][0] == "p":
                        act.activation(probT[:, n % 4, :], mb[2][:, 0:3 * P], ACT.Copy).then_inc(pt_ready, 1)
                    else:
                        act.activation(probT[:, n % 4, 0:P], mb[2][:, 0:P], ACT.Copy)
                        act.activation(probT[0:TS, n % 4, P:2 * P], mb[2][0:TS, P:2 * P], ACT.Copy).then_inc(pt_ready, 1)
                if t < len(ITEMS):
                    kind, c, half = ITEMS[t]
                    b = t % 2
                    act.wait_ge(neg_ready, t + 1)
                    if kind == "p":
                        head = (2 * (c // 4) + half) * 4 + c % 4
                        parts, sink = ((0, P), (P, 3 * P)), snk[:, head:head + 1]
                    else:
                        parts, sink = ((0, CACHE + TS),), snks[:, 2 * c + half:2 * c + half + 1]
                    for j, (lo_, hi_) in enumerate(parts):
                        v = prob[:, t % 4, lo_:hi_]
                        act.activation(v, v, ACT.Exp, bias=s_neg[:, b, j:j + 1], accum_out=s_sum[:, b, j:j + 1])
                    act.activation(s_sk[:, b, 0:len(parts)], s_neg[:, b, 0:len(parts)], ACT.Exp, bias=sink).then_inc(exp_ready, 1)

            def swa_in(i, norm):
                c0_ = 2 * FIRST_UNIT[i]
                act.wait_ge(mix_in, MIX_SWA)
                rms(norm + 1)
                for what, p in SWA_GROUPS:
                    if what == "piece":
                        hi_ahead(0, c0_ + SWA_PIECES.index(p))
                    if (what, p) in SWA_TICKS:
                        tick(SWA_TICKS[what, p])
                for t in TAIL_TICKS:
                    tick(t)

            act.dma_start(norms[:, :, :], a["norms"]).then_inc(norms_in, 16)
            act.dma_start(cst[:, :], a["cst"][:, 0:3 * P]).then_inc(cst_in, 16)
            split_hi(act, 0, 0, 8)
            act.wait_ge(norms_in, 16)
            for m in range(KD):
                if m == 4:
                    split_hi(act, 0, 1, 8)
                act.wait_ge(x_in[m // 2], 16)
                hi_of_x(m, N_F1)
                if m % 2 == 1:
                    act.activation(x_squares[:, m // 2, :], x[:, m, :], ACT.Square).then_inc(x_sq, 1)
            split_hi(act, 0, 2, 8)
            split_hi(act, 0, 3, 8)
            act.dma_start(graw[:, :, :], a["w_gates"]).then_inc(par_in, 16)
            act.dma_start(bg[:, :], a["b_gates"]).then_inc(par_in, 16)
            act.dma_start(m0[:, :], a["m0"]).then_inc(par_in, 16)
            act.dma_start(c0[:, :, :], a["c0"]).then_inc(par_in, 16)
            act.dma_start(tri[:, :], a["cst"][:, C_TRI:C_TRI + 2 * P]).then_inc(par_in, 16)
            act.dma_start(sel[:, :, :], a["cst"][:, C_SEL:C_SEL + NH * P]).then_inc(par_in, 16)
            act.wait_ge(const_done, 1)
            ffn_in(0, 0)
            act.wait_ge(g_zero, 2)
            act.wait_ge(par_in, PAR_IN)
            for j in range(2):
                act.activation(ghi[:, :, 32 * j:32 * j + NH], graw[:, :, NH * j:NH * j + NH], ACT.Copy).then_inc(g_hi, 1)
            ffn_out(1, 1)
            mlstm_in(2, 1)
            mix_out(3, 2)
            ffn_in(4, 2)
            ffn_out(5, 3)
            ffn_in(6, 3)
            ffn_out(7, 4)
            swa_in(8, 4)
            mix_out(9, 5)
            ffn_in(10, 5)
            ffn_out(11, 6)
            rms(7)
            for m in range(0, Y_POOL, 2):
                e = min(m + 2, Y_POOL)
                act.wait_ge(y_out, e)
                act.dma_start(a["yT"][:, m:e, :], x[:, m:e, :]).then_inc(y_dma, 16)
            act.wait_ge(y_out_pool, KD - Y_POOL)
            act.dma_start(a["yT"][:, Y_POOL:KD, :], x[:, Y_POOL:KD, :]).then_inc(y_dma, 16)
            act.wait_ge(y_dma, 16 * ((Y_POOL + 1) // 2 + 1))

        @block.vector
        def _(dve):
            n_d = [0]

            def own(ins):
                n_d[0] += 1
                ins.then_inc(chain_d, 1)
                dve.wait_ge(chain_d, n_d[0])

            def lo_of_x(m, norm, n):
                dve.wait_ge(xhi_done, n)
                dve.scalar_tensor_tensor(xlo[:, m, :], x[:, m, :], norms[:, norm, m:m + 1], xhi[:, m, :].bitcast(F32),
                                         ALU.mult, ALU.subtract).then_inc(xlo_done, 1)

            def rms(done):
                dve.wait_ge(std_done, done)
                dve.reciprocal(rstd[:, :], std[:, :]).then_inc(r_done, 1)
                dve.wait_ge(r_done, done)

            def lo_ahead(it, c):
                L = ahead(c)
                if L:
                    split_lo(dve, it, c + 4, L)

            def ffn_in(i, norm):
                c0_, G0 = 2 * FIRST_UNIT[i], FIRST_GROUP[i]
                f0 = KF * FFN_NO[i]
                split_lo(dve, 0, c0_ + 4, 8)
                rms(norm + 1)

                def unit(it, u, look, begun=False):
                    c, G = c0_ + 2 * u, G0 + 2 * u
                    b = u % 2
                    dve.wait_ge(piece_done, 4 * it + c + 1)
                    dve.tensor_tensor(f_gate[:, b, :], group_bank(2 * u), rstd[:, :], ALU.mult).then_inc(evac, 1)
                    if look and not begun:
                        split_lo(dve, it, c + 4, look)
                    dve.wait_ge(piece_done, 4 * it + c + 2)
                    dve.tensor_tensor(f_up[:, b, :], group_bank(2 * u + 1), rstd[:, :], ALU.mult).then_inc(evac, 1)
                    dve.wait_ge(silu_done, 2 * it + f0 + u + 1)
                    dve.wait_ge(evac, 4 * it + G + 2)
                    dve.tensor_tensor(f_prod[:, b, :], f_silu[:, b, :], f_up[:, b, :], ALU.mult).then_inc(prod_done, 1)
                    if look:
                        split_lo(dve, it, c + 5, look)
                    dve.wait_ge(ahi_done, 2 * it + f0 + u + 1)
                    dve.tensor_tensor(alo[:, bass.ds(2 * it + u, 1), :], f_prod[:, b:b + 1, :],
                                      ahi[:, bass.ds(2 * it + u, 1), :].bitcast(F32), ALU.subtract).then_inc(alo_done, 1)

                unit(0, 0, 8, begun=True)
                unit(0, 1, 8)
                with dve.Fori(1, KF // 2 - 1) as it:
                    unit(it, 0, 8)
                    unit(it, 1, 8)
                for u in range(2):
                    unit(KF // 2 - 1, u, 11)

            def ffn_out(i, norm):
                c0_, G0 = 2 * FIRST_UNIT[i], FIRST_GROUP[i]

                def unit(it, u, look):
                    c = c0_ + 2 * u
                    m = bass.ds(2 * it + u, 1)
                    if look:
                        split_lo(dve, it, c + 4, look)
                    dve.wait_ge(piece_done, 4 * it + c + 2)
                    dve.scalar_tensor_tensor(x[:, m, :], acc[u][:, 0:T].rearrange("p (a t) -> p a t", a=1), 0.5, x[:, m, :],
                                             ALU.mult, ALU.add).then_inc(evac, 1)
                    if norm < N_FINAL:
                        dve.wait_ge(xhi_done, 2 * it + KD * norm + u + 1)
                        dve.scalar_tensor_tensor(xlo[:, m, :], x[:, m, :], norms[:, norm, m], xhi[:, m, :].bitcast(F32),
                                                 ALU.mult, ALU.subtract).then_inc(xlo_done, 1)
                    if look:
                        split_lo(dve, it, c + 5, look)

                with dve.Fori(0, 3) as it:
                    for u in range(2):
                        unit(it, u, 11)
                for u in range(2):
                    unit(3, u, ahead(c0_ + 12 + 2 * u))

            def mix_out(i, norm):
                c0_, G0 = 2 * FIRST_UNIT[i], FIRST_GROUP[i]
                for m in range(KD):
                    dve.wait_ge(piece_done, c0_ + m + 1)
                    dve.tensor_tensor(x[:, m, :], group_bank(m), x[:, m, :], ALU.add).then_inc(evac, 1)
                    lo_of_x(m, norm, KD * norm + m + 1)
                    lo_ahead(0, c0_ + m)

            def gate_rows(part):
                if part == 0:
                    dve.wait_ge(g_mm, 1)
                    dve.tensor_tensor(row[0], mb[0][0:NH, 0:T], rstd[0:NH, :], ALU.mult)
                    own(dve.tensor_tensor(row[1], mb[0][32:32 + NH, 0:T], rstd[32:32 + NH, :], ALU.mult))
                    dve.tensor_scalar(row[1], row[1], bg[:, 1:2], None, ALU.add).then_inc(fg_ready, 1)
                    own(dve.tensor_scalar(row[0], row[0], bg[:, 0:1], None, ALU.add))
                    return
                dve.wait_ge(l_ready, 1)
                dve.wait_ge(fg_ready, 1)
                own(dve.scalar_tensor_tensor(row[3], row[1], 0.0, row[2], ALU.min, ALU.subtract))
                dve.tensor_tensor_scan(row[4][:, 0:TP], one_row, row[3][:, 0:TP], 0.0, ALU.mult, ALU.add)
                own(dve.tensor_tensor_scan(row[4][:, TP:T], one_row[:, 0:TS], row[3][:, TP:T], 0.0, ALU.mult, ALU.add))
                own(dve.tensor_tensor(row[0], row[0], row[4], ALU.subtract))
                dve.tensor_tensor_scan(row[5][:, 0:TP], one_row, row[0][:, 0:TP], 0.0, ALU.mult, ALU.max)
                own(dve.tensor_tensor_scan(row[5][:, TP:T], one_row[:, 0:TS], row[0][:, TP:T], m0[:, 0:1], ALU.mult, ALU.max))
                own(dve.tensor_tensor(row[1], row[4], row[5], ALU.add))
                dve.tensor_copy(mout[:, 0:1], row[1][:, TP - 1:TP])
                dve.tensor_copy(mout[:, 1:2], row[1][:, T - 1:T]).then_inc(rows_ready, 1)

            def decay_rows():
                dve.wait_ge(at_mm, 1)
                dve.tensor_copy(acol[:, 0:2 * NH], mb[1][:, 0:2 * NH])
                dve.tensor_copy(acol[0:TS, 2 * NH:3 * NH], mb[1][0:TS, 2 * NH:3 * NH]).then_inc(acol_ready, 1)
                for h in range(NH):
                    dve.wait_ge(mb_mm, h + 1)
                    bank = spread_bank(h)
                    dve.tensor_tensor(dec[:, h, 0:256], bank[:, 0:256], tri, ALU.add).then_inc(dm_ready, 1)
                    dve.tensor_tensor(dec[:, h, 256:384], bank[:, 128:256], tri[:, 0:P], ALU.add).then_inc(dm_ready, 1)
                    dve.tensor_tensor(dec[0:TS, h, 384:416], bank[0:TS, TP:T], tri[0:TS, 0:TS], ALU.add).then_inc(dm_ready, 1)

            def em_rows():
                for h in range(NH):
                    dve.wait_ge(ei_mm, h + 1)
                    bank = spread_bank(h)
                    dve.tensor_copy(emb[:, h, :], bank[:, 0:T]).then_inc(ei_ready, 1)
                    dve.tensor_copy(intb[:, h, :], bank[:, T:T + TS]).then_inc(ei_ready, 1)

            def head_work(h, step, G0):
                b = h % 2
                if step == 0:
                    dve.wait_ge(qk_mm, h + 1)
                    dve.wait_ge(d_ready, 3 * h + 3)
                    dve.wait_ge(ei_ready, 2 * NH)
                    dve.tensor_tensor(wts[:, 0:384], mb[3][:, 0:384], dec[:, h, 0:384], ALU.mult).then_inc(wts_ready, 1)
                    dve.tensor_tensor(wts[0:TS, 384:416], mb[3][0:TS, 384:416], dec[0:TS, h, 384:416], ALU.mult).then_inc(wts_ready, 1)
                    dve.tensor_tensor(qi, qT[:, b, TP:T], intb[:, h, :], ALU.mult).then_inc(wts_ready, 1)
                    dve.tensor_scalar(n0rep, ones, c0[:, h, DV:DV + 1], None, ALU.mult).then_inc(wts_ready, 1)
                if step == 1:
                    dve.wait_ge(den_used, h + 1)
                    own(dve.tensor_tensor(den[:, :], den[:, :], emb[:, h, :], ALU.max))
                if step == 2:
                    dve.wait_ge(ssq_mm, h + 1)
                    dve.scalar_tensor_tensor(den2[:, :], den[:, :], DV * EPS, mb[2][:, 0:T], ALU.mult, ALU.add).then_inc(y_ready, 1)
                    dve.wait_ge(sts_mm, h + 1)
                    if h >= 1:
                        dve.wait_ge(st_dma, 32 * h)
                    dve.scalar_tensor_tensor(outs[:, :], c0[:, h, :], intb[:, h, TS - 1:TS], mb[3][:, 0:DV + 1],
                                             ALU.mult, ALU.add).then_inc(outs_ready, 1)
                if step == 3:
                    dve.wait_ge(sd_ready, h + 1)
                    own(dve.reciprocal(rinv[:, :], rinv[:, :]))
                    for e in range(2):
                        c = 2 * h + e
                        dve.scalar_tensor_tensor(hn[:, e, :], num[:, e, 0:T], norms[:, N_HEAD, c:c + 1], rinv[:, :],
                                                 ALU.mult, ALU.mult).then_inc(hn_used, 1)
                    dve.wait_ge(th_ready, h + 1)
                    dve.wait_ge(hn_used, 2 * h + 2)
                    dve.scalar_tensor_tensor(hn[:, :, :], oT[:, b, :, :], 1.0, hn[:, :, :], ALU.add, ALU.mult).then_inc(m_ready, 1)
                if step == 4:
                    dve.wait_ge(mhi_ready, h + 1)
                    dve.tensor_tensor(alo[:, 2 * h:2 * h + 2, :], hn[:, :, :], ahi[:, 2 * h:2 * h + 2, :].bitcast(F32),
                                      ALU.subtract).then_inc(mlo_ready, 1)

            def mlstm_in(i, norm):
                c0_, G0 = 2 * FIRST_UNIT[i], FIRST_GROUP[i]
                rms(norm + 1)
                own(dve.tensor_scalar(norms[:, N_HEAD, :], norms[:, N_HEAD, :], 0.5, None, ALU.mult))
                dve.memset(vtok[:, :, DV:DV + 1], 1.0)
                for n in range(HEAD_START[-1] + 5):
                    if n < 6 * NH:
                        b = (n // 6) % 2
                        dve.wait_ge(piece_done, c0_ + n + 1)
                        ps = group_bank(n)
                        dst = (kT[:, b, :], qT[:, b, :], vT[:, b, 0, :], vT[:, b, 1, :], oT[:, b, 0, :], oT[:, b, 1, :])[n % 6]
                        if n % 6 == 0:
                            dve.scalar_tensor_tensor(dst, ps, float(DK) ** -0.5, rstd[:, :], ALU.mult, ALU.mult).then_inc(evac, 1)
                        else:
                            dve.tensor_tensor(dst, ps, rstd[:, :], ALU.mult).then_inc(evac, 1)
                        lo_ahead(0, c0_ + n)
                    if n == 1:
                        gate_rows(0)
                    if n == 2:
                        gate_rows(1)
                    if n == 5:
                        decay_rows()
                    if n == 6:
                        em_rows()
                    if n in HEAD_STEPS:
                        head_work(*HEAD_STEPS[n], G0)

            def scores(t):
                if t < len(ITEMS):
                    kind, c, half = ITEMS[t]
                    b = t % 2
                    dve.wait_ge(s_mm, t + 1)
                    if t >= 4:
                        dve.wait_ge(pt_mm, t - 3)
                    if kind == "p":
                        head = (2 * (c // 4) + half) * 4 + c % 4
                        parts, sink = ((0, P), (P, 3 * P)), snk[:, head:head + 1]
                        offs = (0, P)
                    else:
                        parts, sink = ((0, CACHE + TS),), snks[:, 2 * c + half:2 * c + half + 1]
                        offs = (3 * P,)
                    for j, ((lo_, hi_), o) in enumerate(zip(parts, offs)):
                        ins = dve.tensor_tensor_reduce(prob[:, t % 4, lo_:hi_], mb[b][:, lo_:hi_], mask[:, o:o + hi_ - lo_],
                                                       float(HD) ** -0.5, -3e38, ALU.add, ALU.max, s_mx[:, b, j:j + 1])
                    own(ins)
                    dve.tensor_scalar(s_neg[:, b, 0:len(parts)], s_mx[:, b, 0:len(parts)], sink, -1.0, ALU.max, ALU.mult)\
                        .then_inc(neg_ready, 1)

            def divide(t):
                if 1 <= t <= len(ITEMS):
                    n = t - 1
                    b = n % 2
                    parts = ((0, P), (P, 3 * P)) if ITEMS[n][0] == "p" else ((0, CACHE + TS),)
                    dve.wait_ge(exp_ready, n + 1)
                    J = len(parts)
                    own(dve.tensor_tensor(s_den[:, b, 0:J], s_sum[:, b, 0:J], s_sk[:, b, 0:J], ALU.add))
                    own(dve.reciprocal(s_inv[:, b, 0:J], s_den[:, b, 0:J]))
                    for j, (lo_, hi_) in enumerate(parts):
                        v = prob[:, n % 4, lo_:hi_]
                        ins = dve.tensor_scalar(v, v, s_inv[:, b, j:j + 1], None, ALU.mult)
                    ins.then_inc(p_ready, 1)

            def outputs_lo(t):
                if t >= 5 and t % 2 == 1:
                    kind, c, _ = ITEMS[t - 5]
                    dve.wait_ge(ohi_ready, (t - 3) // 2)
                    if kind == "p":
                        dve.tensor_tensor(alo[:, c, 0:TP], mb[3][:, 0:TP], ahi[:, c, 0:TP].bitcast(F32), ALU.subtract)\
                            .then_inc(olo_ready, 1)
                    else:
                        dve.tensor_tensor(alo[:, 4 * c:4 * c + 4, TP:T], mb[3][:, 0:P].rearrange("p (g t) -> p g t", g=4),
                                          ahi[:, 4 * c:4 * c + 4, TP:T].bitcast(F32), ALU.subtract).then_inc(olo_ready, 1)

            def tick(t):
                if t % 2 == 0:
                    divide(t)
                    scores(t)
                else:
                    scores(t)
                    divide(t)
                outputs_lo(t)

            def swa_in(i, norm):
                c0_ = 2 * FIRST_UNIT[i]
                rms(norm + 1)
                dve.wait_ge(mix_in, MIX_SWA)
                dve.tensor_tensor(rc, cos, rstd[:, :], ALU.mult).then_inc(rcs_ready, 1)
                own(dve.tensor_tensor(rs, sin, rstd[:, :], ALU.mult))
                for g, (what, p) in enumerate(SWA_GROUPS):
                    n = SWA_PIECES.index(p)
                    bank = group_bank(g)
                    xi = ROPE.index(p) if p in ROPE else None
                    if what == "piece":
                        dve.wait_ge(piece_done, c0_ + n + 1)
                        if xi is None:
                            dve.tensor_tensor(s_vT[:, :], bank, rstd[:, :], ALU.mult).then_inc(evac, 1)
                        else:
                            if xi >= 2:
                                dve.wait_ge(t1_ready, xi - 1)
                            dve.tensor_copy(s_raw[:, xi % 2, :], bank).then_inc(evac, 1)
                        lo_ahead(0, c0_ + n)
                    else:
                        dve.wait_ge(turn_mm, n + 1)
                        if what == "swap":
                            if xi >= 2:
                                dve.wait_ge(rope_done, xi - 1)
                            dve.tensor_tensor(s_t2[:, xi % 2, :], bank, rs, ALU.mult).then_inc(evac, 1)
                        else:
                            j = int(p[1]) * P
                            bank = acc[(g + BANK) % 4]
                            dve.tensor_copy(s_v[0:TS, 2, j:j + P], bank[0:TS, 2 * P:3 * P])
                            dve.tensor_copy(s_v[:, 0:2, j:j + P], bank[:, 0:2 * P].rearrange("p (t c) -> p t c", t=2))\
                                .then_inc(evac, 1)
                    if (what, p) in SWA_TICKS:
                        tick(SWA_TICKS[what, p])
                for t in TAIL_TICKS:
                    tick(t)

            dve.memset(epst[:, :], EPS).then_inc(const_done, 1)
            dve.memset(ghi[:, :, :].bitcast(F32), 0.0).then_inc(g_zero, 1)
            dve.memset(glo[:, :, :].bitcast(F32), 0.0).then_inc(g_zero, 1)
            split_lo(dve, 0, 0, 8)
            dve.wait_ge(norms_in, 16)
            for m in range(KD):
                if m == 4:
                    split_lo(dve, 0, 1, 8)
                dve.wait_ge(x_in[m // 2], 16)
                lo_of_x(m, N_F1, m + 1)
            split_lo(dve, 0, 2, 8)
            split_lo(dve, 0, 3, 8)
            ffn_in(0, 0)
            dve.wait_ge(par_in, PAR_IN)
            for j in range(2):
                dve.wait_ge(g_hi, j + 1)
                dve.tensor_tensor(glo[:, :, 32 * j:32 * j + NH], graw[:, :, NH * j:NH * j + NH],
                                  ghi[:, :, 32 * j:32 * j + NH].bitcast(F32), ALU.subtract).then_inc(g_done, 1)
            ffn_out(1, 1)
            mlstm_in(2, 1)
            mix_out(3, 2)
            ffn_in(4, 2)
            ffn_out(5, 3)
            ffn_in(6, 3)
            ffn_out(7, 4)
            swa_in(8, 4)
            mix_out(9, 5)
            ffn_in(10, 5)
            ffn_out(11, 6)
            rms(7)
            dve.wait_ge(xhi_done, KD * (N_FINAL + 1))
            for m in range(Y_POOL):
                dve.tensor_tensor(x[:, m, :], xg[:, m, :], rstd[:, :], ALU.mult).then_inc(y_out, 1)

        @block.gpsimd
        def _(pool):
            n_p = [0]

            def squares(norm, done):
                for m in range(KD):
                    done(m)
                    if m == 0:
                        if norm:
                            pool.wait_ge(ss_mm, norm)
                        pool.tensor_tensor(ssq[:, :], x[:, 0, :], x[:, 0, :], ALU.mult).then_inc(pool_sq, 1)
                        n_p[0] += 1
                        continue
                    if norm == 0 and m % 2 == 1:
                        pool.wait_ge(x_sq, m // 2 + 1)
                        pool.wait_ge(pool_sq, n_p[0])
                        add = pool.tensor_tensor(ssq[:, :], ssq[:, :], x_squares[:, m // 2, :], ALU.add)
                        add.then_inc(ss_done if m == KD - 1 else pool_sq, 1)
                        n_p[0] += m < KD - 1
                        continue
                    pool.tensor_tensor(sqr[:, m % 2, :], x[:, m, :], x[:, m, :], ALU.mult).then_inc(pool_sq, 1)
                    n_p[0] += 1
                    pool.wait_ge(pool_sq, n_p[0])
                    add = pool.tensor_tensor(ssq[:, :], ssq[:, :], sqr[:, m % 2, :], ALU.add)
                    if m == KD - 1:
                        add.then_inc(ss_done, 1)
                    else:
                        add.then_inc(pool_sq, 1)
                        n_p[0] += 1

            def after(i):
                return lambda m: pool.wait_ge(evac, FIRST_GROUP[i] + m + 1)

            squares(0, lambda m: pool.wait_ge(x_in[m // 2], 16))
            squares(1, after(1))
            for h in range(NH):
                pool.wait_ge(outp_ready, h + 1)
                pool.dma_start(a["cp"][:, h, :], outp[:, :]).then_inc(st_dma, 16)
                pool.wait_ge(outs_ready, h + 1)
                pool.dma_start(a["cs"][:, h, :], outs[:, :]).then_inc(st_dma, 16)
            pool.dma_start(a["mo"], mout[:, :]).then_inc(out_dma, 16)
            squares(2, after(3))
            pool.wait_ge(mlo_ready, NH)
            pool.wait_ge(ss_done, 3)
            pool.dma_start(vc[:, :], a["cache_v"]).then_inc(mix_in, 16)
            pool.dma_start(ks[:, :, 0:CACHE], a["cache_kT"]).then_inc(mix_in, 16)
            pool.dma_start(work[:, 8768:8768 + 2 * T + N_MASK], a["cst"][:, C_COS:N_CONST]).then_inc(mix_in, 16)
            pool.dma_start(snk[:, :], a["sinks"].to_broadcast([P, AH])).then_inc(mix_in, 16)
            for g in range(4):
                pool.dma_start(snks[TS * g:TS * g + TS, :], a["sinks_g"][g:g + 1, :].to_broadcast([TS, KV])).then_inc(mix_in, 16)
            squares(3, after(5))
            squares(4, after(7))
            G0 = FIRST_GROUP[8]
            pool.wait_ge(rcs_ready, 1)
            pool.wait_ge(mix_in, MIX_SWA)
            for xi, p in enumerate(ROPE):
                b, c = xi % 2, int(p[1])
                pool.wait_ge(evac, G0 + group_of("piece", p) + 1)
                pool.tensor_tensor(s_t1[:, b, :], s_raw[:, b, :], rc, ALU.mult).then_inc(t1_ready, 1)
                pool.wait_ge(evac, G0 + group_of("swap", p) + 1)
                pool.wait_ge(t1_ready, xi + 1)
                dst = s_k[:, c, :] if p[0] == "k" else s_q[:, c, :]
                pool.tensor_tensor(dst, s_t1[:, b, :], s_t2[:, b, :], ALU.add).then_inc(rope_done, 1)
                pool.wait_ge(rope_done, xi + 1)
                again = ks[:, c, CACHE:CACHE + TS] if p[0] == "k" else s_qs[:, c // 4, TS * (c % 4):TS * (c % 4) + TS]
                pool.tensor_copy(again, dst[:, TP:T]).then_inc(ks_ready, 1)
            pool.dma_start(a["kT_out"], s_k[:, :, TP - P:T]).then_inc(out_dma, 16)
            pool.wait_ge(evac, G0 + group_of("turn", "v1") + 1)
            pool.dma_start(a["v_out"][0:P, :], s_v[:, 1, :]).then_inc(out_dma, 16)
            pool.dma_start(a["v_out"][P:P + TS, :], s_v[0:TS, 2, :]).then_inc(out_dma, 16)
            squares(5, after(9))
            squares(6, after(11))
            pool.wait_ge(r_done, N_FINAL + 1)
            pool.wait_ge(xhi_done, KD * (N_FINAL + 1))
            for m in range(Y_POOL, KD):
                pool.tensor_tensor(x[:, m, :], xg[:, m, :], rstd[:, :], ALU.mult).then_inc(y_out_pool, 1)
            pool.wait_ge(st_dma, 32 * NH)
            pool.wait_ge(out_dma, 16 * OUT_DMAS)


def prod(v):
    return int(np.prod(v))


FFN_NO = {0: 0, 4: 1, 6: 2, 10: 3}
PAR_IN = 16 * 6
MIX_SWA = 16 * 8
OUT_DMAS = 4


def layouts(v):
    f = np.ascontiguousarray

    def pieces(wt, per):
        k, n = wt.shape[0] // P, wt.shape[1] // P
        return f(wt.reshape(k, P, n // per, per, P).transpose(2, 1, 3, 0, 4)).reshape(n // per, P, per * k * P)

    def chunks(g):
        return g.reshape(KD, P).T

    def ffn_in(wt):
        gate, up = wt[:, :FF].reshape(D, KF, 1, P), wt[:, FF:].reshape(D, KF, 1, P)
        return pieces(np.concatenate([gate, up], axis=2).reshape(D, 2 * FF), 2)

    a = {}
    x = np.concatenate([v["x_prompt"][0], v["x_sample"][0]])
    a["xT"] = f(x.T.reshape(KD, P, T).transpose(1, 0, 2))
    ffn = [(v[f"ffn_w_in{n}"][i], v[f"ffn_w_out{n}"][i]) for i in range(2) for n in (1, 2)]
    for i, (w_in, w_out) in zip((0, 4, 6, 10), ffn):
        a[f"w{i}"], a[f"w{i + 1}"] = ffn_in(w_in), pieces(w_out, 1)
    m = v["mlstm_w_in"][0]
    hk, hv = NH * DK, NH * DV
    part = [m[:, hk:2 * hk].reshape(D, NH, DK), m[:, 0:hk].reshape(D, NH, DK),
            m[:, 2 * hk:2 * hk + hv].reshape(D, NH, DV), m[:, 2 * hk + hv:2 * hk + 2 * hv].reshape(D, NH, DV)]
    a["w2"] = pieces(np.concatenate(part, axis=2).reshape(D, -1), 2)
    a["w_gates"] = f(m[:, 2 * hk + 2 * hv:].reshape(KD, P, 2 * NH).transpose(1, 0, 2))
    a["w3"] = pieces(v["mlstm_w_out"][0], 2)
    q = v["swa_w_qkv"][0]
    def pairs(t, axis):
        s = t.shape
        t = t.reshape(*s[:axis], 2, 2, 4, HD, *s[axis + 1:])
        return np.swapaxes(t, axis + 1, axis + 2).reshape(s)
    q = np.concatenate([pairs(q[:, :AH * HD], 1), q[:, AH * HD:]], axis=1).reshape(D, -1, P)
    first = {"q": 0, "k": KD, "v": KD + 2}
    a["w8"] = pieces(q[:, [first[p[0]] + int(p[1]) for p in SWA_PIECES]].reshape(D, -1), 2)
    a["w9"] = pieces(pairs(v["swa_w_out"][0], 0), 2)
    rows = []
    for i in range(2):
        rows += [v["ffn_norm1"][i], v["mix_norm"][i], v["ffn_norm2"][i]]
    rows += [v["final_norm"], v["mlstm_head_norm"][0]]
    a["norms"] = f(np.stack([chunks(r) for r in rows], axis=1))
    a["b_gates"] = f(v["mlstm_b_gates"][0].reshape(2, NH).T)
    a["m0"] = f(v["state_mlstm_m"][0, 0].reshape(NH, 1))
    c = np.concatenate([v["state_mlstm_C"][0, 0], v["state_mlstm_n"][0, 0][:, :, None]], axis=2)
    a["c0"] = f(c.transpose(1, 0, 2))
    a["cache_kT"] = f(v["cache_swa_k"][0, 0].reshape(CACHE, 2, 2 * HD).transpose(2, 1, 0))
    a["cache_v"] = f(v["cache_swa_v"][0, 0].reshape(CACHE, KV * HD))
    a["sinks"] = f(v["swa_sinks"])
    a["sinks_g"] = f(v["swa_sinks"].reshape(KV, 4).T)
    a["cst"] = constants()
    return a


OUTS = {"yT": (P, KD, T), "cp": (P, NH, DV + 1), "cs": (P, NH, DV + 1), "mo": (NH, 2),
        "kT_out": (P, 2, P + TS), "v_out": (P + TS, KV * HD)}


def kernel(**inputs):
    import concourse.bacc as bacc
    from concourse.bass_utils import run_bass_kernel_spmd

    nc = bacc.Bacc("TRN2", target_bir_lowering=False, num_devices=1)
    arrays = layouts({k: np.asarray(t) for k, t in inputs.items()})
    aps = {k: nc.dram_tensor(f"in_{k}", t.shape, F32, kind="ExternalInput").ap() for k, t in arrays.items()}
    aps.update({k: nc.dram_tensor(f"out_{k}", s, F32, kind="ExternalOutput").ap() for k, s in OUTS.items()})
    program(nc, aps)
    r = run_bass_kernel_spmd(nc, [{f"in_{k}": t for k, t in arrays.items()}], core_ids=[0]).results[0]
    o = {k: np.asarray(r[f"out_{k}"]) for k in OUTS}
    y = o["yT"].transpose(1, 0, 2).reshape(D, T).T
    kT = o["kT_out"].transpose(2, 1, 0).reshape(P + TS, KV, HD)
    v = o["v_out"].reshape(P + TS, KV, HD)
    c = {g: o[g].transpose(1, 0, 2) for g in ("cp", "cs")}
    f = np.ascontiguousarray
    return (f(y[None, :TP]), f(y[None, TP:]),
            f(c["cp"][None, None, :, :, :DV]), f(c["cp"][None, None, :, :, DV]), f(o["mo"][:, 0][None, None]),
            f(kT[None, None, :P]), f(v[None, None, :P]),
            f(c["cs"][None, None, :, :, :DV]), f(c["cs"][None, None, :, :, DV]), f(o["mo"][:, 1][None, None]),
            f(kT[None, None, P:]), f(v[None, None, P:]))
```

```python
from contextlib import ExitStack

import numpy as np

import concourse.bass as bass
from concourse import mybir

F32 = mybir.dt.float32
F32R = mybir.dt.float32r
ALU = mybir.AluOpType
ACT = mybir.ActivationFunctionType

P = 128
D = 1024
KD = D // P
TP, TS = 256, 32
T = TP + TS
FF = 11 * D // 4
KF = FF // P
NH, DK, DV = 4, 128, 256
AH, KV, HD = 16, 4, 64
CACHE = 128
PAST = 512
CHUNK, WIN = 64, 2
EPS = 1e-6
BIG, TINY = 1e30, 1e-30
Y_POOL = 6
WARM_UP = 16
RAW = 2 * (KF // 2)
TOK = [(0, 128), (128, 128), (256, 32)]

STAGES = [("ffn_in", 22, 44, 8), ("ffn_out", 8, 8, 11), ("mlstm_in", 12, 24, 8), ("mix_out", 4, 8, 8),
          ("ffn_in", 22, 44, 8), ("ffn_out", 8, 8, 11), ("ffn_in", 22, 44, 8), ("ffn_out", 8, 8, 11),
          ("swa_in", 6, 24, 8), ("mix_out", 4, 8, 8), ("ffn_in", 22, 44, 8), ("ffn_out", 8, 8, 11)]
FIRST_UNIT = [sum(s[1] for s in STAGES[:i]) for i in range(len(STAGES) + 1)]
FIRST_GROUP = [sum(s[2] for s in STAGES[:i]) for i in range(len(STAGES) + 1)]
UNITS = FIRST_UNIT[-1]
TILES = [s[3] for s in STAGES for _ in range(s[1])]
BANK = 2

SWA_PIECES = ["k0", "q0", "v0", "q1", "q2", "q3", "k1", "q4", "q5", "q6", "v1", "q7"]
ROPE = [p for p in SWA_PIECES if p[0] != "v"]
TURN_AFTER = {"q1": "v0", "v1": "v1"}
SWA_GROUPS = []
for _n, _p in enumerate(SWA_PIECES):
    SWA_GROUPS.append(("piece", _p))
    if _n and SWA_PIECES[_n - 1] in ROPE:
        SWA_GROUPS.append(("swap", SWA_PIECES[_n - 1]))
    if _p in TURN_AFTER:
        SWA_GROUPS.append(("turn", TURN_AFTER[_p]))
SWA_GROUPS.append(("swap", SWA_PIECES[-1]))
TURNS = [g for g in SWA_GROUPS if g[0] != "piece"]
ITEMS = [it for i in range(2) for it in
         [("p", c, half) for c in range(4 * i, 4 * i + 4) for half in range(2)] + [("s", i, half) for half in range(2)]]
FIRST_TICK = 4
SWA_TICKS = {}
for _n in range(FIRST_TICK, len(SWA_PIECES)):
    _g = SWA_GROUPS.index(("piece", SWA_PIECES[_n]))
    SWA_TICKS[SWA_GROUPS[_g]], SWA_TICKS[SWA_GROUPS[_g + 1]] = 2 * (_n - FIRST_TICK), 2 * (_n - FIRST_TICK) + 1
TAIL_TICKS = range(2 * (len(SWA_PIECES) - FIRST_TICK), len(ITEMS) + 4)
FILL = {}
for _n, _step in enumerate((m, ks) for m in range(4) for ks in ([0, 1], [2, 3])):
    FILL.setdefault(TAIL_TICKS[max(_n // 2, _n - 2)], []).append(_step)
HEAD_START = (7, 12, 17, 22)
HEAD_STEPS = {p + s: (h, s) for h, p in enumerate(HEAD_START) for s in range(5)}


def group_of(what, piece):
    return SWA_GROUPS.index((what, piece))


N_F1, N_FINAL, N_HEAD = 0, 6, 7

C_ID, C_ONE, C_PERM, C_TRI, C_SEL = 0, 128, 256, 384, 640
C_COS = C_SEL + NH * P
C_SIN = C_COS + T
C_MASK = C_SIN + T
N_MASK = 3 * P + CACHE + TS
N_CONST = C_MASK + N_MASK


def constants():
    c = np.zeros((P, N_CONST), np.float32)
    p = np.arange(P)
    c[:, C_ID:C_ID + P] = np.eye(P)
    c[:, C_ONE:C_ONE + P] = 1.0
    c[p, C_PERM + (p ^ 32)] = 1.0
    c[:, C_TRI:C_TRI + P] = np.where(p[:, None] > p[None, :], BIG, 0.0)
    for h in range(NH):
        c[h, C_SEL + h * P:C_SEL + (h + 1) * P] = 1.0
    pos = np.concatenate([np.arange(TP), PAST + np.arange(TS)]).astype(np.float32)
    inv = (np.float32(10000.0) ** (-np.arange(0, HD, 2, dtype=np.float32) / np.float32(HD))).astype(np.float32)
    ang = inv[p % 32][:, None] * pos[None, :]
    c[:, C_COS:C_COS + T] = np.cos(ang)
    c[:, C_SIN:C_SIN + T] = np.sin(ang) * np.where(p % HD < 32, -1.0, 1.0)[:, None]
    for tile in range(2):
        q = (tile * P + p) // CHUNK
        k = np.arange((tile + 1) * P) // CHUNK
        ok = (k[None, :] <= q[:, None]) & (k[None, :] >= q[:, None] - WIN)
        at = C_MASK + tile * P
        c[:, at:at + (tile + 1) * P] = np.where(ok, 0.0, -BIG)
    return c


def program(nc, a):
    ctx = ExitStack()
    with ctx:
        def sb(name, shape, dt=F32):
            return ctx.enter_context(nc.sbuf_tensor(name, shape, dt))

        def sem(name):
            return ctx.enter_context(nc.semaphore(name))

        raw = sb("raw", [P, 2, RAW * P])
        whi = sb("whi", [P, 4, KF // 2, P], F32R)
        wlo = sb("wlo", [P, 4, KF // 2, P], F32R)
        x = sb("x", [P, KD, T])
        xhi = sb("xhi", [P, KD, T], F32R)
        xlo = sb("xlo", [P, KD, T], F32R)
        ahi = sb("ahi", [P, KF, T], F32R)
        alo = sb("alo", [P, KF, T], F32R)
        rstd = sb("rstd", [P, T])
        std = sb("std", [P, T])
        ssq = sb("ssq", [P, T])
        sqr = sb("sqr", [P, 2, T])
        norms = sb("norms", [P, 8, KD])
        epst, warm = sb("epst", [P, 1]), sb("warm", [P, 10])
        cst = sb("cst", [P, 3 * P])
        ghi = sb("ghi", [P, KD, P], F32R)
        glo = sb("glo", [P, KD, P], F32R)
        graw = sb("graw", [P, KD, 2 * NH])
        bg = sb("bg", [NH, 2])
        m0 = sb("m0", [NH, 1])
        mout = sb("mout", [NH, 2])
        acol = sb("acol", [P, 3 * NH])
        one_row = cst[0:NH, P:P + 1].to_broadcast([NH, TP])
        work = sb("work", [P, 12496])
        ident, ones, perm = cst[:, 0:P], cst[:, P:2 * P], cst[:, 2 * P:3 * P]

        def w(at, *shape):
            n = int(np.prod(shape))
            v = work[:, at:at + n]
            if len(shape) == 2:
                v = v.rearrange("p (a b) -> p a b", a=shape[0])
            if len(shape) == 3:
                v = v.rearrange("p (a b c) -> p a b c", a=shape[0], b=shape[1])
            return v

        x_squares = w(0, KD // 2, T)
        f_gate, f_up, f_silu, f_prod = (w(i * 2 * T, 2, T) for i in range(4))
        xg = w(4 * 2 * T, KD, T)
        kT, qT, vT, oT = w(0, 2, T), w(576, 2, T), w(1152, 2, 2, T), w(2304, 2, 2, T)
        ktok, vtok = w(3456, 3, P), w(3840, 3, DV + 1)
        dec = w(4612, NH, 416)
        emb, intb = w(6276, NH, T), w(7428, NH, TS)
        wts, qi, n0rep = w(7556, 416), w(7972, TS), w(8004, P)
        sqn, den, rinv, hn, den2 = w(8132, 2, T), w(8708, T), w(8996, T), w(9284, 2, T), w(9860, T)
        row = [work[0:NH, 8132 + i * T:8132 + (i + 1) * T] for i in range(7)]
        r_em = work[0:NH, 8132 + 6 * T:8132 + 7 * T + TS]
        outp, outs, c0 = w(10180, DV + 1), w(10438, DV + 1), w(10696, NH, DV + 1)
        tri, sel = w(11724, 2 * P), w(11980, NH, P)
        s_raw, s_t1, s_t2, s_vT = w(0, 2, T), w(576, 2, T), w(1152, 2, T), w(1728, T)
        s_q, s_k, s_v = w(2304, KD, T), w(4608, 2, T), w(5184, 3, 2 * P)
        rc, rs = w(5952, T), w(6240, T)
        prob, probT = w(6528, 4, 3 * P), w(10176, 4, 3 * P)
        s_mx, s_neg, s_sum, s_sk, s_den, s_inv = (w(8064 + 4 * i, 2, 2) for i in range(6))
        vc, ks = w(8192, 2 * P), w(8448, 2, CACHE + TS)
        tables = w(8768, 2 * T + N_MASK)
        cos, sin, mask = tables[:, 0:T], tables[:, T:2 * T], tables[:, 2 * T:2 * T + N_MASK]
        snk, snks = w(9888, AH), w(9904, KV)
        s_qs = w(9920, 2, 4 * TS)

        acc = [ctx.enter_context(nc.psum_tensor(f"acc{i}", [P, 512], F32)) for i in range(4)]
        num = ctx.enter_context(nc.psum_tensor("num", [P, 2, 512], F32))
        mb = [num[:, 0, :], num[:, 1, :],
              ctx.enter_context(nc.psum_tensor("mb2", [P, 512], F32))[:, :],
              ctx.enter_context(nc.psum_tensor("mb3", [P, 512], F32))[:, :]]

        landed = [sem("landed0"), sem("landed1")]
        x_in = [sem(f"x_in{i}") for i in range(KD // 2)]
        chain_d, chain_a = sem("vector_chain"), sem("scalar_chain")
        first_in = sem("first_in")
        hi_done = sem("hi_done")
        lo_done = sem("lo_done")
        piece_done = sem("piece_done")
        evac = sem("evac")
        norms_in = sem("norms_in")
        cst_in = sem("cst_in")
        par_in = sem("par_in")
        mix_in = sem("mix_in")
        const_done = sem("const_done")
        xhi_done = sem("xhi_done")
        xlo_done = sem("xlo_done")
        silu_done = sem("silu_done")
        prod_done = sem("prod_done")
        ahi_done = sem("ahi_done")
        alo_done = sem("alo_done")
        x_sq = sem("x_sq")
        pool_sq = sem("pool_sq")
        ss_done = sem("ss_done")
        ss_mm = sem("ss_mm")
        std_done = sem("std_done")
        r_done = sem("r_done")
        g_zero = sem("g_zero")
        g_hi = sem("g_hi")
        g_done = sem("g_done")
        g_mm = sem("g_mm")
        fg_ready = sem("fg_ready")
        l_ready = sem("l_ready")
        rows_ready = sem("rows_ready")
        em_ready = sem("em_ready")
        at_mm = sem("at_mm")
        acol_ready = sem("acol_ready")
        mb_mm = sem("mb_mm")
        dm_ready = sem("dm_ready")
        d_ready = sem("d_ready")
        ei_mm = sem("ei_mm")
        ei_ready = sem("ei_ready")
        tok_mm = sem("tok_mm")
        tok_ready = sem("tok_ready")
        qk_mm = sem("qk_mm")
        wts_ready = sem("wts_ready")
        num_mm = sem("num_mm")
        den_mm = sem("den_mm")
        den_used = sem("den_used")
        sqn_ready = sem("sqn_ready")
        sqs_ready = sem("sqs_ready")
        ssq_mm = sem("ssq_mm")
        stp_mm = sem("stp_mm")
        outp_ready = sem("outp_ready")
        sts_mm = sem("sts_mm")
        outs_ready = sem("outs_ready")
        y_ready = sem("y_ready")
        sd_ready = sem("sd_ready")
        th_ready = sem("th_ready")
        hn_used = sem("hn_used")
        m_ready = sem("m_ready")
        mhi_ready = sem("mhi_ready")
        mlo_ready = sem("mlo_ready")
        rcs_ready = sem("rcs_ready")
        t1_ready = sem("t1_ready")
        rope_done = sem("rope_done")
        ks_ready = sem("ks_ready")
        turn_mm = sem("turn_mm")
        s_mm = sem("s_mm")
        neg_ready = sem("neg_ready")
        exp_ready = sem("exp_ready")
        p_ready = sem("p_ready")
        pt_mm = sem("pt_mm")
        pt_ready = sem("pt_ready")
        pv_mm = sem("pv_mm")
        ohi_ready = sem("ohi_ready")
        olo_ready = sem("olo_ready")
        y_out = sem("y_out")
        y_out_pool = sem("y_out_pool")
        out_dma = sem("out_dma")
        st_dma = sem("st_dma")
        y_dma = sem("y_dma")
        y_dma_pool = sem("y_dma_pool")

        block = ctx.enter_context(nc.Block())

        @block.sync
        def _(sp):
            def load(src, L, it, u):
                dst = raw[:, u % 2, 0:2 * L * P]
                sp.dma_start(dst, src).then_inc(landed[u % 2], 16)

            half = TILES[0] * P
            for n in range(KD // 2):
                if n == 0:
                    sp.dma_start(raw[:, 0, 0:half], a["w0"][0][:, 0:half]).then_inc(first_in, 16)
                if n == 2:
                    sp.dma_start(raw[:, 0, half:2 * half], a["w0"][0][:, half:2 * half]).then_inc(landed[0], 16)
                sp.dma_start(x[:, 2 * n:2 * n + 2, :], a["xT"][:, 2 * n:2 * n + 2, :]).then_inc(x_in[n], 16)
            for i, (kind, units, _, L) in enumerate(STAGES):
                src = a[f"w{i}"]
                u0 = FIRST_UNIT[i]
                first = 2 if i == 0 else 0
                if i == 0:
                    load(src[1], L, 0, 1)
                with sp.Fori(0, (units - first) // 2) as it:
                    for u in range(2):
                        sp.wait_ge(lo_done, 4 * it + 2 * (u0 + first + u - 2) + 2)
                        load(src[bass.ds(2 * it + (first + u), 1)].rearrange("a p n -> p (a n)"), L, it, u0 + first + u)
            sp.wait_ge(y_out_pool, KD - Y_POOL)
            sp.dma_start(a["yT"][:, Y_POOL:KD, :], x[:, Y_POOL:KD, :]).then_inc(y_dma_pool, 16)
            sp.wait_ge(y_dma_pool, 16)

        def split_hi(act, it, c, L):
            if c == 0 and isinstance(it, int):
                act.wait_ge(first_in, 16)
            else:
                act.wait_ge(landed[(c // 2) % 2], 16 * it + 16 * (c // 4 + 1))
            if c >= 4:
                act.wait_ge(piece_done, 4 * it + c - 3)
            src = raw[:, (c // 2) % 2, (c % 2) * L * P:(c % 2 + 1) * L * P]
            dst = whi[:, c % 4, 0:L, :].rearrange("p a b -> p (a b)")
            act.activation(dst, src, ACT.Copy).then_inc(hi_done, 1)

        def split_lo(dve, it, c, L):
            dve.wait_ge(hi_done, 4 * it + c + 1)
            src = raw[:, (c // 2) % 2, (c % 2) * L * P:(c % 2 + 1) * L * P]
            hi = whi[:, c % 4, 0:L, :].rearrange("p a b -> p (a b)").bitcast(F32)
            dst = wlo[:, c % 4, 0:L, :].rearrange("p a b -> p (a b)")
            dve.tensor_tensor(dst, src, hi, ALU.subtract).then_inc(lo_done, 1)

        def ahead(c):
            n = c // 2 + 2
            return TILES[n] if n < UNITS else None

        def products(pe, out, slot, tiles, hi, lo, first, last, before=None):
            for n, (t, k) in enumerate(tiles):
                if before:
                    before(k)
                wh, wl = whi[:, slot, t, :], wlo[:, slot, t, :]
                pe.matmul(out, wh, hi[:, k, :], start=(first and n == 0), stop=False)
                pe.matmul(out, wh, lo[:, k, :], start=False, stop=False)
                mm = pe.matmul(out, wl, hi[:, k, :], start=False, stop=(last and n == len(tiles) - 1))
            return mm

        def group_bank(g):
            return acc[(g + BANK) % 4][:, 0:T]

        def spread_bank(h):
            return mb[(h + 2) % 4]

        @block.tensor
        def _(pe):
            norm_no = [0]

            def x_ready(k):
                pe.wait_ge(xlo_done, KD * norm_no[0] + k + 1)

            def ss_sum():
                if norm_no[0] == 0:
                    pe.wait_ge(cst_in, 16)
                pe.wait_ge(ss_done, norm_no[0] + 1)
                final = norm_no[0] == N_FINAL
                mm = pe.matmul(mb[3][:, 0:T], ones, ssq[:, :], start=True, stop=not final)
                if final:
                    pe.wait_ge(x_sq, KD // 2 + 1)
                    mm = pe.matmul(mb[3][:, 0:T], ones, sqr[:, 1, :], start=False, stop=True)
                mm.then_inc(ss_mm, 1)

            def in_piece(i, it, c, g, G):
                pe.wait_ge(lo_done, 4 * it + c + 1)
                if not isinstance(it, int) or 4 * it + G >= 4:
                    pe.wait_ge(evac, 4 * it + G - 3)
                products(pe, group_bank(g), c % 4, [(k, k) for k in range(KD)], xhi, xlo, True, True).then_inc(piece_done, 1)

            def first_two(i, c, G):
                for ks in (range(0, 4), range(4, KD - 1), range(KD - 1, KD)):
                    for q in range(2):
                        if ks[0] == 0:
                            pe.wait_ge(lo_done, c + q + 1)
                            if G + q >= 4:
                                pe.wait_ge(evac, G + q - 3)
                        mm = products(pe, group_bank(q), (c + q) % 4, [(k, k) for k in ks], xhi, xlo,
                                      ks[0] == 0, ks[-1] == KD - 1, before=x_ready if q == 0 else None)
                        if ks[-1] == KD - 1:
                            mm.then_inc(piece_done, 1)
                ss_sum()
                norm_no[0] += 1

            def ffn_in(i):
                c0_, G0 = 2 * FIRST_UNIT[i], FIRST_GROUP[i]
                first_two(i, c0_, G0)
                for q in range(2, 4):
                    in_piece(i, 0, c0_ + q, q, G0 + q)
                with pe.Fori(1, KF // 2) as it:
                    for q in range(4):
                        in_piece(i, it, c0_ + q, q, G0 + q)

            n_alo = [0]

            def ffn_out(i):
                c0_, G0 = 2 * FIRST_UNIT[i], FIRST_GROUP[i]

                def unit(it, u, before=None):
                    pe.wait_ge(evac, 2 * it + G0 + u - 1)
                    for q in range(2):
                        c = c0_ + 2 * u + q
                        pe.wait_ge(lo_done, 4 * it + c + 1)
                        products(pe, acc[u][:, 0:T], c % 4, [(t, t + 11 * q) for t in range(11)], ahi, alo,
                                 q == 0, q == 1, before).then_inc(piece_done, 1)

                unit(0, 0, before=lambda k: pe.wait_ge(alo_done, n_alo[0] + k + 1))
                n_alo[0] += KF
                unit(0, 1)
                with pe.Fori(1, 4) as it:
                    for u in range(2):
                        unit(it, u)

            def mix_partial(i, m, chunks):
                c = 2 * FIRST_UNIT[i] + m
                if chunks[0] == 0:
                    pe.wait_ge(evac, FIRST_GROUP[i] - 3 + m)
                    pe.wait_ge(lo_done, c + 1)
                mm = products(pe, group_bank(m), c % 4, [(k, k) for k in chunks], ahi, alo,
                              chunks[0] == 0, chunks[-1] == KD - 1)
                if chunks[-1] == KD - 1:
                    mm.then_inc(piece_done, 1)

            def mix_rest(i):
                c0_, G0 = 2 * FIRST_UNIT[i], FIRST_GROUP[i]
                for m in range(4, KD):
                    pe.wait_ge(evac, G0 + m - 3)
                    pe.wait_ge(lo_done, c0_ + m + 1)
                    products(pe, group_bank(m), (c0_ + m) % 4, [(k, k) for k in range(KD)], ahi, alo, True, True)\
                        .then_inc(piece_done, 1)

            def gates():
                pe.wait_ge(g_done, 2)
                for k in range(KD):
                    for n, (wt, xt) in enumerate(((ghi, xhi), (ghi, xlo), (glo, xhi))):
                        mm = pe.matmul(mb[0][:, 0:T], wt[:, k, :], xt[:, k, :], start=(k == 0 and n == 0),
                                       stop=(k == KD - 1 and n == 2))
                mm.then_inc(g_mm, 1)

            def row_spread(part):
                if part == 0:
                    pe.wait_ge(rows_ready, 1)
                    for t, (s, n) in enumerate(TOK):
                        mm = pe.transpose(mb[1][0:n, NH * t:NH * t + NH], row[0][:, s:s + n], ident[0:NH, 0:NH])
                    mm.then_inc(at_mm, 1)
                    for h in range(NH):
                        if h == 3:
                            pe.wait_ge(acol_ready, 1)
                        pe.matmul(spread_bank(h)[:, 0:T], sel[0:NH, h, :], row[5], start=True, stop=True).then_inc(mb_mm, 1)
                else:
                    pe.wait_ge(em_ready, 2)
                    for h in range(NH):
                        pe.wait_ge(dm_ready, 3 * (h + 1))
                        pe.matmul(spread_bank(h)[:, 0:T + TS], sel[0:NH, h, :], r_em, start=True, stop=True).then_inc(ei_mm, 1)

            def head_work(h, step, G0):
                b = h % 2
                if step == 0:
                    pe.wait_ge(evac, G0 + 6 * h + 4)
                    if h >= 1:
                        pe.wait_ge(hn_used, 2 * h)
                    else:
                        pe.wait_ge(ei_ready, 2 * NH)
                    for t, (s, n) in enumerate(TOK):
                        for j, src in enumerate((kT[:, b], vT[:, b, 0], vT[:, b, 1])):
                            mm = pe.transpose(mb[t][0:n, j * P:(j + 1) * P], src[:, s:s + n], ident)
                        mm.then_inc(tok_mm, 1)
                    if h >= 1:
                        pe.wait_ge(outs_ready, h)
                    pe.matmul(mb[3][:, 0:256], kT[:, b, 0:128], qT[:, b, 0:256], start=True, stop=True)
                    pe.matmul(mb[3][:, 256:384], kT[:, b, 128:256], qT[:, b, 128:256], start=True, stop=True)
                    pe.matmul(mb[3][0:TS, 384:416], kT[:, b, 256:288], qT[:, b, 256:288], start=True, stop=True).then_inc(qk_mm, 1)
                if step == 1:
                    pe.wait_ge(tok_ready, 6 * (h + 1))
                    pe.wait_ge(wts_ready, 4 * (h + 1))
                    for e in range(3):
                        if e < 2:
                            src = [vtok[0:n, t, e * P:(e + 1) * P] for t, (_, n) in enumerate(TOK)]
                            st = c0[:, h, e * P:(e + 1) * P]
                        else:
                            src, st = [ones[0:n, :] for _, n in TOK], n0rep
                        kw = dict(skip_group_check=True)
                        pe.matmul(mb[e][:, 0:256], src[0], wts[:, 0:256], start=True, stop=False, **kw)
                        pe.matmul(mb[e][:, 128:256], src[1], wts[:, 256:384], start=False, stop=False, **kw)
                        pe.matmul(mb[e][:, 256:288], src[2], wts[0:TS, 384:416], start=False, stop=False, **kw)
                        mm = pe.matmul(mb[e][:, 256:288], st, qi, start=False, stop=True, **kw)
                        if e == 1:
                            mm.then_inc(num_mm, 1)
                    mm.then_inc(den_mm, 1)
                    for t in range(2):
                        mm = pe.matmul(mb[3][:, 0:DV + 1], ktok[:, t, :], vtok[:, t, :], start=(t == 0), stop=(t == 1))
                    mm.then_inc(stp_mm, 1)
                if step == 2:
                    pe.wait_ge(den_used, h + 1)
                    pe.wait_ge(sqs_ready, h + 1)
                    pe.matmul(mb[2][:, 0:T], ones, sqn[:, 0, :], start=True, stop=True).then_inc(ssq_mm, 1)
                    pe.wait_ge(outp_ready, h + 1)
                    pe.matmul(mb[3][:, 0:DV + 1], ktok[0:TS, 2, :], vtok[0:TS, 2, :], start=True, stop=True).then_inc(sts_mm, 1)

            def mlstm_in(i):
                c0_, G0 = 2 * FIRST_UNIT[i], FIRST_GROUP[i]
                for n in range(HEAD_START[-1] + 5):
                    if n == 0:
                        first_two(i, c0_, G0)
                    elif 1 < n < 6 * NH:
                        in_piece(i, 0, c0_ + n, n, G0 + n)
                    if n == 1:
                        gates()
                    if n == 5:
                        row_spread(0)
                    if n == 6:
                        row_spread(1)
                    if n in HEAD_STEPS:
                        head_work(*HEAD_STEPS[n], G0)

            def mlstm_out(i):
                for m in range(4):
                    for h in range(NH - 1):
                        if m == 0:
                            pe.wait_ge(mlo_ready, h + 1)
                        mix_partial(i, m, [2 * h, 2 * h + 1])
                pe.wait_ge(mlo_ready, NH)
                for m in range(4):
                    mix_partial(i, m, [KD - 2, KD - 1])
                mix_rest(i)

            def tick(t, G0):
                if t % 2 == 0 and t < len(ITEMS):
                    kind, c, _ = ITEMS[t]
                    if t >= 2:
                        pe.wait_ge(neg_ready, t)
                    halves = [(mb[u], u * HD, u * HD + HD) for u in range(2)]
                    if kind == "p":
                        pe.wait_ge(rope_done, ROPE.index(f"q{c}") + 1)
                        for bank, lo_, hi_ in halves:
                            pe.matmul(bank[:, 0:128], s_q[lo_:hi_, c, 0:128], s_k[lo_:hi_, c // 4, 0:128], start=True, stop=True)
                        for bank, lo_, hi_ in halves:
                            pe.matmul(bank[:, 128:384], s_q[lo_:hi_, c, 128:256], s_k[lo_:hi_, c // 4, 0:256],
                                      start=True, stop=True).then_inc(s_mm, 1)
                    else:
                        pe.wait_ge(ks_ready, ROPE.index(f"q{4 * c + 3}") + 1)
                        for bank, lo_, hi_ in halves:
                            pe.matmul(bank[:, 0:CACHE + TS], s_qs[lo_:hi_, c, :], ks[lo_:hi_, c, :],
                                      start=True, stop=True).then_inc(s_mm, 1)
                if 2 <= t < len(ITEMS) + 2:
                    n = t - 2
                    pe.wait_ge(p_ready, n + 1)
                    if n >= 1:
                        pe.wait_ge(pt_ready, n)
                    pr = prob[:, n % 4, :]
                    if ITEMS[n][0] == "p":
                        for j in range(3):
                            mm = pe.transpose(mb[2][:, j * P:(j + 1) * P], pr[:, j * P:(j + 1) * P], ident)
                    else:
                        pe.transpose(mb[2][:, 0:P], pr[:, 0:P], ident)
                        mm = pe.transpose(mb[2][0:TS, P:2 * P], pr[:, P:P + TS], ident)
                    mm.then_inc(pt_mm, 1)
                if t >= 4 and t % 2 == 0:
                    kind, c, _ = ITEMS[t - 4]
                    pe.wait_ge(pt_ready, t - 2)
                    pe.wait_ge(evac, G0 + group_of("turn", f"v{c // 4 if kind == 'p' else c}") + 1)
                    if t >= 6:
                        pe.wait_ge(olo_ready, (t - 4) // 2)
                    kw = dict(skip_group_check=True)
                    if kind == "p":
                        steps = ((0, 0, 0), (128, 0, 128), (128, 1, 256))
                        for n, (q, key, p) in enumerate(steps):
                            for u in range(2):
                                kv = 2 * (c // 4) + u
                                mm = pe.matmul(mb[3][u * HD:(u + 1) * HD, q:q + 128], s_v[:, key, kv * HD:(kv + 1) * HD],
                                               probT[:, (t - 4 + u) % 4, p:p + 128], start=n == 0, stop=n == 2, **kw)
                                if n == 2:
                                    mm.then_inc(pv_mm, 1)
                    else:
                        for u in range(2):
                            kv = 2 * c + u
                            pe.matmul(mb[3][u * HD:(u + 1) * HD, 0:128], vc[:, kv * HD:(kv + 1) * HD],
                                      probT[:, (t - 4 + u) % 4, 0:128], start=True, stop=False, **kw)
                        for u in range(2):
                            kv = 2 * c + u
                            pe.matmul(mb[3][u * HD:(u + 1) * HD, 0:128], s_v[0:TS, 2, kv * HD:(kv + 1) * HD],
                                      probT[0:TS, (t - 4 + u) % 4, 128:256], start=False, stop=True, **kw).then_inc(pv_mm, 1)

            def swa_in(i):
                c0_, G0 = 2 * FIRST_UNIT[i], FIRST_GROUP[i]
                pe.wait_ge(mix_in, MIX_SWA)
                for g, (what, p) in enumerate(SWA_GROUPS):
                    n = SWA_PIECES.index(p)
                    bank = group_bank(g)
                    if what == "piece":
                        if n == 0:
                            first_two(i, c0_, G0)
                        if n > 1:
                            in_piece(i, 0, c0_ + n, g, G0 + g)
                    elif what == "swap":
                        pe.wait_ge(evac, max(G0 + group_of("piece", p) + 1, G0 + g - 3))
                        pe.matmul(bank, perm, s_raw[:, ROPE.index(p) % 2, :], start=True, stop=True).then_inc(turn_mm, 1)
                    else:
                        pe.wait_ge(evac, max(G0 + group_of("piece", p) + 1, G0 + g - 3))
                        for t, (at, m) in enumerate(TOK):
                            mm = pe.transpose(acc[(g + BANK) % 4][0:m, t * P:(t + 1) * P], s_vT[:, at:at + m], ident)
                        mm.then_inc(turn_mm, 1)
                    if (what, p) in SWA_TICKS:
                        tick(SWA_TICKS[what, p], G0)

            def swa_out(i):
                G0 = FIRST_GROUP[i - 1]
                for t in TAIL_TICKS:
                    for m, ks in FILL.get(t, ()):
                        pe.wait_ge(olo_ready, 5)
                        mix_partial(i, m, ks)
                    tick(t, G0)
                pe.wait_ge(olo_ready, len(ITEMS) // 2)
                for m in range(4):
                    mix_partial(i, m, [4, 5, 6, 7])
                mix_rest(i)

            pe.wait_ge(g_zero, 1)
            for _ in range(WARM_UP):
                pe.matmul(group_bank(0), ghi[:, 0, :], ghi[:, 0:3, 0:T // 3], start=True, stop=True)
            ffn_in(0)
            ffn_out(1)
            pe.wait_ge(par_in, PAR_IN)
            mlstm_in(2)
            mlstm_out(3)
            ffn_in(4)
            ffn_out(5)
            ffn_in(6)
            ffn_out(7)
            swa_in(8)
            swa_out(9)
            ffn_in(10)
            ffn_out(11)
            ss_sum()

        @block.scalar
        def _(act):
            n_s = [0]

            def hi_of_x(m, norm):
                act.activation(xhi[:, m, :], x[:, m, :], ACT.Copy, scale=norms[:, norm, m:m + 1]).then_inc(xhi_done, 1)

            def rms(done):
                if done <= N_FINAL:
                    act.activation(warm[:, done:done + 1], epst[:, :], ACT.Sqrt)
                act.wait_ge(ss_mm, done)
                act.activation(std[:, :], mb[3][:, 0:T], ACT.Sqrt, bias=epst[:, :], scale=1.0 / D).then_inc(std_done, 1)

            def hi_ahead(it, c):
                L = ahead(c)
                if L:
                    split_hi(act, it, c + 4, L)

            def ffn_in(i, norm):
                c0_, G0 = 2 * FIRST_UNIT[i], FIRST_GROUP[i]
                f0 = KF * FFN_NO[i]
                split_hi(act, 0, c0_ + 4, 8)
                rms(norm + 1)

                def unit(it, u, look, begun=False):
                    c, G = c0_ + 2 * u, G0 + 2 * u
                    if look and not begun:
                        split_hi(act, it, c + 4, look)
                    act.wait_ge(evac, 4 * it + G + 1)
                    act.activation(f_silu[:, u % 2, :], f_gate[:, u % 2, :], ACT.Silu).then_inc(silu_done, 1)
                    if look:
                        split_hi(act, it, c + 5, look)
                    act.wait_ge(prod_done, 2 * it + f0 + u + 1)
                    act.activation(ahi[:, bass.ds(2 * it + u, 1), :], f_prod[:, u % 2:u % 2 + 1, :], ACT.Copy)\
                        .then_inc(ahi_done, 1)

                unit(0, 0, 8, begun=True)
                unit(0, 1, 8)
                with act.Fori(1, KF // 2 - 1) as it:
                    unit(it, 0, 8)
                    unit(it, 1, 8)
                for u in range(2):
                    unit(KF // 2 - 1, u, 11)

            def ffn_out(i, norm):
                c0_, G0 = 2 * FIRST_UNIT[i], FIRST_GROUP[i]

                def unit(it, u, look, final=False):
                    c = c0_ + 2 * u
                    if look:
                        split_hi(act, it, c + 4, look)
                    if final:
                        act.activation(warm[:, norm + 1:norm + 2], epst[:, :], ACT.Sqrt)
                        act.wait_ge(ss_done, norm + 1)
                    act.wait_ge(evac, 2 * it + G0 + u + 1)
                    if final:
                        act.activation(sqr[:, 1, :], x[:, KD - 1, :], ACT.Square).then_inc(x_sq, 1)
                    m = bass.ds(2 * it + u, 1)
                    act.activation(xhi[:, m, :] if norm < N_FINAL else xg[:, m, :], x[:, m, :], ACT.Copy,
                                   scale=norms[:, norm, m]).then_inc(xhi_done, 1)
                    if look:
                        split_hi(act, it, c + 5, look)

                with act.Fori(0, 3) as it:
                    for u in range(2):
                        unit(it, u, 11)
                for u in range(2):
                    unit(3, u, ahead(c0_ + 12 + 2 * u), final=u == 1 and norm == N_FINAL)

            def mix_out(i, norm):
                c0_, G0 = 2 * FIRST_UNIT[i], FIRST_GROUP[i]
                for m in range(KD):
                    hi_ahead(0, c0_ + m)
                    act.wait_ge(evac, G0 + m + 1)
                    hi_of_x(m, norm)

            def gate_logs():
                act.activation(warm[:, 8:9], epst[:, :], ACT.Exp)
                act.wait_ge(fg_ready, 1)
                n = n_s[0]
                act.activation(row[2], row[1], ACT.Abs).then_inc(chain_a, 1)
                act.wait_ge(chain_a, n + 1)
                act.activation(row[2], row[2], ACT.Exp, scale=-1.0).then_inc(chain_a, 1)
                act.wait_ge(chain_a, n + 2)
                act.activation(row[2], row[2], ACT.Ln, bias=cst[0:NH, P:P + 1]).then_inc(l_ready, 1)
                n_s[0] += 2

            def gate_exps():
                act.wait_ge(rows_ready, 1)
                act.activation(r_em[:, 0:T], row[1], ACT.Exp, scale=-2.0).then_inc(em_ready, 1)
                act.activation(r_em[:, T:T + TS], row[5][:, TP:T], ACT.Exp, scale=-1.0, bias=m0[:, :]).then_inc(em_ready, 1)

            def decays():
                for h in range(NH):
                    act.wait_ge(dm_ready, 3 * h + 3)
                    for t, (lo_, hi_, n) in enumerate(((0, 256, P), (256, 384, P), (384, 416, TS))):
                        v = dec[0:n, h, lo_:hi_]
                        act.activation(v, v, ACT.Exp, scale=-1.0, bias=acol[0:n, NH * t + h:NH * t + h + 1]).then_inc(d_ready, 1)

            def head_work(h, step, G0):
                b = h % 2
                if step == 0:
                    act.wait_ge(d_ready, 3 * h + 3)
                    for t, (_, n) in enumerate(TOK):
                        act.wait_ge(tok_mm, 3 * h + t + 1)
                        act.activation(vtok[0:n, t, 0:DV], mb[t][0:n, P:3 * P], ACT.Copy).then_inc(tok_ready, 1)
                        col = (255, 383, 415)[t]
                        act.activation(ktok[0:n, t, :], mb[t][0:n, 0:P], ACT.Copy,
                                       scale=dec[0:n, h, col:col + 1]).then_inc(tok_ready, 1)
                if step == 1:
                    act.wait_ge(num_mm, h + 1)
                    act.activation(sqn[:, :, :], num[:, :, 0:T], ACT.Square).then_inc(sqn_ready, 1)
                    act.wait_ge(den_mm, h + 1)
                    act.activation(den[:, :], mb[2][:, 0:T], ACT.Square).then_inc(den_used, 1)
                    act.wait_ge(stp_mm, h + 1)
                    if h >= 1:
                        act.wait_ge(st_dma, 32 * h)
                    act.activation(outp[:, :], mb[3][:, 0:DV + 1], ACT.Copy).then_inc(outp_ready, 1)
                if step == 2:
                    act.wait_ge(evac, G0 + 6 * h + 6)
                    act.activation(oT[:, b, :, :], oT[:, b, :, :], ACT.Tanh, scale=0.5).then_inc(th_ready, 1)
                    act.wait_ge(y_ready, h + 1)
                    act.activation(rinv[:, :], den2[:, :], ACT.Sqrt, scale=1.0 / DV).then_inc(sd_ready, 1)
                if step == 4:
                    act.wait_ge(m_ready, h + 1)
                    act.activation(ahi[:, 2 * h:2 * h + 2, :], hn[:, :, :], ACT.Copy).then_inc(mhi_ready, 1)

            def mlstm_in(i, norm):
                c0_, G0 = 2 * FIRST_UNIT[i], FIRST_GROUP[i]
                rms(norm + 1)
                for n in range(HEAD_START[-1] + 5):
                    if n < 6 * NH:
                        hi_ahead(0, c0_ + n)
                    if n == 1:
                        gate_logs()
                    if n == 3:
                        gate_exps()
                    if n == 5:
                        decays()
                    if n in HEAD_STEPS:
                        head_work(*HEAD_STEPS[n], G0)

            def tick(t):
                if t >= 5 and t % 2 == 1:
                    kind, c, _ = ITEMS[t - 5]
                    act.wait_ge(pv_mm, t - 3)
                    if kind == "p":
                        act.activation(ahi[:, c, 0:TP], mb[3][:, 0:TP], ACT.Copy).then_inc(ohi_ready, 1)
                    else:
                        act.activation(ahi[:, 4 * c:4 * c + 4, TP:T], mb[3][:, 0:P].rearrange("p (g t) -> p g t", g=4),
                                       ACT.Copy).then_inc(ohi_ready, 1)
                if 2 <= t < len(ITEMS) + 2:
                    n = t - 2
                    act.wait_ge(pt_mm, n + 1)
                    if n >= 4:
                        act.wait_ge(pv_mm, n - 3)
                    if ITEMS[n][0] == "p":
                        act.activation(probT[:, n % 4, :], mb[2][:, 0:3 * P], ACT.Copy).then_inc(pt_ready, 1)
                    else:
                        act.activation(probT[:, n % 4, 0:P], mb[2][:, 0:P], ACT.Copy)
                        act.activation(probT[0:TS, n % 4, P:2 * P], mb[2][0:TS, P:2 * P], ACT.Copy).then_inc(pt_ready, 1)
                if t < len(ITEMS):
                    kind, c, half = ITEMS[t]
                    b = t % 2
                    act.wait_ge(neg_ready, t + 1)
                    if kind == "p":
                        head = (2 * (c // 4) + half) * 4 + c % 4
                        parts, sink = ((0, P), (P, 3 * P)), snk[:, head:head + 1]
                    else:
                        parts, sink = ((0, CACHE + TS),), snks[:, 2 * c + half:2 * c + half + 1]
                    for j, (lo_, hi_) in enumerate(parts):
                        v = prob[:, t % 4, lo_:hi_]
                        act.activation(v, v, ACT.Exp, bias=s_neg[:, b, j:j + 1], accum_out=s_sum[:, b, j:j + 1])
                    act.activation(s_sk[:, b, 0:len(parts)], s_neg[:, b, 0:len(parts)], ACT.Exp, bias=sink).then_inc(exp_ready, 1)

            def swa_in(i, norm):
                c0_ = 2 * FIRST_UNIT[i]
                act.wait_ge(mix_in, MIX_SWA)
                rms(norm + 1)
                act.activation(warm[:, 9:10], epst[:, :], ACT.Exp)
                for what, p in SWA_GROUPS:
                    if what == "piece":
                        hi_ahead(0, c0_ + SWA_PIECES.index(p))
                    if (what, p) in SWA_TICKS:
                        tick(SWA_TICKS[what, p])
                for t in TAIL_TICKS:
                    tick(t)

            act.dma_start(norms[:, :, :], a["norms"]).then_inc(norms_in, 16)
            split_hi(act, 0, 0, 8)
            act.wait_ge(norms_in, 16)
            for m in range(KD):
                if m == 4:
                    act.dma_start(cst[:, :], a["cst"][:, 0:3 * P]).then_inc(cst_in, 16)
                    split_hi(act, 0, 1, 8)
                act.wait_ge(x_in[m // 2], 16)
                hi_of_x(m, N_F1)
                if m % 2 == 1:
                    act.activation(x_squares[:, m // 2, :], x[:, m, :], ACT.Square).then_inc(x_sq, 1)
            split_hi(act, 0, 2, 8)
            split_hi(act, 0, 3, 8)
            act.dma_start(graw[:, :, :], a["w_gates"]).then_inc(par_in, 16)
            act.dma_start(bg[:, :], a["b_gates"]).then_inc(par_in, 16)
            act.dma_start(m0[:, :], a["m0"]).then_inc(par_in, 16)
            act.dma_start(c0[:, :, :], a["c0"]).then_inc(par_in, 16)
            act.dma_start(tri[:, :], a["cst"][:, C_TRI:C_TRI + 2 * P]).then_inc(par_in, 16)
            act.dma_start(sel[:, :, :], a["cst"][:, C_SEL:C_SEL + NH * P]).then_inc(par_in, 16)
            act.wait_ge(const_done, 1)
            ffn_in(0, 0)
            act.wait_ge(g_zero, 2)
            act.wait_ge(par_in, PAR_IN)
            for j in range(2):
                act.activation(ghi[:, :, 32 * j:32 * j + NH], graw[:, :, NH * j:NH * j + NH], ACT.Copy).then_inc(g_hi, 1)
            ffn_out(1, 1)
            mlstm_in(2, 1)
            mix_out(3, 2)
            ffn_in(4, 2)
            ffn_out(5, 3)
            ffn_in(6, 3)
            ffn_out(7, 4)
            swa_in(8, 4)
            mix_out(9, 5)
            ffn_in(10, 5)
            ffn_out(11, 6)
            rms(7)
            for m in range(0, Y_POOL, 2):
                e = min(m + 2, Y_POOL)
                act.wait_ge(y_out, e)
                act.dma_start(a["yT"][:, m:e, :], x[:, m:e, :]).then_inc(y_dma, 16)
            act.wait_ge(y_dma, 16 * ((Y_POOL + 1) // 2))

        @block.vector
        def _(dve):
            n_d = [0]

            def own(ins):
                n_d[0] += 1
                ins.then_inc(chain_d, 1)
                dve.wait_ge(chain_d, n_d[0])

            def lo_of_x(m, norm, n):
                dve.wait_ge(xhi_done, n)
                dve.scalar_tensor_tensor(xlo[:, m, :], x[:, m, :], norms[:, norm, m:m + 1], xhi[:, m, :].bitcast(F32),
                                         ALU.mult, ALU.subtract).then_inc(xlo_done, 1)

            def rms(done):
                dve.wait_ge(std_done, done)
                dve.reciprocal(rstd[:, :], std[:, :]).then_inc(r_done, 1)
                dve.wait_ge(r_done, done)

            def lo_ahead(it, c):
                L = ahead(c)
                if L:
                    split_lo(dve, it, c + 4, L)

            def ffn_in(i, norm):
                c0_, G0 = 2 * FIRST_UNIT[i], FIRST_GROUP[i]
                f0 = KF * FFN_NO[i]
                split_lo(dve, 0, c0_ + 4, 8)
                rms(norm + 1)

                def unit(it, u, look, begun=False):
                    c, G = c0_ + 2 * u, G0 + 2 * u
                    b = u % 2
                    dve.wait_ge(piece_done, 4 * it + c + 1)
                    dve.tensor_tensor(f_gate[:, b, :], group_bank(2 * u), rstd[:, :], ALU.mult).then_inc(evac, 1)
                    if look and not begun:
                        split_lo(dve, it, c + 4, look)
                    dve.wait_ge(piece_done, 4 * it + c + 2)
                    dve.tensor_tensor(f_up[:, b, :], group_bank(2 * u + 1), rstd[:, :], ALU.mult).then_inc(evac, 1)
                    dve.wait_ge(silu_done, 2 * it + f0 + u + 1)
                    dve.wait_ge(evac, 4 * it + G + 2)
                    dve.tensor_tensor(f_prod[:, b, :], f_silu[:, b, :], f_up[:, b, :], ALU.mult).then_inc(prod_done, 1)
                    if look:
                        split_lo(dve, it, c + 5, look)
                    dve.wait_ge(ahi_done, 2 * it + f0 + u + 1)
                    dve.tensor_tensor(alo[:, bass.ds(2 * it + u, 1), :], f_prod[:, b:b + 1, :],
                                      ahi[:, bass.ds(2 * it + u, 1), :].bitcast(F32), ALU.subtract).then_inc(alo_done, 1)

                unit(0, 0, 8, begun=True)
                unit(0, 1, 8)
                with dve.Fori(1, KF // 2 - 1) as it:
                    unit(it, 0, 8)
                    unit(it, 1, 8)
                for u in range(2):
                    unit(KF // 2 - 1, u, 11)

            def ffn_out(i, norm):
                c0_, G0 = 2 * FIRST_UNIT[i], FIRST_GROUP[i]

                def unit(it, u, look):
                    c = c0_ + 2 * u
                    m = bass.ds(2 * it + u, 1)
                    if look:
                        split_lo(dve, it, c + 4, look)
                    dve.wait_ge(piece_done, 4 * it + c + 2)
                    dve.scalar_tensor_tensor(x[:, m, :], acc[u][:, 0:T].rearrange("p (a t) -> p a t", a=1), 0.5, x[:, m, :],
                                             ALU.mult, ALU.add).then_inc(evac, 1)
                    if norm < N_FINAL:
                        dve.wait_ge(xhi_done, 2 * it + KD * norm + u + 1)
                        dve.scalar_tensor_tensor(xlo[:, m, :], x[:, m, :], norms[:, norm, m], xhi[:, m, :].bitcast(F32),
                                                 ALU.mult, ALU.subtract).then_inc(xlo_done, 1)
                    if look:
                        split_lo(dve, it, c + 5, look)

                with dve.Fori(0, 3) as it:
                    for u in range(2):
                        unit(it, u, 11)
                for u in range(2):
                    unit(3, u, ahead(c0_ + 12 + 2 * u))

            def mix_out(i, norm):
                c0_, G0 = 2 * FIRST_UNIT[i], FIRST_GROUP[i]
                for m in range(KD):
                    dve.wait_ge(piece_done, c0_ + m + 1)
                    dve.tensor_tensor(x[:, m, :], group_bank(m), x[:, m, :], ALU.add).then_inc(evac, 1)
                    lo_ahead(0, c0_ + m)
                    lo_of_x(m, norm, KD * norm + m + 1)

            def gate_rows(part):
                if part == 0:
                    dve.wait_ge(g_mm, 1)
                    dve.tensor_tensor(row[0], mb[0][0:NH, 0:T], rstd[0:NH, :], ALU.mult)
                    own(dve.tensor_tensor(row[1], mb[0][32:32 + NH, 0:T], rstd[32:32 + NH, :], ALU.mult))
                    dve.tensor_scalar(row[1], row[1], bg[:, 1:2], None, ALU.add).then_inc(fg_ready, 1)
                    own(dve.tensor_scalar(row[0], row[0], bg[:, 0:1], None, ALU.add))
                    return
                dve.wait_ge(l_ready, 1)
                dve.wait_ge(fg_ready, 1)
                own(dve.scalar_tensor_tensor(row[3], row[1], 0.0, row[2], ALU.min, ALU.subtract))
                dve.tensor_tensor_scan(row[4][:, 0:TP], one_row, row[3][:, 0:TP], 0.0, ALU.mult, ALU.add)
                own(dve.tensor_tensor_scan(row[4][:, TP:T], one_row[:, 0:TS], row[3][:, TP:T], 0.0, ALU.mult, ALU.add))
                own(dve.tensor_tensor(row[0], row[0], row[4], ALU.subtract))
                dve.tensor_tensor_scan(row[5][:, 0:TP], one_row, row[0][:, 0:TP], 0.0, ALU.mult, ALU.max)
                own(dve.tensor_tensor_scan(row[5][:, TP:T], one_row[:, 0:TS], row[0][:, TP:T], m0[:, 0:1], ALU.mult, ALU.max))
                own(dve.tensor_tensor(row[1], row[4], row[5], ALU.add))
                dve.tensor_copy(mout[:, 0:1], row[1][:, TP - 1:TP])
                dve.tensor_copy(mout[:, 1:2], row[1][:, T - 1:T]).then_inc(rows_ready, 1)

            def decay_rows():
                dve.wait_ge(at_mm, 1)
                dve.tensor_copy(acol[:, 0:2 * NH], mb[1][:, 0:2 * NH])
                dve.tensor_copy(acol[0:TS, 2 * NH:3 * NH], mb[1][0:TS, 2 * NH:3 * NH]).then_inc(acol_ready, 1)
                for h in range(NH):
                    dve.wait_ge(mb_mm, h + 1)
                    bank = spread_bank(h)
                    dve.tensor_tensor(dec[:, h, 0:256], bank[:, 0:256], tri, ALU.add).then_inc(dm_ready, 1)
                    dve.tensor_tensor(dec[:, h, 256:384], bank[:, 128:256], tri[:, 0:P], ALU.add).then_inc(dm_ready, 1)
                    dve.tensor_tensor(dec[0:TS, h, 384:416], bank[0:TS, TP:T], tri[0:TS, 0:TS], ALU.add).then_inc(dm_ready, 1)

            def em_rows():
                for h in range(NH):
                    dve.wait_ge(ei_mm, h + 1)
                    bank = spread_bank(h)
                    dve.tensor_scalar(emb[:, h, :], bank[:, 0:T], TINY, None, ALU.max).then_inc(ei_ready, 1)
                    dve.tensor_copy(intb[:, h, :], bank[:, T:T + TS]).then_inc(ei_ready, 1)

            def head_work(h, step, G0):
                b = h % 2
                if step == 0:
                    dve.wait_ge(qk_mm, h + 1)
                    dve.wait_ge(d_ready, 3 * h + 3)
                    dve.wait_ge(ei_ready, 2 * NH)
                    dve.tensor_tensor(wts[:, 0:384], mb[3][:, 0:384], dec[:, h, 0:384], ALU.mult).then_inc(wts_ready, 1)
                    dve.tensor_tensor(wts[0:TS, 384:416], mb[3][0:TS, 384:416], dec[0:TS, h, 384:416], ALU.mult).then_inc(wts_ready, 1)
                    dve.tensor_tensor(qi, qT[:, b, TP:T], intb[:, h, :], ALU.mult).then_inc(wts_ready, 1)
                    dve.tensor_scalar(n0rep, ones, c0[:, h, DV:DV + 1], None, ALU.mult).then_inc(wts_ready, 1)
                if step == 1:
                    dve.wait_ge(den_used, h + 1)
                    own(dve.tensor_tensor(den[:, :], den[:, :], emb[:, h, :], ALU.max))
                if step == 2:
                    dve.wait_ge(ssq_mm, h + 1)
                    dve.scalar_tensor_tensor(den2[:, :], den[:, :], DV * EPS, mb[2][:, 0:T], ALU.mult, ALU.add).then_inc(y_ready, 1)
                    dve.wait_ge(sts_mm, h + 1)
                    if h >= 1:
                        dve.wait_ge(st_dma, 32 * h)
                    dve.scalar_tensor_tensor(outs[:, :], c0[:, h, :], intb[:, h, TS - 1:TS], mb[3][:, 0:DV + 1],
                                             ALU.mult, ALU.add).then_inc(outs_ready, 1)
                if step == 3:
                    dve.wait_ge(sd_ready, h + 1)
                    own(dve.reciprocal(rinv[:, :], rinv[:, :]))
                    for e in range(2):
                        c = 2 * h + e
                        dve.scalar_tensor_tensor(hn[:, e, :], num[:, e, 0:T], norms[:, N_HEAD, c:c + 1], rinv[:, :],
                                                 ALU.mult, ALU.mult).then_inc(hn_used, 1)
                    dve.wait_ge(th_ready, h + 1)
                    dve.wait_ge(hn_used, 2 * h + 2)
                    dve.scalar_tensor_tensor(hn[:, :, :], oT[:, b, :, :], 1.0, hn[:, :, :], ALU.add, ALU.mult).then_inc(m_ready, 1)
                if step == 4:
                    dve.wait_ge(mhi_ready, h + 1)
                    dve.tensor_tensor(alo[:, 2 * h:2 * h + 2, :], hn[:, :, :], ahi[:, 2 * h:2 * h + 2, :].bitcast(F32),
                                      ALU.subtract).then_inc(mlo_ready, 1)

            def mlstm_in(i, norm):
                c0_, G0 = 2 * FIRST_UNIT[i], FIRST_GROUP[i]
                rms(norm + 1)
                own(dve.tensor_scalar(norms[:, N_HEAD, :], norms[:, N_HEAD, :], 0.5, None, ALU.mult))
                dve.memset(vtok[:, :, DV:DV + 1], 1.0)
                for n in range(HEAD_START[-1] + 5):
                    if n < 6 * NH:
                        b = (n // 6) % 2
                        dve.wait_ge(piece_done, c0_ + n + 1)
                        ps = group_bank(n)
                        dst = (kT[:, b, :], qT[:, b, :], vT[:, b, 0, :], vT[:, b, 1, :], oT[:, b, 0, :], oT[:, b, 1, :])[n % 6]
                        if n % 6 == 0:
                            dve.scalar_tensor_tensor(dst, ps, float(DK) ** -0.5, rstd[:, :], ALU.mult, ALU.mult).then_inc(evac, 1)
                        else:
                            dve.tensor_tensor(dst, ps, rstd[:, :], ALU.mult).then_inc(evac, 1)
                    if n == 2:
                        gate_rows(1)
                    if n == 5:
                        decay_rows()
                    h, step = HEAD_STEPS.get(n, (None, None))
                    if step == 3:
                        head_work(h, step, G0)
                    if n < 6 * NH:
                        lo_ahead(0, c0_ + n)
                    if n == 1:
                        gate_rows(0)
                    if n == 6:
                        em_rows()
                    if step not in (None, 3):
                        head_work(h, step, G0)

            def scores(t):
                if t < len(ITEMS):
                    kind, c, half = ITEMS[t]
                    b = t % 2
                    dve.wait_ge(s_mm, t + 1)
                    if t >= 4:
                        dve.wait_ge(pt_mm, t - 3)
                    if kind == "p":
                        head = (2 * (c // 4) + half) * 4 + c % 4
                        parts, sink = ((0, P), (P, 3 * P)), snk[:, head:head + 1]
                        offs = (0, P)
                    else:
                        parts, sink = ((0, CACHE + TS),), snks[:, 2 * c + half:2 * c + half + 1]
                        offs = (3 * P,)
                    for j, ((lo_, hi_), o) in enumerate(zip(parts, offs)):
                        ins = dve.tensor_tensor_reduce(prob[:, t % 4, lo_:hi_], mb[b][:, lo_:hi_], mask[:, o:o + hi_ - lo_],
                                                       float(HD) ** -0.5, -3e38, ALU.add, ALU.max, s_mx[:, b, j:j + 1])
                    own(ins)
                    dve.tensor_scalar(s_neg[:, b, 0:len(parts)], s_mx[:, b, 0:len(parts)], sink, -1.0, ALU.max, ALU.mult)\
                        .then_inc(neg_ready, 1)

            def divide(t):
                if 1 <= t <= len(ITEMS):
                    n = t - 1
                    b = n % 2
                    parts = ((0, P), (P, 3 * P)) if ITEMS[n][0] == "p" else ((0, CACHE + TS),)
                    dve.wait_ge(exp_ready, n + 1)
                    J = len(parts)
                    own(dve.tensor_tensor(s_den[:, b, 0:J], s_sum[:, b, 0:J], s_sk[:, b, 0:J], ALU.add))
                    own(dve.reciprocal(s_inv[:, b, 0:J], s_den[:, b, 0:J]))
                    for j, (lo_, hi_) in enumerate(parts):
                        v = prob[:, n % 4, lo_:hi_]
                        ins = dve.tensor_scalar(v, v, s_inv[:, b, j:j + 1], None, ALU.mult)
                    ins.then_inc(p_ready, 1)

            def outputs_lo(t):
                if t >= 5 and t % 2 == 1:
                    kind, c, _ = ITEMS[t - 5]
                    dve.wait_ge(ohi_ready, (t - 3) // 2)
                    if kind == "p":
                        dve.tensor_tensor(alo[:, c, 0:TP], mb[3][:, 0:TP], ahi[:, c, 0:TP].bitcast(F32), ALU.subtract)\
                            .then_inc(olo_ready, 1)
                    else:
                        dve.tensor_tensor(alo[:, 4 * c:4 * c + 4, TP:T], mb[3][:, 0:P].rearrange("p (g t) -> p g t", g=4),
                                          ahi[:, 4 * c:4 * c + 4, TP:T].bitcast(F32), ALU.subtract).then_inc(olo_ready, 1)

            def tick(t):
                scores(t)
                if t % 2 == 1:
                    divide(t)
                outputs_lo(t)

            def swa_in(i, norm):
                c0_ = 2 * FIRST_UNIT[i]
                for g, (what, p) in enumerate(SWA_GROUPS):
                    n = SWA_PIECES.index(p)
                    bank = group_bank(g)
                    xi = ROPE.index(p) if p in ROPE else None
                    if what == "piece":
                        dve.wait_ge(piece_done, c0_ + n + 1)
                        if xi is None:
                            dve.tensor_tensor(s_vT[:, :], bank, rstd[:, :], ALU.mult).then_inc(evac, 1)
                        else:
                            if xi >= 2:
                                dve.wait_ge(t1_ready, xi - 1)
                            dve.tensor_copy(s_raw[:, xi % 2, :], bank).then_inc(evac, 1)
                        if n == 1:
                            rms(norm + 1)
                            dve.wait_ge(mix_in, MIX_SWA)
                            dve.tensor_tensor(rc, cos, rstd[:, :], ALU.mult).then_inc(rcs_ready, 1)
                            own(dve.tensor_tensor(rs, sin, rstd[:, :], ALU.mult))
                        if n >= FIRST_TICK:
                            divide(2 * (n - FIRST_TICK))
                        if n == 1:
                            lo_ahead(0, c0_)
                        if n > 0:
                            lo_ahead(0, c0_ + n)
                    else:
                        dve.wait_ge(turn_mm, TURNS.index((what, p)) + 1)
                        if what == "swap":
                            if xi >= 2:
                                dve.wait_ge(rope_done, xi - 1)
                            dve.tensor_tensor(s_t2[:, xi % 2, :], bank, rs, ALU.mult).then_inc(evac, 1)
                        else:
                            j = int(p[1]) * P
                            bank = acc[(g + BANK) % 4]
                            dve.tensor_copy(s_v[0:TS, 2, j:j + P], bank[0:TS, 2 * P:3 * P])
                            dve.tensor_copy(s_v[:, 0:2, j:j + P], bank[:, 0:2 * P].rearrange("p (t c) -> p t c", t=2))\
                                .then_inc(evac, 1)
                    if (what, p) in SWA_TICKS:
                        tick(SWA_TICKS[what, p])
                for t in TAIL_TICKS:
                    if t % 2 == 0:
                        divide(t)
                    tick(t)

            dve.memset(epst[:, :], EPS).then_inc(const_done, 1)
            dve.memset(ghi[:, :, :].bitcast(F32), 0.0).then_inc(g_zero, 1)
            dve.memset(glo[:, :, :].bitcast(F32), 0.0).then_inc(g_zero, 1)
            split_lo(dve, 0, 0, 8)
            dve.wait_ge(norms_in, 16)
            for m in range(KD):
                if m == 4:
                    split_lo(dve, 0, 1, 8)
                dve.wait_ge(x_in[m // 2], 16)
                lo_of_x(m, N_F1, m + 1)
            split_lo(dve, 0, 2, 8)
            split_lo(dve, 0, 3, 8)
            ffn_in(0, 0)
            dve.wait_ge(par_in, PAR_IN)
            for j in range(2):
                dve.wait_ge(g_hi, j + 1)
                dve.tensor_tensor(glo[:, :, 32 * j:32 * j + NH], graw[:, :, NH * j:NH * j + NH],
                                  ghi[:, :, 32 * j:32 * j + NH].bitcast(F32), ALU.subtract).then_inc(g_done, 1)
            ffn_out(1, 1)
            mlstm_in(2, 1)
            mix_out(3, 2)
            ffn_in(4, 2)
            ffn_out(5, 3)
            ffn_in(6, 3)
            ffn_out(7, 4)
            swa_in(8, 4)
            mix_out(9, 5)
            ffn_in(10, 5)
            ffn_out(11, 6)
            rms(7)
            dve.wait_ge(xhi_done, KD * (N_FINAL + 1))
            for m in range(Y_POOL):
                dve.tensor_tensor(x[:, m, :], xg[:, m, :], rstd[:, :], ALU.mult).then_inc(y_out, 1)

        @block.gpsimd
        def _(pool):
            n_p = [0]

            def squares(norm, done):
                chunks = KD - 1 if norm == N_FINAL else KD
                for m in range(chunks):
                    done(m)
                    if m == 0:
                        if norm:
                            pool.wait_ge(ss_mm, norm)
                        pool.tensor_tensor(ssq[:, :], x[:, 0, :], x[:, 0, :], ALU.mult).then_inc(pool_sq, 1)
                        n_p[0] += 1
                        continue
                    if norm == 0 and m % 2 == 1:
                        pool.wait_ge(x_sq, m // 2 + 1)
                        pool.wait_ge(pool_sq, n_p[0])
                        add = pool.tensor_tensor(ssq[:, :], ssq[:, :], x_squares[:, m // 2, :], ALU.add)
                        add.then_inc(ss_done if m == KD - 1 else pool_sq, 1)
                        n_p[0] += m < KD - 1
                        continue
                    pool.tensor_tensor(sqr[:, m % 2, :], x[:, m, :], x[:, m, :], ALU.mult).then_inc(pool_sq, 1)
                    n_p[0] += 1
                    pool.wait_ge(pool_sq, n_p[0])
                    add = pool.tensor_tensor(ssq[:, :], ssq[:, :], sqr[:, m % 2, :], ALU.add)
                    if m == chunks - 1:
                        add.then_inc(ss_done, 1)
                    else:
                        add.then_inc(pool_sq, 1)
                        n_p[0] += 1

            def after(i):
                return lambda m: pool.wait_ge(evac, FIRST_GROUP[i] + m + 1)

            squares(0, lambda m: pool.wait_ge(x_in[m // 2], 16))
            squares(1, after(1))
            for h in range(NH):
                pool.wait_ge(sqn_ready, h + 1)
                pool.tensor_tensor(sqn[:, 0, :], sqn[:, 0, :], sqn[:, 1, :], ALU.add).then_inc(sqs_ready, 1)
                pool.wait_ge(outp_ready, h + 1)
                pool.dma_start(a["cp"][:, h, :], outp[:, :]).then_inc(st_dma, 16)
                pool.wait_ge(outs_ready, h + 1)
                pool.dma_start(a["cs"][:, h, :], outs[:, :]).then_inc(st_dma, 16)
            pool.dma_start(a["mo"], mout[:, :]).then_inc(out_dma, 16)
            squares(2, after(3))
            pool.wait_ge(mlo_ready, NH)
            pool.wait_ge(ss_done, 3)
            pool.dma_start(vc[:, :], a["cache_v"]).then_inc(mix_in, 16)
            pool.dma_start(ks[:, :, 0:CACHE], a["cache_kT"]).then_inc(mix_in, 16)
            pool.dma_start(tables, a["cst"][:, C_COS:N_CONST]).then_inc(mix_in, 16)
            pool.dma_start(snk[:, :], a["sinks"].to_broadcast([P, AH])).then_inc(mix_in, 16)
            for g in range(4):
                pool.dma_start(snks[TS * g:TS * g + TS, :], a["sinks_g"][g:g + 1, :].to_broadcast([TS, KV])).then_inc(mix_in, 16)
            squares(3, after(5))
            squares(4, after(7))
            G0 = FIRST_GROUP[8]
            pool.wait_ge(rcs_ready, 1)
            pool.wait_ge(mix_in, MIX_SWA)
            for xi, p in enumerate(ROPE):
                b, c = xi % 2, int(p[1])
                pool.wait_ge(evac, G0 + group_of("piece", p) + 1)
                pool.tensor_tensor(s_t1[:, b, :], s_raw[:, b, :], rc, ALU.mult).then_inc(t1_ready, 1)
                pool.wait_ge(evac, G0 + group_of("swap", p) + 1)
                pool.wait_ge(t1_ready, xi + 1)
                dst = s_k[:, c, :] if p[0] == "k" else s_q[:, c, :]
                pool.tensor_tensor(dst, s_t1[:, b, :], s_t2[:, b, :], ALU.add).then_inc(rope_done, 1)
                pool.wait_ge(rope_done, xi + 1)
                again = ks[:, c, CACHE:CACHE + TS] if p[0] == "k" else s_qs[:, c // 4, TS * (c % 4):TS * (c % 4) + TS]
                pool.tensor_copy(again, dst[:, TP:T]).then_inc(ks_ready, 1)
            pool.dma_start(a["kT_out"], s_k[:, :, TP - P:T]).then_inc(out_dma, 16)
            pool.wait_ge(evac, G0 + group_of("turn", "v1") + 1)
            pool.dma_start(a["v_out"][0:P, :], s_v[:, 1, :]).then_inc(out_dma, 16)
            pool.dma_start(a["v_out"][P:P + TS, :], s_v[0:TS, 2, :]).then_inc(out_dma, 16)
            squares(5, after(9))
            squares(6, after(11))
            pool.wait_ge(r_done, N_FINAL + 1)
            pool.wait_ge(xhi_done, KD * (N_FINAL + 1))
            for m in range(Y_POOL, KD):
                pool.tensor_tensor(x[:, m, :], xg[:, m, :], rstd[:, :], ALU.mult).then_inc(y_out_pool, 1)
            pool.wait_ge(st_dma, 32 * NH)
            pool.wait_ge(out_dma, 16 * OUT_DMAS)


def prod(v):
    return int(np.prod(v))


FFN_NO = {0: 0, 4: 1, 6: 2, 10: 3}
PAR_IN = 16 * 6
MIX_SWA = 16 * 8
OUT_DMAS = 4


def layouts(v):
    f = np.ascontiguousarray

    def pieces(wt, per):
        k, n = wt.shape[0] // P, wt.shape[1] // P
        return f(wt.reshape(k, P, n // per, per, P).transpose(2, 1, 3, 0, 4)).reshape(n // per, P, per * k * P)

    def chunks(g):
        return g.reshape(KD, P).T

    def ffn_in(wt):
        gate, up = wt[:, :FF].reshape(D, KF, 1, P), wt[:, FF:].reshape(D, KF, 1, P)
        return pieces(np.concatenate([gate, up], axis=2).reshape(D, 2 * FF), 2)

    a = {}
    x = np.concatenate([v["x_prompt"][0], v["x_sample"][0]])
    a["xT"] = f(x.T.reshape(KD, P, T).transpose(1, 0, 2))
    ffn = [(v[f"ffn_w_in{n}"][i], v[f"ffn_w_out{n}"][i]) for i in range(2) for n in (1, 2)]
    for i, (w_in, w_out) in zip((0, 4, 6, 10), ffn):
        a[f"w{i}"], a[f"w{i + 1}"] = ffn_in(w_in), pieces(w_out, 1)
    m = v["mlstm_w_in"][0]
    hk, hv = NH * DK, NH * DV
    part = [m[:, hk:2 * hk].reshape(D, NH, DK), m[:, 0:hk].reshape(D, NH, DK),
            m[:, 2 * hk:2 * hk + hv].reshape(D, NH, DV), m[:, 2 * hk + hv:2 * hk + 2 * hv].reshape(D, NH, DV)]
    a["w2"] = pieces(np.concatenate(part, axis=2).reshape(D, -1), 2)
    a["w_gates"] = f(m[:, 2 * hk + 2 * hv:].reshape(KD, P, 2 * NH).transpose(1, 0, 2))
    a["w3"] = pieces(v["mlstm_w_out"][0], 2)
    q = v["swa_w_qkv"][0]
    def pairs(t, axis):
        s = t.shape
        t = t.reshape(*s[:axis], 2, 2, 4, HD, *s[axis + 1:])
        return np.swapaxes(t, axis + 1, axis + 2).reshape(s)
    q = np.concatenate([pairs(q[:, :AH * HD], 1), q[:, AH * HD:]], axis=1).reshape(D, -1, P)
    first = {"q": 0, "k": KD, "v": KD + 2}
    a["w8"] = pieces(q[:, [first[p[0]] + int(p[1]) for p in SWA_PIECES]].reshape(D, -1), 2)
    a["w9"] = pieces(pairs(v["swa_w_out"][0], 0), 2)
    rows = []
    for i in range(2):
        rows += [v["ffn_norm1"][i], v["mix_norm"][i], v["ffn_norm2"][i]]
    rows += [v["final_norm"], v["mlstm_head_norm"][0]]
    a["norms"] = f(np.stack([chunks(r) for r in rows], axis=1))
    a["b_gates"] = f(v["mlstm_b_gates"][0].reshape(2, NH).T)
    a["m0"] = f(v["state_mlstm_m"][0, 0].reshape(NH, 1))
    c = np.concatenate([v["state_mlstm_C"][0, 0], v["state_mlstm_n"][0, 0][:, :, None]], axis=2)
    a["c0"] = f(c.transpose(1, 0, 2))
    a["cache_kT"] = f(v["cache_swa_k"][0, 0].reshape(CACHE, 2, 2 * HD).transpose(2, 1, 0))
    a["cache_v"] = f(v["cache_swa_v"][0, 0].reshape(CACHE, KV * HD))
    a["sinks"] = f(v["swa_sinks"])
    a["sinks_g"] = f(v["swa_sinks"].reshape(KV, 4).T)
    a["cst"] = constants()
    return a


OUTS = {"yT": (P, KD, T), "cp": (P, NH, DV + 1), "cs": (P, NH, DV + 1), "mo": (NH, 2),
        "kT_out": (P, 2, P + TS), "v_out": (P + TS, KV * HD)}


def kernel(**inputs):
    import concourse.bacc as bacc
    from concourse.bass_utils import run_bass_kernel_spmd

    nc = bacc.Bacc("TRN2", target_bir_lowering=False, num_devices=1)
    arrays = layouts({k: np.asarray(t) for k, t in inputs.items()})
    aps = {k: nc.dram_tensor(f"in_{k}", t.shape, F32, kind="ExternalInput").ap() for k, t in arrays.items()}
    aps.update({k: nc.dram_tensor(f"out_{k}", s, F32, kind="ExternalOutput").ap() for k, s in OUTS.items()})
    program(nc, aps)
    r = run_bass_kernel_spmd(nc, [{f"in_{k}": t for k, t in arrays.items()}], core_ids=[0]).results[0]
    o = {k: np.asarray(r[f"out_{k}"]) for k in OUTS}
    y = o["yT"].transpose(1, 0, 2).reshape(D, T).T
    kT = o["kT_out"].transpose(2, 1, 0).reshape(P + TS, KV, HD)
    v = o["v_out"].reshape(P + TS, KV, HD)
    c = {g: o[g].transpose(1, 0, 2) for g in ("cp", "cs")}
    f = np.ascontiguousarray
    return (f(y[None, :TP]), f(y[None, TP:]),
            f(c["cp"][None, None, :, :, :DV]), f(c["cp"][None, None, :, :, DV]), f(o["mo"][:, 0][None, None]),
            f(kT[None, None, :P]), f(v[None, None, :P]),
            f(c["cs"][None, None, :, :, :DV]), f(c["cs"][None, None, :, :, DV]), f(o["mo"][:, 1][None, None]),
            f(kT[None, None, P:]), f(v[None, None, P:]))
```
